# Optimizing a Trainium2 kernel written in Bass

```python
import jax, jax.numpy as jnp
from jax import lax
import numpy as np

D_MODEL = 1024
BATCH = 1
SEQ = 512
DEPTH = 2

GRID_W = 64
CTX_LEN = 256
N_MIXERS = 2
N_RET_LAYERS = (DEPTH + 1) // 2
N_CONV_LAYERS = DEPTH // 2
RET_HEADS = 4
RET_QK_DIM = D_MODEL // RET_HEADS
RET_V_DIM = 2 * RET_QK_DIM
RET_QK_TOTAL = RET_HEADS * RET_QK_DIM
RET_V_TOTAL = RET_HEADS * RET_V_DIM
RET_IN_DIM = 2 * RET_QK_TOTAL + 2 * RET_V_TOTAL
RET_CHUNK = 128
ROPE_AXES = (64, 96, 96)
ROPE_THETA = 10000.0
CONV_WIDTH = 31
N_EXPERTS = 64
TOP_K = 8
N_GROUPS = 8
TOPK_GROUPS = 4
EXPERT_DIM = 256
SHARED_DIM = 256
ROUTE_SCALE = 2.5
MOE_BLOCK = 128
NORM_EPS = 1e-6
LN_EPS = 1e-5

kernel_name = 'hybrid_retention_conformer_moe_dit'

def rms_norm(x, g):
    xf = x.astype(jnp.float32)
    y = xf * lax.rsqrt(jnp.mean(xf * xf, -1, keepdims=True) + NORM_EPS)
    return (y * g.astype(jnp.float32)).astype(x.dtype)

def modulate(x, shift, scale):
    return x * (1 + scale) + shift

def rope_angles(pos):
    parts = []
    for a, d in enumerate(ROPE_AXES):
        inv = ROPE_THETA ** (-jnp.arange(0, d, 2, dtype=jnp.float32) / d)
        parts.append(pos[:, a:a + 1].astype(jnp.float32) * inv[None, :])
    return jnp.concatenate(parts, -1)

def apply_rope(x, ang):
    cos = jnp.cos(ang)[None, :, None, :].astype(x.dtype)
    sin = jnp.sin(ang)[None, :, None, :].astype(x.dtype)
    xr = x.reshape(x.shape[:-1] + (-1, 2))
    x0, x1 = xr[..., 0], xr[..., 1]
    return jnp.stack([x0 * cos - x1 * sin, x0 * sin + x1 * cos], -1).reshape(x.shape)

def retention_chunkwise(q, k, v, log_g, s0):
    b, h, n, dk = q.shape
    dv = v.shape[-1]
    c = RET_CHUNK
    nc = n // c
    qc = q.reshape(b, h, nc, c, dk)
    kc = k.reshape(b, h, nc, c, dk)
    vc = v.reshape(b, h, nc, c, dv)
    idx = jnp.arange(c, dtype=jnp.float32)
    rel = idx[:, None] - idx[None, :]
    dmask = jnp.where(rel >= 0, jnp.exp(log_g[:, None, None] * jnp.maximum(rel, 0.0)), 0.0).astype(q.dtype)
    scores = jnp.einsum('bhcid,bhcjd->bhcij', qc, kc) * dmask[None, :, None]
    o_intra = jnp.einsum('bhcij,bhcje->bhcie', scores, vc)
    q_dec = jnp.exp(log_g[:, None] * (idx + 1.0)).astype(q.dtype)[None, :, :, None]
    k_dec = jnp.exp(log_g[:, None] * (c - 1.0 - idx)).astype(q.dtype)[None, :, :, None]
    c_dec = jnp.exp(log_g * c).astype(q.dtype)[None, :, None, None]

    def step(s, inp):
        qi, ki, vi = inp
        o = jnp.einsum('bhid,bhde->bhie', qi * q_dec, s)
        s = s * c_dec + jnp.einsum('bhjd,bhje->bhde', ki * k_dec, vi)
        return s, o

    xs = (jnp.moveaxis(qc, 2, 0), jnp.moveaxis(kc, 2, 0), jnp.moveaxis(vc, 2, 0))
    _, o_inter = lax.scan(step, s0, xs)
    o = o_intra + jnp.moveaxis(o_inter, 0, 2)
    return o.reshape(b, h, n, dv)

def retention_final_state(k, v, log_g, reverse):
    n = k.shape[2]
    pos = jnp.arange(n, dtype=jnp.float32)
    dist = pos if reverse else (n - 1.0 - pos)
    w = jnp.exp(log_g[:, None] * dist).astype(k.dtype)
    return jnp.einsum('bhmd,bhme->bhde', k * w[None, :, :, None], v)

def retention_mixer(h_lat, h_ctx, ang_lat, ang_ctx, w_in, w_out, decay_logit, with_ctx_out):
    log_g = jax.nn.log_sigmoid(decay_logit.astype(jnp.float32))

    def heads(z, d):
        return z.reshape(z.shape[0], z.shape[1], RET_HEADS, d)

    def to_bhnd(t):
        return jnp.transpose(t, (0, 2, 1, 3))

    def qkvg(hh, ang):
        z = hh @ w_in
        q, k, v, g = jnp.split(z, [RET_QK_TOTAL, 2 * RET_QK_TOTAL, 2 * RET_QK_TOTAL + RET_V_TOTAL], -1)
        q = apply_rope(heads(q, RET_QK_DIM), ang) * (RET_QK_DIM ** -0.5)
        k = apply_rope(heads(k, RET_QK_DIM), ang)
        return to_bhnd(q), to_bhnd(k), to_bhnd(heads(v, RET_V_DIM)), g

    def bidir(q, k, v, s_f, s_b):
        fwd = retention_chunkwise(q, k, v, log_g[0], s_f)
        bwd = retention_chunkwise(jnp.flip(q, 2), jnp.flip(k, 2), jnp.flip(v, 2), log_g[1], s_b)
        return fwd + jnp.flip(bwd, 2)

    def readout(y, g):
        yf = y.astype(jnp.float32)
        yf = yf * lax.rsqrt(jnp.mean(yf * yf, -1, keepdims=True) + NORM_EPS)
        yb = jnp.transpose(yf.astype(y.dtype), (0, 2, 1, 3)).reshape(y.shape[0], y.shape[2], RET_V_TOTAL)
        return (yb * jax.nn.silu(g)) @ w_out

    if with_ctx_out:
        qc, kc, vc, gc = qkvg(h_ctx, ang_ctx)
    else:
        z = h_ctx @ w_in[:, RET_QK_TOTAL:2 * RET_QK_TOTAL + RET_V_TOTAL]
        kc_, vc_ = jnp.split(z, [RET_QK_TOTAL], -1)
        kc = to_bhnd(apply_rope(heads(kc_, RET_QK_DIM), ang_ctx))
        vc = to_bhnd(heads(vc_, RET_V_DIM))
    s_f = retention_final_state(kc, vc, log_g[0], False)
    s_b = retention_final_state(kc, vc, log_g[1], True)
    q, k, v, g = qkvg(h_lat, ang_lat)
    out_lat = readout(bidir(q, k, v, s_f, s_b), g)
    if with_ctx_out:
        zero = jnp.zeros_like(s_f)
        out_ctx = readout(bidir(qc, kc, vc, zero, zero), gc)
        return out_lat, out_ctx
    return out_lat, None

def conv_module(hh, w1, b1, w_dw, b_dw, ln_g, ln_b, w2, b2):
    z = hh @ w1 + b1
    a, gate = jnp.split(z, 2, -1)
    u = a * jax.nn.sigmoid(gate)
    u = lax.conv_general_dilated(u, w_dw[:, None, :].astype(u.dtype), window_strides=(1,),
                                 padding=[(CONV_WIDTH // 2, CONV_WIDTH // 2)],
                                 dimension_numbers=('NWC', 'WIO', 'NWC'),
                                 feature_group_count=D_MODEL) + b_dw
    uf = u.astype(jnp.float32)
    mu = jnp.mean(uf, -1, keepdims=True)
    var = jnp.mean(jnp.square(uf - mu), -1, keepdims=True)
    uf = (uf - mu) * lax.rsqrt(var + LN_EPS) * ln_g.astype(jnp.float32) + ln_b.astype(jnp.float32)
    u = jax.nn.silu(uf.astype(u.dtype))
    return u @ w2 + b2

def swiglu(t, w1, w3, w2):
    return (jax.nn.silu(t @ w1) * (t @ w3)) @ w2

def moe_ffn(hh, w_router, router_bias, w1, w3, w2, ws1, ws3, ws2):
    shp = hh.shape
    hf = hh.reshape(-1, D_MODEL)
    n = hf.shape[0]
    scores = jax.nn.sigmoid(hf.astype(jnp.float32) @ w_router.astype(jnp.float32))
    biased = scores + router_bias.astype(jnp.float32)
    per = N_EXPERTS // N_GROUPS
    grp_score = lax.top_k(biased.reshape(n, N_GROUPS, per), 2)[0].sum(-1)
    _, gidx = lax.top_k(grp_score, TOPK_GROUPS)
    gmask = jax.nn.one_hot(gidx, N_GROUPS, dtype=jnp.float32).sum(1) > 0
    emask = jnp.repeat(gmask, per, axis=1)
    _, eidx = lax.top_k(jnp.where(emask, biased, -jnp.inf), TOP_K)
    wsel = jnp.take_along_axis(scores, eidx, 1)
    wsel = wsel / wsel.sum(-1, keepdims=True) * ROUTE_SCALE
    a = n * TOP_K
    e_flat = eidx.reshape(a).astype(jnp.int32)
    tok_flat = jnp.arange(a, dtype=jnp.int32) // TOP_K
    w_flat = wsel.reshape(a)
    order = jnp.argsort(e_flat)
    e_s = e_flat[order]
    tok_s = tok_flat[order]
    w_s = w_flat[order]
    counts = jax.ops.segment_sum(jnp.ones(a, jnp.int32), e_flat, num_segments=N_EXPERTS)
    start = jnp.cumsum(counts) - counts
    pcounts = (counts + MOE_BLOCK - 1) // MOE_BLOCK * MOE_BLOCK
    pend = jnp.cumsum(pcounts)
    pstart = pend - pcounts
    dest = pstart[e_s] + (jnp.arange(a, dtype=jnp.int32) - start[e_s])
    n_rows = -(-a // MOE_BLOCK) * MOE_BLOCK + N_EXPERTS * MOE_BLOCK
    n_blk = n_rows // MOE_BLOCK
    row_tok = jnp.zeros(n_rows, jnp.int32).at[dest].set(tok_s)
    row_w = jnp.zeros(n_rows, jnp.float32).at[dest].set(w_s)
    blk_e = jnp.minimum(jnp.searchsorted(pend, jnp.arange(n_blk, dtype=jnp.int32) * MOE_BLOCK, side='right'),
                        N_EXPERTS - 1)

    def block(acc, inp):
        toks, ws, e = inp
        y = swiglu(hf[toks], w1[e], w3[e], w2[e])
        return acc.at[toks].add((y * ws[:, None]).astype(acc.dtype)), None

    routed, _ = lax.scan(block, jnp.zeros_like(hf),
                         (row_tok.reshape(n_blk, MOE_BLOCK), row_w.reshape(n_blk, MOE_BLOCK), blk_e))
    out = routed + swiglu(hf, ws1, ws3, ws2)
    return out.reshape(shp)

def setup_inputs(seed: int = 0) -> dict:
    key = jax.random.key(seed)
    ks = jax.random.split(key, 32)

    def nrm(k, shape, scale):
        return jax.random.normal(k, shape, jnp.float32) * scale

    D = D_MODEL
    p = 1.0 - 2.0 ** (-5.0 - np.arange(RET_HEADS))
    decay_base = jnp.asarray(np.log(p / (1.0 - p)), jnp.float32)
    return {
        'x': nrm(ks[0], (BATCH, SEQ, D), 1.0),
        'c': nrm(ks[1], (BATCH, D), 1.0),
        'ctx': nrm(ks[2], (BATCH, CTX_LEN, D), 1.0),
        'c_ctx': nrm(ks[3], (D,), 1.0),
        'mod_w': nrm(ks[4], (DEPTH, D, 6 * D), 0.5 * D ** -0.5),
        'mod_b': nrm(ks[5], (DEPTH, 6 * D), 0.02),
        'norms': 1.0 + nrm(ks[6], (DEPTH, 4, D), 0.05),
        'ret_w_in': nrm(ks[7], (N_RET_LAYERS, D, RET_IN_DIM), D ** -0.5),
        'ret_w_out': nrm(ks[8], (N_RET_LAYERS, RET_V_TOTAL, D), RET_V_TOTAL ** -0.5),
        'ret_decay': decay_base[None, None, :] + nrm(ks[9], (N_RET_LAYERS, 2, RET_HEADS), 0.1),
        'conv_w1': nrm(ks[10], (N_CONV_LAYERS, D, 2 * D), D ** -0.5),
        'conv_b1': nrm(ks[11], (N_CONV_LAYERS, 2 * D), 0.02),
        'conv_dw': nrm(ks[12], (N_CONV_LAYERS, CONV_WIDTH, D), CONV_WIDTH ** -0.5),
        'conv_b_dw': nrm(ks[13], (N_CONV_LAYERS, D), 0.02),
        'conv_ln_g': 1.0 + nrm(ks[14], (N_CONV_LAYERS, D), 0.05),
        'conv_ln_b': nrm(ks[15], (N_CONV_LAYERS, D), 0.02),
        'conv_w2': nrm(ks[16], (N_CONV_LAYERS, D, D), D ** -0.5),
        'conv_b2': nrm(ks[17], (N_CONV_LAYERS, D), 0.02),
        'moe_router': nrm(ks[18], (DEPTH, D, N_EXPERTS), D ** -0.5),
        'moe_bias': nrm(ks[19], (DEPTH, N_EXPERTS), 0.01),
        'moe_w1': nrm(ks[20], (DEPTH, N_EXPERTS, D, EXPERT_DIM), D ** -0.5),
        'moe_w3': nrm(ks[21], (DEPTH, N_EXPERTS, D, EXPERT_DIM), D ** -0.5),
        'moe_w2': nrm(ks[22], (DEPTH, N_EXPERTS, EXPERT_DIM, D), EXPERT_DIM ** -0.5),
        'shared_w1': nrm(ks[23], (DEPTH, D, SHARED_DIM), D ** -0.5),
        'shared_w3': nrm(ks[24], (DEPTH, D, SHARED_DIM), D ** -0.5),
        'shared_w2': nrm(ks[25], (DEPTH, SHARED_DIM, D), SHARED_DIM ** -0.5),
    }

def reference(x, c, ctx, c_ctx, mod_w, mod_b, norms, ret_w_in, ret_w_out, ret_decay,
              conv_w1, conv_b1, conv_dw, conv_b_dw, conv_ln_g, conv_ln_b, conv_w2, conv_b2,
              moe_router, moe_bias, moe_w1, moe_w3, moe_w2, shared_w1, shared_w3, shared_w2):
    T = x.shape[1]
    L = ctx.shape[1]
    ROWS = T // GRID_W
    rows, cols = jnp.meshgrid(jnp.arange(ROWS, dtype=jnp.int32), jnp.arange(GRID_W, dtype=jnp.int32), indexing='ij')
    pos_lat = jnp.stack([jnp.full((T,), L, jnp.int32), rows.reshape(-1), cols.reshape(-1)], -1)
    zl = jnp.zeros((L,), jnp.int32)
    pos_ctx = jnp.stack([jnp.arange(L, dtype=jnp.int32), zl, zl], -1)
    ang_lat = rope_angles(pos_lat)
    ang_ctx = rope_angles(pos_ctx)
    silu_c = jax.nn.silu(c)
    silu_cc = jax.nn.silu(c_ctx)

    h, hc = x, ctx
    for i in range(DEPTH):
        kind = i % N_MIXERS
        j = i // N_MIXERS
        ctx_after = any((l % N_MIXERS) == 0 for l in range(i + 1, DEPTH))
        mod = (silu_c @ mod_w[i] + mod_b[i])[:, None, :]
        sh_m, sc_m, g_m, sh_f, sc_f, g_f = jnp.split(mod, 6, -1)
        if kind == 0 or ctx_after:
            mod_c = silu_cc @ mod_w[i] + mod_b[i]
            csh_m, csc_m, cg_m, csh_f, csc_f, cg_f = jnp.split(mod_c, 6, -1)
            uc = modulate(rms_norm(hc, norms[i, 0]), csh_m, csc_m)
        u = modulate(rms_norm(h, norms[i, 0]), sh_m, sc_m)
        if kind == 0:
            y, yc = retention_mixer(u, uc, ang_lat, ang_ctx, ret_w_in[j], ret_w_out[j], ret_decay[j], ctx_after)
        else:
            conv_args = (conv_w1[j], conv_b1[j], conv_dw[j], conv_b_dw[j], conv_ln_g[j], conv_ln_b[j],
                         conv_w2[j], conv_b2[j])
            y = conv_module(u, *conv_args)
            yc = conv_module(uc, *conv_args) if ctx_after else None
        h = h + g_m * rms_norm(y, norms[i, 1])
        moe_args = (moe_router[i], moe_bias[i], moe_w1[i], moe_w3[i], moe_w2[i],
                    shared_w1[i], shared_w3[i], shared_w2[i])
        u = modulate(rms_norm(h, norms[i, 2]), sh_f, sc_f)
        h = h + g_f * rms_norm(moe_ffn(u, *moe_args), norms[i, 3])
        if ctx_after:
            hc = hc + cg_m * rms_norm(yc, norms[i, 1])
            uc = modulate(rms_norm(hc, norms[i, 2]), csh_f, csc_f)
            hc = hc + cg_f * rms_norm(moe_ffn(uc, *moe_args), norms[i, 3])
    return h


_drawn_inputs = setup_inputs


def setup_inputs(seed=0):
    import zlib

    import numpy as np

    out = dict(_drawn_inputs(seed))
    spreads = {}
    factors = {'conv_b1': 3.302, 'conv_ln_b': 3.652, 'conv_b2': 2.819}
    for name, (base, spread) in spreads.items():
        noise = np.random.default_rng([zlib.crc32(name.encode()), seed]).standard_normal(out[name].shape)
        drawn = base * np.exp(spread * noise) if base else spread * noise
        out[name] = __import__('jax').numpy.asarray(drawn.astype(out[name].dtype))
    for name, factor in factors.items():
        out[name] = (out[name] * factor).astype(out[name].dtype)
    return out
```

```python
from contextlib import ExitStack

import numpy as np

import concourse.bass as bass
from concourse import mybir

ALU = mybir.AluOpType
ACT = mybir.ActivationFunctionType
AX = mybir.AxisListType
F32 = mybir.dt.float32
I32 = mybir.dt.int32
ds = bass.ds

P = 128
D = 1024
KT = D // P
SEQ = 512
CTX = 256
NT = SEQ // P
HEADS = 4
DK = D // HEADS
DV = 2 * DK
KEYT = (SEQ + CTX) // P
W = 512
MODW = 6 * D
TAPS = 31
HALO = TAPS // 2
NE = 64
TOPK = 8
NG = 8
PER = NE // NG
F = 256
FT = F // P
ROUTE_SCALE = 2.5
BLOCKS = 128
PAIRS = 48
BIG = float(BLOCKS * P)
MARK = 3.0e38
LOW = -1.0e30
BAND = 640 + SEQ + CTX

C_ID = 0
C_TRI = C_ID + P
C_TRII = C_TRI + P
C_ONE = C_TRII + P
C_IOTA = C_ONE + P
C_POS = C_IOTA + P
C_COS = C_POS + BAND
C_SIN = C_COS + SEQ + CTX
C_TOK = C_SIN + SEQ + CTX
C_THR = C_TOK + NT
C_EPS = C_THR + NT
C_ALL = C_EPS + 2


def shape_constants():
    c = np.zeros((P, C_ALL), np.float32)
    r = np.arange(P)
    c[:, C_ID:C_ID + P] = np.eye(P)
    c[:, C_TRI:C_TRI + P] = r[:, None] < r[None, :]
    c[:, C_TRII:C_TRII + P] = r[:, None] <= r[None, :]
    c[:, C_ONE:C_ONE + P] = 1.0
    c[:, C_IOTA:C_IOTA + P] = r[None, :]
    c[:, C_POS:C_POS + BAND] = np.arange(BAND)[None, :] - 640 - r[:, None]
    at = np.arange(SEQ)
    lat = np.stack([np.full(SEQ, CTX), at // 64, at % 64], -1)
    ctx = np.stack([np.arange(CTX), np.zeros(CTX), np.zeros(CTX)], -1)
    pos = np.concatenate([lat, ctx]).astype(np.float32)
    ang = []
    for a, d in enumerate((64, 96, 96)):
        inv = (10000.0 ** (-np.arange(0, d, 2, dtype=np.float32) / np.float32(d))).astype(np.float32)
        ang.append(pos[:, a:a + 1] * inv[None, :])
    ang = np.concatenate(ang, -1).astype(np.float64).T
    c[:, C_COS:C_COS + SEQ + CTX] = np.cos(ang)
    c[:, C_SIN:C_SIN + SEQ + CTX] = np.sin(ang)
    c[:, C_TOK:C_TOK + NT] = r[:, None] + P * np.arange(NT)[None, :]
    c[:, C_THR:C_THR + NT] = P * np.arange(NT)[None, :]
    c[:, C_EPS] = 1e-6
    c[:, C_EPS + 1] = 1e-5
    return c


class Steps:

    def __init__(self, eng, sem):
        self.eng, self.sem, self.n = eng, sem, 0

    def done(self, ins):
        ins.then_inc(self.sem, 1)
        self.n = self.n + 1
        return self.n

    def then(self, ins):
        self.eng.wait_ge(self.sem, self.done(ins))


def peeled(eng, n):
    yield 0
    with eng.Fori(1, n) as i:
        yield i


def after(eng, sem, n):
    if not isinstance(n, int) or n > 0:
        eng.wait_ge(sem, n)


def build(nc, x, c, ctx, c_ctx, mod_w, mod_b, norms, ret_w_in, ret_w_out, ret_decay,
          conv_w1, conv_b1, conv_dw, conv_b_dw, conv_ln_g, conv_ln_b, conv_w2, conv_b2,
          moe_router, moe_bias, moe_w1, moe_w3, moe_w2, shared_w1, shared_w3, shared_w2,
          consts, out):
    with ExitStack() as stack:
        def sem(name):
            return stack.enter_context(nc.semaphore(name))

        def sb(name, cols, dt=F32):
            return stack.enter_context(nc.sbuf_tensor(name, [P, cols], dt))

        mod_rows = nc.dram_tensor("mod_rows", [2, 2, MODW], F32, kind="Internal").ap()
        u_rows = [nc.dram_tensor(f"u_rows{i}", [SEQ, D], F32, kind="Internal").ap() for i in range(2)]
        slot_tok = [nc.dram_tensor(f"slot_tok{i}", [BLOCKS * P, 1], F32, kind="Internal").ap() for i in range(2)]
        y_rows = nc.dram_tensor("y_rows", [2 * PAIRS * P, D], F32, kind="Internal").ap()

        cst = sb("cst", C_ALL)
        h = sb("h", NT * D)[:, :].rearrange("p (j d) -> p j d", j=NT)
        modb = sb("modb", MODW)[:, :].rearrange("p (r d) -> p r d", r=6)
        uT = sb("uT", KT * SEQ)[:, :].rearrange("p (t n) -> p t n", t=KT)
        ring_all = sb("ring", 4 * KT * W)
        ring = [ring_all[:, s * KT * W:(s + 1) * KT * W] for s in range(4)]
        col = sb("col", 160)
        arena_cols = 18700
        arena = sb("arena", arena_cols)
        ps = stack.enter_context(nc.psum_tensor("ps", [P, 8, W], F32))

        ident = cst[:, C_ID:C_ID + P]
        ones = cst[:, C_ONE:C_ONE + P]
        cos = cst[:, C_COS:C_COS + SEQ + CTX]
        sin = cst[:, C_SIN:C_SIN + SEQ + CTX]
        eps_norm = cst[:, C_EPS:C_EPS + 1]
        eps_ln = cst[:, C_EPS + 1:C_EPS + 2]

        ss = col[:, 0:8]
        sd = col[:, 8:16]
        rs = col[:, 16:24]
        dec = col[:, 24:32]
        dec_t = [col[:, 32 + 8 * i:40 + 8 * i] for i in range(6)]
        lgf = col[:, 80:84]
        nlgb = col[:, 84:88]
        c_raw = col[:, 96:112].rearrange("p (r t) -> p r t", r=2)
        c_act = col[:, 112:128].rearrange("p (t r) -> p t r", r=2)

        def view(off, n):
            assert off + n <= arena_cols
            return arena[:, off:off + n]

        yT = view(0, 8192).rearrange("p (c n) -> p c n", c=4 * HEADS)
        ctx_x = view(0, 2048).rearrange("p (j d) -> p j d", j=2)
        cmod = view(2048, 2048).rearrange("p (r d) -> p r d", r=2)
        nrm = view(4096, 4096).rearrange("p (r d) -> p r d", r=4)
        uTc = view(8192, 2048).rearrange("p (t n) -> p t n", t=KT)
        qT = view(10240, 1024).rearrange("p (e n) -> p e n", e=2)
        kT = view(11264, 1536).rearrange("p (e n) -> p e n", e=2)
        osq = view(10240, 2048).rearrange("p (c n) -> p c n", c=4)
        sgT = view(12800, 2048).rearrange("p (c n) -> p c n", c=4)
        ST = view(14848, 3072).rearrange("p (m n) -> p m n", m=KEYT)
        rot = view(14848, 2048).rearrange("p (i n) -> p i n", i=4)
        orstd = view(17920, 512)
        ubuf = view(14848, 2048).rearrange("p (s d) -> p s d", s=2)
        junk = view(16896, 1024)
        band = modb[:, 0:2, :].rearrange("p r d -> p (r d)")[:, 0:BAND]
        otmp = modb[:, 0:2, :].rearrange("p r d -> p (r d)")[:, BAND:BAND + SEQ]
        zrow = modb[:, 0:2, :].rearrange("p r d -> p (r d)")[:, BAND + SEQ:2 * D]
        V = ring[3][:, 0:KEYT * W].rearrange("p (m n) -> p m n", m=KEYT)
        dctx = ring[3][:, KEYT * W:KT * W].rearrange("p (m n) -> p m n", m=2)
        brow = view(12800, 1024).rearrange("p (s n) -> p s n", s=2)[0:2]
        mrow = view(13824, 1024).rearrange("p (s n) -> p s n", s=2)[0:2]

        zin = view(0, KT * (SEQ + 2 * HALO)).rearrange("p (c n) -> p c n", c=KT)
        cacc = view(4352, 4096).rearrange("p (c n) -> p c n", c=KT)
        sgate = view(8448, 1024).rearrange("p (s n) -> p s n", s=2)
        chp = view(9472, 8 * 36).rearrange("p (c k) -> p c k", c=KT)
        chrow = view(9760, 1024)
        b2row = view(10784, 1024)
        mu = view(11808, 512)
        lrs = view(12320, 512)
        lsq = view(12832, 1024).rearrange("p (s n) -> p s n", s=2)
        ybuf = view(13856, 4096).rearrange("p (j d) -> p j d", j=NT)
        cubuf = view(0, 2048).rearrange("p (s d) -> p s d", s=2)
        cjunk = view(2048, 1024)

        xg = view(0, 2048).rearrange("p (s d) -> p s d", s=2)
        xT = view(2048, 2048).rearrange("p (s t n) -> p s t n", s=2, t=KT)
        gbuf = view(0, 4096).rearrange("p (s d) -> p s d", s=4)
        yb = view(4096, 2048).rearrange("p (s d) -> p s d", s=2)
        macc = view(6144, 4096).rearrange("p (j d) -> p j d", j=NT)
        mubuf = view(10240, 2048).rearrange("p (s d) -> p s d", s=2)
        hsT = view(12288, 1024).rearrange("p (f n) -> p f n", f=FT)
        sgs = view(13312, 1024).rearrange("p (f n) -> p f n", f=FT)
        ex_g = view(10240, 512).rearrange("p (s n) -> p s n", s=2)
        ex_h = view(10752, 512).rearrange("p (s n) -> p s n", s=2)
        ex_hT = view(11264, 512).rearrange("p (s f n) -> p s f n", s=2, f=FT)
        idx_col = view(11776, 2).bitcast(I32)
        mjunk = view(13312, 1024)
        at = 14336

        def small(n):
            nonlocal at
            at += n
            return view(at - n, n)

        wr = small(KT * NE).rearrange("p (t e) -> p t e", t=KT)
        score = small(256).rearrange("p (j e) -> p j e", j=NT)
        bias = small(64)
        biased = small(256).rearrange("p (j e) -> p j e", j=NT)
        gtop = small(256).rearrange("p (j g k) -> p j g k", j=NT, g=NG)
        gsx = small(48).rearrange("p (j k) -> p j k", j=NT)
        gmax = small(32).rearrange("p (j k) -> p j k", j=NT)
        grep = small(32).rearrange("p (j k) -> p j k", j=NT)
        gout = small(48).rearrange("p (j k) -> p j k", j=NT)
        gmask = small(32).rearrange("p (j g) -> p j g", j=NT)
        gneg = small(32).rearrange("p (j g) -> p j g", j=NT)
        top8 = small(32).rearrange("p (j k) -> p j k", j=NT)
        rep = small(256).rearrange("p (j e) -> p j e", j=NT)
        sel = small(256).rearrange("p (j e) -> p j e", j=NT)
        wn = small(256).rearrange("p (j e) -> p j e", j=NT)
        wsum = small(8)
        slotk = small(256).rearrange("p (j e) -> p j e", j=NT)
        topslot = small(32).rearrange("p (j k) -> p j k", j=NT)
        dest = small(32).bitcast(I32).rearrange("p (j k) -> p j k", j=NT)
        eq = small(512).rearrange("p (k e) -> p k e", k=TOPK)
        wk = small(32).rearrange("p (j k) -> p j k", j=NT)
        cnt = small(12)
        nblk_b = small(P)
        started = small(P)
        ctrl = small(BLOCKS + 2).bitcast(I32)
        slots = small(P)
        tok_idx = small(BLOCKS).bitcast(I32)
        zero = small(P)

        def expert(s):
            w = ring_all[:, s * 6144:(s + 1) * 6144]
            return (w[:, 0:2048].rearrange("p (t f) -> p t f", t=KT), w[:, 2048:4096].rearrange("p (t f) -> p t f", t=KT),
                    w[:, 4096:6144].rearrange("p (f d) -> p f d", f=FT))

        s_const, s_c, s_x, s_ctx, s_decay = (sem(n) for n in ("const_in", "c_in", "x_in", "ctx_in", "decay_in"))
        s_cact = sem("c_silu")
        s_mw = [sem(f"mod_panel_in{s}") for s in range(2)]
        s_mbias = [sem(f"mod_bias_in{s}") for s in range(2)]
        s_mps = [sem(f"mod_product{s}") for s in range(2)]
        s_mrow = [sem(f"mod_row{s}") for s in range(2)]
        s_mout = [sem(f"mod_stored{s}") for s in range(2)]
        s_modb = [sem(f"mod_bcast_in{i}") for i in range(2)]
        s_cmod = sem("ctx_mod_in")
        s_folded = [sem(f"mod_folded{i}") for i in range(2)]
        s_dve, s_act, s_pool = sem("dve_steps"), sem("act_steps"), sem("pool_steps")
        s_log = sem("decay_exp")

        s_nrms, s_nu, s_ntp, s_ncp = (sem(n) for n in ("norm_rms", "norm_u", "norm_turned", "norm_uT"))

        class Norm:
            def __init__(self, stage, tile):
                self.stage, self.tile = stage, tile

        n_ctx, n_mix, n_moe = Norm(0, 0), [Norm(1, 2), Norm(3, 10)], [Norm(2, 6), Norm(4, 14)]
        s_y, s_yrms, s_h = sem("mixer_y"), sem("y_rms"), sem("h_added")
        h_base = {"ret": 0, "moe0": 2 * NT, "conv": 4 * NT, "moe1": 6 * NT}

        s_zrow, s_zfill = sem("zero_row"), sem("results_zeroed")
        s_wqk, s_wv, s_wg = sem("qk_panel_in"), sem("v_panel_in"), sem("g_panel_in")
        s_q, s_k, s_kc = sem("q_product"), sem("k_product"), sem("kctx_product")
        s_qkr = sem("qk_rotated")
        s_v, s_vc = sem("v_product"), sem("v_copied")
        s_g, s_gc = sem("g_product"), sem("g_silu")
        s_band, s_bexp, s_bandok = sem("band_exponent"), sem("band_exp"), sem("band_ready")
        s_s, s_sc = sem("scores"), sem("scores_decayed")
        s_o, s_osq, s_oss, s_ord, s_yT = (sem(n) for n in ("o_product", "o_squared", "o_sumsq", "o_rms", "yT_head"))
        s_wo = [sem(f"w_out_in{s}") for s in range(4)]

        s_cw1 = [sem(f"conv_w1_in{s}") for s in range(4)]
        s_crow, s_ccolp, s_ccol = sem("conv_rows_in"), sem("conv_cols_product"), sem("conv_cols")
        s_cag, s_csg, s_zin = sem("conv_glu_product"), sem("conv_gate"), sem("conv_glu")
        s_tap, s_lmu, s_lmuc, s_lcen = sem("conv_taps"), sem("ln_sum"), sem("ln_mean"), sem("ln_centred")
        s_lsq, s_lvar, s_lsd, s_lnx, s_lnu = (sem(n) for n in ("ln_squared", "ln_sumsq", "ln_std", "ln_scaled", "conv_act"))
        s_cw2 = [sem(f"conv_w2_in{s}") for s in range(2)]
        s_cb2 = sem("conv_b2_in")
        s_cy = sem("conv_w2_product")

        class MoeFixed:

            def __init__(self, t):
                self.wr, self.bias = sem(t + "router_in"), sem(t + "bias_in")
                self.urow = [sem(t + f"u_stored{s}") for s in range(2)]
                self.logit, self.score = sem(t + "logits"), sem(t + "scores")
                self.sel, self.cnt, self.nblk = sem(t + "selected"), sem(t + "counts"), sem(t + "blocks")
                self.pos, self.started, self.blk = sem(t + "slots"), sem(t + "started"), sem(t + "block_experts")
                self.ctrl, self.dest = sem(t + "control"), sem(t + "dest")
                self.zero, self.zeroed, self.scat = sem(t + "zero"), sem(t + "list_zeroed"), sem(t + "list_written")
                self.list, self.listT, self.tok = sem(t + "list_in"), sem(t + "list_turned"), sem(t + "token_index")
                self.sw = sem(t + "shared_in")
                self.sup, self.ssg, self.sh = sem(t + "shared_up"), sem(t + "shared_silu"), sem(t + "shared_h")
                self.sy, self.sacc = sem(t + "shared_y"), sem(t + "shared_sum")
                self.tail = sem(t + "blocks_done")
                self.gb = [sem(t + f"result_gathered{s}") for s in range(4)]
                self.gu = sem(t + "result_added")

        class MoeLoop:

            def __init__(self, t):
                self.w1 = [sem(t + f"w1_in{s}") for s in range(2)]
                self.w3 = [sem(t + f"w3_in{s}") for s in range(2)]
                self.w2 = [sem(t + f"w2_in{s}") for s in range(2)]
                self.idx = sem(t + "index")
                self.xg = [sem(t + f"x_gathered{s}") for s in range(2)]
                self.xt = sem(t + "x_turned")
                self.xc = sem(t + "xT")
                self.g1 = sem(t + "gate_product")
                self.up = sem(t + "up_product")
                self.sg = sem(t + "gate_silu")
                self.hm = sem(t + "expert_h")
                self.ht = sem(t + "expert_h_turned")
                self.hc = sem(t + "expert_hT")
                self.y = sem(t + "expert_y")
                self.yc = sem(t + "expert_y_copied")
                self.yo = [sem(t + f"expert_y_stored{s}") for s in range(2)]

        mf = MoeFixed("moe_")
        mo = [MoeLoop(f"moe{i}_") for i in range(2)]
        s_out = sem("out_stored")

        win = ret_w_in[0].rearrange("(p t) n -> p t n", t=KT)
        wqk = ring[0].rearrange("p (t n) -> p t n", t=KT)
        wv = ring[1].rearrange("p (t n) -> p t n", t=KT)
        wg = ring[2].rearrange("p (t n) -> p t n", t=KT)
        wo = [r.rearrange("p (c n) -> p c n", c=4) for r in ring]
        wo_dram = ret_w_out[0].rearrange("(h c p) n -> h p c n", h=HEADS, p=P)
        panel = [r.rearrange("p (t n) -> p t n", t=KT) for r in ring]

        block = stack.enter_context(nc.Block())

        @block.sync
        def _(sp):
            sp.dma_start(cst[:, :], consts).then_inc(s_const, 16)
            sp.dma_start(c_raw[:, 0, :], c[0].rearrange("(p t) -> p t", t=KT)).then_inc(s_c, 16)
            sp.dma_start(c_raw[:, 1, :], c_ctx.rearrange("(p t) -> p t", t=KT)).then_inc(s_c, 16)

            for i in range(2):
                for n in peeled(sp, MODW // W // 2):
                    for s in range(2):
                        after(sp, s_mps[s], n + 6 * i)
                        sp.dma_start(panel[s], mod_w[i].rearrange("(p t) n -> p t n", t=KT)[:, :, ds(n * (2 * W) + s * W, W)])\
                            .then_inc(s_mw[s], 16)
                        after(sp, s_mrow[s], n + 6 * i)
                        for r in range(2):
                            sp.dma_start(brow[r:r + 1, s, :], mod_b[i:i + 1, ds(n * (2 * W) + s * W, W)])\
                                .then_inc(s_mbias[s], 16)
            sp.dma_start(h, x[0].rearrange("(j p) d -> p j d", p=P)).then_inc(s_x, 16)
            sp.dma_start(ctx_x, ctx[0].rearrange("(j p) d -> p j d", p=P)).then_inc(s_ctx, 16)
            sp.dma_start(dec, ret_decay[0].rearrange("a h -> (a h)").partition_broadcast(P)).then_inc(s_decay, 16)
            sp.dma_start(nrm.rearrange("p r d -> p (r d)"), norms[0].rearrange("r d -> (r d)").partition_broadcast(P)).then_inc(s_modb[0], 16)
            for s in range(2):
                sp.wait_ge(s_mout[s], 16 * 12)
            sp.dma_start(modb.rearrange("p r d -> p (r d)"), mod_rows[0, 0].partition_broadcast(P)).then_inc(s_modb[0], 16)
            sp.dma_start(cmod.rearrange("p r d -> p (r d)"), mod_rows[0, 1, 0:2 * D].partition_broadcast(P)).then_inc(s_cmod, 16)

            for s in range(2):
                sp.wait_ge(s_mps[s], 12)
            for hd in peeled(sp, HEADS):
                after(sp, s_kc, hd)
                sp.dma_start(wqk[:, :, 0:DK], win[:, :, ds(hd * DK, DK)]).then_inc(s_wqk, 16)
                sp.dma_start(wqk[:, :, DK:2 * DK], win[:, :, ds(hd * DK + D, DK)]).then_inc(s_wqk, 16)
                after(sp, s_v, hd * KEYT)
                sp.dma_start(wv, win[:, :, ds(hd * DV + 2 * D, DV)]).then_inc(s_wv, 16)
                after(sp, s_g, hd * 4)
                sp.dma_start(wg, win[:, :, ds(hd * DV + 4 * D, DV)]).then_inc(s_wg, 16)
                sp.wait_ge(s_zrow, 1)
                for g in range(4):
                    rows = y_rows.rearrange("(b p q) d -> b p (q d)", p=P, q=4)[ds(hd * 4 + (8 + g), 1), :, :]
                    sp.dma_start(rows.rearrange("b p (r z) -> p (b r) z", z=P), zrow.unsqueeze(1).to_broadcast([P, 4 * D // P, P])).then_inc(s_zfill, 16)
            sp.wait_ge(s_zfill, 16 * HEADS * 4)
            sp.wait_ge(s_kc, HEADS)
            sp.dma_start(wo[0], wo_dram[0]).then_inc(s_wo[0], 16)
            sp.wait_ge(s_v, HEADS * KEYT)
            sp.dma_start(wo[1], wo_dram[1]).then_inc(s_wo[1], 16)
            sp.wait_ge(s_g, HEADS * 4)
            sp.dma_start(wo[2], wo_dram[2]).then_inc(s_wo[2], 16)
            sp.wait_ge(s_o, HEADS * 4)
            sp.dma_start(wo[3], wo_dram[3]).then_inc(s_wo[3], 16)

            def moe(i, mixer, mixer_y):
                m = mo[i]
                sp.wait_ge(s_h, h_base[mixer] + 2 * NT)
                sp.dma_start(wr, moe_router[i].rearrange("(p t) e -> p t e", t=KT)).then_inc(mf.wr, 16)
                sp.dma_start(bias, moe_bias[i].partition_broadcast(P)).then_inc(mf.bias, 16)
                w1, w3, w2 = expert(1)
                sp.dma_start(w1, shared_w1[i].rearrange("(p t) f -> p t f", t=KT)).then_inc(mf.sw, 16)
                sp.dma_start(w3, shared_w3[i].rearrange("(p t) f -> p t f", t=KT)).then_inc(mf.sw, 16)
                sp.dma_start(w2, shared_w2[i].rearrange("(p f) d -> p f d", f=FT)).then_inc(mf.sw, 16)
                sp.wait_ge(mf.zero, i + 1)
                sp.dma_start(slot_tok[i].rearrange("(p n) o -> p (n o)", p=P), zero).then_inc(mf.zeroed, 16)
                for j in range(NT):
                    sp.wait_ge(s_nu, n_moe[i].tile + j + 1)
                    sp.dma_start(u_rows[i][j * P:(j + 1) * P, :], mubuf[:, j % 2, :]).then_inc(mf.urow[j % 2], 16)
                sp.wait_ge(mf.ctrl, i + 1)
                pairs = sp.value_load(ctrl[0:1, BLOCKS:BLOCKS + 1], min_val=1, max_val=PAIRS)

                def load(s, b):
                    e = sp.value_load(ctrl[0:1, ds(b, 1)] if not isinstance(b, int) else ctrl[0:1, b:b + 1], min_val=0, max_val=NE - 1)
                    w1, w3, w2 = expert(s)
                    sp.dma_start(w1, moe_w1[i].rearrange("e (p t) f -> p e (t f)", t=KT)[:, ds(e, 1), :].rearrange("p e (t f) -> p (e t) f", t=KT)).then_inc(m.w1[s], 16)
                    sp.dma_start(w3, moe_w3[i].rearrange("e (p t) f -> p e (t f)", t=KT)[:, ds(e, 1), :].rearrange("p e (t f) -> p (e t) f", t=KT)).then_inc(m.w3[s], 16)
                    return w2, e

                def load2(s, w2, e):
                    sp.dma_start(w2, moe_w2[i].rearrange("e (p f) d -> p e (f d)", f=FT)[:, ds(e, 1), :].rearrange("p e (f d) -> p (e f) d", f=FT)).then_inc(m.w2[s], 16)

                load2(0, *load(0, 0))
                sp.wait_ge(mf.scat, i * 16 * NT * TOPK + 16 * NT * TOPK)
                sp.dma_start(slots, slot_tok[i].rearrange("(b s) o -> b (s o)", s=P)).then_inc(mf.list, 16)
                sp.wait_ge(mf.sy, i * 2 * NT + 2 * NT)
                load2(1, *load(1, 1))
                with sp.Fori(1, pairs) as it:
                    for s in range(2):
                        after(sp, m.up, it * 2 + (s - 1))
                        w2, e = load(s, it * 2 + s)
                        after(sp, m.y, it * 2 + (s - 1))
                        load2(s, w2, e)

            moe(0, "ret", None)

            sp.wait_ge(s_h, h_base["moe0"] + 2 * NT)
            sp.dma_start(nrm.rearrange("p r d -> p (r d)"), norms[1].rearrange("r d -> (r d)").partition_broadcast(P)).then_inc(s_modb[1], 16)
            sp.dma_start(modb.rearrange("p r d -> p (r d)"), mod_rows[1, 0].partition_broadcast(P)).then_inc(s_modb[1], 16)
            cw1 = conv_w1[0].rearrange("(p t) n -> p t n", t=KT)
            for s in (0, 2, 1, 3):
                sp.dma_start(panel[s], cw1[:, :, s * W:(s + 1) * W]).then_inc(s_cw1[s], 16)
            sp.wait_ge(s_folded[1], 5)
            for r, a in enumerate([conv_dw[0], conv_b_dw, conv_ln_g, conv_ln_b, conv_b1[0:1, 0:D], conv_b1[0:1, D:2 * D]]):
                r0 = 0 if r == 0 else TAPS - 1 + r
                n = TAPS if r == 0 else 1
                sp.dma_start(chrow[r0:r0 + n, :], a).then_inc(s_crow, 16)
            sp.dma_start(b2row, conv_b2[0].partition_broadcast(P)).then_inc(s_cb2, 16)
            cw2 = conv_w2[0].rearrange("(c p) n -> p c n", p=P)
            sp.wait_ge(s_cag, 4)
            for s in range(2):
                sp.dma_start(panel[2 * s], cw2[:, :, s * W:(s + 1) * W]).then_inc(s_cw2[s], 16)
            moe(1, "conv", None)
            for j in range(NT):
                sp.wait_ge(s_h, h_base["moe1"] + 2 * (j + 1))
                sp.dma_start(out[0, j * P:(j + 1) * P, :], h[:, j, :]).then_inc(s_out, 16)
            sp.wait_ge(s_out, 16 * NT)

        @block.gpsimd
        def _(pool):
            def moe(i, mixer):
                m = mo[i]
                pool.wait_ge(s_h, h_base[mixer] + 2 * NT)
                pool.memset(zero, 0.0).then_inc(mf.zero, 1)
                pool.wait_ge(mf.zeroed, i * 16 + 16)
                pool.wait_ge(mf.dest, i * NT + NT)
                for j in range(NT):
                    for k in range(TOPK):
                        pool.indirect_dma_start(slot_tok[i], bass.IndirectOffsetOnAxis(ap=dest[:, j, k:k + 1], axis=0),
                                                cst[:, C_TOK + j:C_TOK + j + 1], None).then_inc(mf.scat, 16)
                pool.wait_ge(mf.tok, i + 1)
                for s in range(2):
                    pool.wait_ge(mf.urow[s], i * (32) + 32)
                pool.wait_ge(mf.ctrl, i + 1)
                pairs = pool.value_load(ctrl[0:1, BLOCKS:BLOCKS + 1], min_val=1, max_val=PAIRS)

                def gather(s, b):
                    colb = tok_idx[:, b:b + 1] if isinstance(b, int) else tok_idx[:, ds(b, 1)]
                    pool.tensor_copy(idx_col[:, s:s + 1], colb).then_inc(m.idx, 1)
                    pool.wait_ge(m.idx, b + 1)
                    pool.sem_inc(s_pool, 1)
                    pool.indirect_dma_start(xg[:, s, :], None, u_rows[i], bass.IndirectOffsetOnAxis(ap=idx_col[:, s:s + 1], axis=0))\
                        .then_inc(m.xg[s], 16)

                gather(0, 0)
                for it in peeled(pool, pairs):
                    after(pool, m.xt, it * 2)
                    gather(1, it * 2 + 1)
                    after(pool, m.xt, it * 2 + 1)
                    gather(0, it * 2 + 2)
                pool.wait_ge(mf.tail, i + 1)
                for n in range(NT * TOPK):
                    if n >= 4:
                        after(pool, mf.gu, i * NT * TOPK + n - 3)
                    j, k = divmod(n, TOPK)
                    pool.indirect_dma_start(gbuf[:, n % 4, :], None, y_rows, bass.IndirectOffsetOnAxis(ap=dest[:, j, k:k + 1], axis=0))\
                        .then_inc(mf.gb[n % 4], 16)

            moe(0, "ret")
            moe(1, "conv")

        @block.scalar
        def _(act):
            st = Steps(act, s_act)

            def rms(ns, tiles, src, junk, ready):
                for j in range(tiles):
                    ready(j)
                    st.then(act.activation(junk, src(j), ACT.Square, accum_out=ss[:, j:j + 1]))
                act.activation(sd[:, 0:tiles], ss[:, 0:tiles], ACT.Sqrt, bias=eps_norm, scale=1.0 / D).then_inc(ns, 1)

            def to_uT(ns, tiles, dst):
                for j in range(tiles):
                    act.wait_ge(s_ntp, ns.tile + j + 1)
                    act.activation(dst[:, :, j * P:(j + 1) * P],
                                   ps[:, 2 * (j % 2):2 * (j % 2) + 2, :].rearrange("p b (t n) -> p (b t) n", n=P), ACT.Copy)\
                        .then_inc(s_ncp, 1)

            act.wait_ge(s_c, 32)
            act.activation(c_act.rearrange("p t r -> p r t"), c_raw, ACT.Silu).then_inc(s_cact, 1)
            for i in range(2):
                for n in peeled(act, MODW // W // 2):
                    for s in range(2):
                        after(act, s_mrow[s], n + (6 * i + 1))
                        act.dma_start(mod_rows[i, :, ds(n * (2 * W) + s * W, W)], mrow[:, s, :]).then_inc(s_mout[s], 16)
            act.wait_ge(s_decay, 16)
            act.wait_ge(s_log, 1)
            act.activation(dec_t[1], dec_t[0], ACT.Exp, scale=-1.0).then_inc(s_log, 1)
            act.wait_ge(s_const, 16)
            act.wait_ge(s_ctx, 16)
            rms(s_nrms, 2, lambda j: ctx_x[:, j, :], junk, lambda j: None)
            to_uT(n_ctx, 2, uTc)
            act.wait_ge(s_x, 16)
            rms(s_nrms, NT, lambda j: h[:, j, :], junk, lambda j: None)
            to_uT(n_mix[0], NT, uT)

            for hd in peeled(act, HEADS):
                after(act, s_band, hd + 1)
                act.activation(band, band, ACT.Exp).then_inc(s_bexp, 1)
                after(act, s_o, hd * 4)
                for m in range(KEYT):
                    after(act, s_v, hd * KEYT + (m + 1))
                    act.activation(V[:, m, :], ps[:, 5 + m % 3, :], ACT.Copy).then_inc(s_vc, 1)
                after(act, s_yT, hd * 4)
                for m in range(4):
                    after(act, s_g, hd * 4 + (m + 1))
                    act.activation(sgT[:, m, :], ps[:, 5 + m % 3, :], ACT.Silu).then_inc(s_gc, 1)
                for m in range(4):
                    after(act, s_o, hd * 4 + (m + 1))
                    act.activation(osq[:, m, :], ps[:, 4 + m, :], ACT.Square).then_inc(s_osq, 1)
                after(act, s_oss, hd + 1)
                act.activation(orstd, ps[:, 3, :], ACT.Sqrt, bias=eps_norm, scale=1.0 / DV).then_inc(s_ord, 1)

            def residual(key, src, junk, per_tile):
                rms(s_yrms, NT, src, junk, per_tile)

            residual("ret", lambda j: ps[:, 2 * j:2 * j + 2, :].rearrange("p b n -> p (b n)"), junk,
                     lambda j: act.wait_ge(s_y, j + 1))

            def moe(i, mixer):
                m = mo[i]
                act.wait_ge(s_h, h_base[mixer] + 2 * NT)
                rms(s_nrms, NT, lambda j: h[:, j, :], mjunk, lambda j: None)
                to_uT(n_moe[i], NT, uT)
                act.wait_ge(mf.logit, i + 1)
                act.activation(score, ps[:, 4, 0:NT * NE].rearrange("p (j e) -> p j e", j=NT), ACT.Sigmoid).then_inc(mf.score, 1)
                for f in range(FT):
                    act.wait_ge(mf.sup, i * 2 * FT + f + 1)
                    act.activation(sgs[:, f, :], ps[:, f, :], ACT.Silu).then_inc(mf.ssg, 1)
                for j in range(NT):
                    act.wait_ge(mf.sy, i * 2 * NT + 2 * j + 2)
                    act.activation(macc[:, j, :], ps[:, 4 + 2 * (j % 2):6 + 2 * (j % 2), :].rearrange("p b n -> p (b n)"), ACT.Copy)\
                        .then_inc(mf.sacc, 1)
                act.wait_ge(mf.ctrl, i + 1)
                pairs = act.value_load(ctrl[0:1, BLOCKS:BLOCKS + 1], min_val=1, max_val=PAIRS)
                for it in peeled(act, pairs):
                    for s in range(2):
                        after(act, m.g1, it * 2 + (s + 1))
                        act.activation(ex_g[:, s, :], ps[:, 0, 0:F], ACT.Silu).then_inc(m.sg, 1)
                        after(act, m.ht, it * 2 + (s + 1))
                        act.activation(ex_hT[:, s], ps[:, 4, 0:F].rearrange("p (f n) -> p f n", f=FT), ACT.Copy).then_inc(m.hc, 1)
                        after(act, m.y, it * 2 + (s + 1))
                        after(act, m.yo[s], it * 16)
                        act.activation(yb[:, s, :], ps[:, 5:7, :].rearrange("p b n -> p (b n)"), ACT.Copy).then_inc(m.yc, 1)
                        after(act, m.yc, it * 2 + (s + 1))
                        act.dma_start(y_rows[ds(it * (2 * P) + s * P, P), :], yb[:, s, :]).then_inc(m.yo[s], 16)
                for s in range(2):
                    act.wait_ge(m.yo[s], pairs * 16)
                act.wait_ge(m.xc, pairs * 2 + 1)
                act.sem_inc(mf.tail, 1)
                act.wait_ge(mf.gu, i * NT * TOPK + NT * TOPK)
                residual(f"moe{i}", lambda j: macc[:, j, :], mjunk, lambda j: None)

            moe(0, "ret")

            act.wait_ge(s_h, h_base["moe0"] + 2 * NT)
            rms(s_nrms, NT, lambda j: h[:, j, :], cjunk, lambda j: None)
            to_uT(n_mix[1], NT, uT)
            act.wait_ge(s_ccolp, 1)
            act.activation(chp, ps[:, 4, 0:KT * 36].rearrange("p (c k) -> p c k", c=KT), ACT.Copy).then_inc(s_ccol, 1)
            act.wait_ge(s_ccol, 1)
            for cc in range(KT):
                act.wait_ge(s_cag, cc + 1)
                if cc >= 2:
                    act.wait_ge(s_zin, cc - 1)
                act.activation(sgate[:, cc % 2, :], ps[:, 2 * (cc % 2) + 1, :], ACT.Sigmoid, bias=chp[:, cc, 35:36]).then_inc(s_csg, 1)
            act.wait_ge(s_lmu, 1)
            act.activation(mu, ps[:, 4, :], ACT.Copy, scale=1.0 / D).then_inc(s_lmuc, 1)
            for cc in range(KT):
                act.wait_ge(s_lcen, cc + 1)
                if cc >= 2:
                    act.wait_ge(s_lvar, cc - 1)
                act.activation(lsq[:, cc % 2, :], cacc[:, cc, :], ACT.Square).then_inc(s_lsq, 1)
            act.wait_ge(s_lvar, KT)
            act.activation(lrs, ps[:, 5, :], ACT.Sqrt, bias=eps_ln, scale=1.0 / D).then_inc(s_lsd, 1)
            for cc in range(KT):
                act.wait_ge(s_lnx, cc + 1)
                act.activation(zin[:, cc, 0:SEQ], cacc[:, cc, :], ACT.Silu, bias=chp[:, cc, 33:34], scale=chp[:, cc, 32:33])\
                    .then_inc(s_lnu, 1)
            residual("conv", lambda j: ybuf[:, j, :], sgate.rearrange("p s n -> p (s n)"),
                     lambda j: act.wait_ge(s_y, NT + j + 1))
            moe(1, "conv")

        @block.tensor
        def _(pe):
            def turn(ns, tiles, src, first):
                for j in range(tiles):
                    pe.wait_ge(s_nu, ns.tile + j + 1)
                    if j >= 2:
                        pe.wait_ge(s_ncp, ns.tile + j - 1)
                    for t in range(KT):
                        last = pe.transpose(ps[:, 2 * (j % 2) + t // 4, (t % 4) * P:(t % 4 + 1) * P],
                                            src(j).rearrange("n (p t) -> n t p", t=KT)[:, t, :], ident)
                    last.then_inc(s_ntp, 1)

            pe.wait_ge(s_cact, 1)
            for i in range(2):
                for n in peeled(pe, MODW // W // 2):
                    for s in range(2):
                        after(pe, s_mw[s], n * 16 + (6 * i + 1) * 16)
                        after(pe, s_mrow[s], n + 6 * i)
                        for t in range(KT):
                            last = pe.matmul(ps[0:2, s, :], c_act[:, t, :], panel[s][:, t, :], start=(t == 0), stop=(t == KT - 1))
                        last.then_inc(s_mps[s], 1)
            pe.wait_ge(s_const, 16)
            turn(n_ctx, 2, lambda j: ubuf[:, j % 2, :], True)
            pe.wait_ge(s_ncp, n_ctx.tile + 2)
            turn(n_mix[0], NT, lambda j: ubuf[:, j % 2, :], True)
            pe.wait_ge(s_ncp, n_mix[0].tile + NT)

            for hd in peeled(pe, HEADS):
                after(pe, s_wqk, hd * 32 + 32)
                after(pe, s_sc, hd * KEYT)
                for e in range(2):
                    for t in range(KT):
                        last = pe.matmul(ps[:, e, :], wqk[:, t, 0:DK].rearrange("p (m e) -> p e m", e=2)[:, e, :], uT[:, t, :],
                                         start=(t == 0), stop=(t == KT - 1))
                last.then_inc(s_q, 1)
                after(pe, s_ord, hd)
                for e in range(2):
                    for t in range(KT):
                        last = pe.matmul(ps[:, 2 + e, :], wqk[:, t, DK:2 * DK].rearrange("p (m e) -> p e m", e=2)[:, e, :], uT[:, t, :],
                                         start=(t == 0), stop=(t == KT - 1))
                last.then_inc(s_k, 1)
                after(pe, s_yT, hd * 4)
                for e in range(2):
                    for t in range(KT):
                        last = pe.matmul(ps[:, 4, e * CTX:(e + 1) * CTX], wqk[:, t, DK:2 * DK].rearrange("p (m e) -> p e m", e=2)[:, e, :],
                                         uTc[:, t, :], start=(t == 0), stop=(t == KT - 1))
                last.then_inc(s_kc, 1)
                after(pe, s_wv, hd * 16 + 16)
                for m in range(KEYT):
                    if m >= 3:
                        after(pe, s_vc, hd * KEYT + (m - 2))
                    src = uT[:, :, m * P:(m + 1) * P] if m < NT else uTc[:, :, (m - NT) * P:(m - NT + 1) * P]
                    for t in range(KT):
                        last = pe.matmul(ps[:, 5 + m % 3, :], src[:, t, :], wv[:, t, :], start=(t == 0), stop=(t == KT - 1))
                    last.then_inc(s_v, 1)
                after(pe, s_wg, hd * 16 + 16)
                for m in range(4):
                    after(pe, s_vc, hd * KEYT + min(m + 4, KEYT))
                    if m == 3:
                        after(pe, s_gc, hd * 4 + 1)
                    for t in range(KT):
                        last = pe.matmul(ps[:, 5 + m % 3, :], wg[:, t, m * P:(m + 1) * P], uT[:, t, :],
                                         start=(t == 0), stop=(t == KT - 1))
                    last.then_inc(s_g, 1)
                for m in range(KEYT):
                    after(pe, s_qkr, hd * 6 + 6)
                    if m >= 4:
                        after(pe, s_sc, hd * KEYT + (m - 3))
                    for e in range(2):
                        last = pe.matmul(ps[:, m % 4, :], kT[:, e, m * P:(m + 1) * P], qT[:, e, :], start=(e == 0), stop=(e == 1))
                    last.then_inc(s_s, 1)
                after(pe, s_vc, hd * KEYT + KEYT)
                after(pe, s_gc, hd * 4 + 4)
                for cc in range(4):
                    for m in range(KEYT):
                        after(pe, s_sc, hd * KEYT + (m + 1))
                        last = pe.matmul(ps[:, 4 + cc, :], V[:, m, cc * P:(cc + 1) * P], ST[:, m, :], start=(m == 0), stop=(m == KEYT - 1))
                    last.then_inc(s_o, 1)
                for cc in range(4):
                    after(pe, s_osq, hd * 4 + (cc + 1))
                    last = pe.matmul(ps[:, 3, :], ones, osq[:, cc, :], start=(cc == 0), stop=(cc == 3))
                last.then_inc(s_oss, 1)

            pe.wait_ge(s_yT, HEADS * 4)
            pe.wait_ge(s_ord, HEADS)
            for j in range(NT):
                for half in range(2):
                    for cc in range(4 * HEADS):
                        pe.wait_ge(s_wo[cc // 4], 16)
                        last = pe.matmul(ps[:, 2 * j + half, :], yT[:, cc, j * P:(j + 1) * P], wo[cc // 4][:, cc % 4, half * W:(half + 1) * W],
                                         start=(cc == 0), stop=(cc == 4 * HEADS - 1))
                last.then_inc(s_y, 1)

            def moe(i, mixer):
                m = mo[i]
                pe.wait_ge(s_h, h_base[mixer] + 2 * NT)
                turn(n_moe[i], NT, lambda j: mubuf[:, j % 2, :], False)
                pe.wait_ge(s_ncp, n_moe[i].tile + NT)
                pe.wait_ge(mf.wr, i * 16 + 16)
                for j in range(NT):
                    for t in range(KT):
                        last = pe.matmul(ps[:, 4, j * NE:(j + 1) * NE], uT[:, t, j * P:(j + 1) * P], wr[:, t, :],
                                         start=(t == 0), stop=(t == KT - 1))
                last.then_inc(mf.logit, 1)
                w1, w3, w2 = expert(1)
                pe.wait_ge(mf.sw, i * 48 + 48)
                for wi, w in enumerate((w1, w3)):
                    for f in range(FT):
                        for t in range(KT):
                            last = pe.matmul(ps[:, 2 * wi + f, :], w[:, t, :].rearrange("p (m f) -> p f m", f=FT)[:, f, :], uT[:, t, :],
                                             start=(t == 0), stop=(t == KT - 1))
                        last.then_inc(mf.sup, 1)
                pe.wait_ge(mf.sel, i * NT + NT)
                for j in range(NT):
                    last = pe.matmul(ps[0:NE, 4, 256:257], sel[:, j, :], ones[:, 0:1], start=(j == 0), stop=(j == NT - 1))
                last.then_inc(mf.cnt, 1)
                pe.wait_ge(mf.nblk, i * 2 + 2)
                for j in range(NT):
                    pe.matmul(ps[:, 5, j * NE:(j + 1) * NE], nblk_b[0:NE, :], cst[0:NE, C_TRI:C_TRI + NE], start=True, stop=False)
                    for jj in range(j):
                        pe.matmul(ps[:, 5, j * NE:(j + 1) * NE], ones, sel[:, jj, :], start=False, stop=False)
                    last = pe.matmul(ps[:, 5, j * NE:(j + 1) * NE], cst[:, C_TRI:C_TRI + P], sel[:, j, :], start=False, stop=True)
                last.then_inc(mf.pos, 1)
                pe.matmul(ps[0:NE, 6, 0:1], cst[0:NE, C_TRII:C_TRII + NE], cnt[0:NE, 4:5], start=True, stop=True).then_inc(mf.started, 1)
                pe.matmul(ps[0:1, 6, 256:257], ones[0:NE, 0:1], cnt[0:NE, 4:5], start=True, stop=True).then_inc(mf.started, 1)
                pe.wait_ge(mf.started, i * 3 + 3)
                pe.matmul(ps[0:1, 7, 0:BLOCKS], ones[0:NE, 0:1], started[0:NE, :], start=True, stop=True).then_inc(mf.blk, 1)
                pe.wait_ge(mf.sh, i * FT + FT)
                pe.wait_ge(mf.ctrl, i + 1)
                pe.wait_ge(mf.dest, i * NT + 1)
                for j in range(NT):
                    if j >= 2:
                        pe.wait_ge(mf.sacc, i * NT + j - 1)
                    for half in range(2):
                        for f in range(FT):
                            last = pe.matmul(ps[:, 4 + 2 * (j % 2) + half, :], hsT[:, f, j * P:(j + 1) * P], w2[:, f, half * W:(half + 1) * W],
                                             start=(f == 0), stop=(f == FT - 1))
                        last.then_inc(mf.sy, 1)
                pe.wait_ge(mf.sacc, i * NT + NT)
                pe.wait_ge(mf.list, i * 16 + 16)
                pe.transpose(ps[:, 7, 0:BLOCKS], slots, ident).then_inc(mf.listT, 1)
                pe.wait_ge(mf.ctrl, i + 1)
                pairs = pe.value_load(ctrl[0:1, BLOCKS:BLOCKS + 1], min_val=1, max_val=PAIRS)

                def turn_x(s, n, part):
                    if part == 0:
                        after(pe, m.xg[s], n)
                    for t in range(4 * part, 4 * part + 4):
                        last = pe.transpose(ps[:, 2 + t // 4, (t % 4) * P:(t % 4 + 1) * P],
                                            xg[:, s, :].rearrange("n (p t) -> n t p", t=KT)[:, t, :], ident)
                    if part == 1:
                        last.then_inc(m.xt, 1)

                turn_x(0, 16, 0)
                turn_x(0, 16, 1)
                for it in peeled(pe, pairs):
                    for s in range(2):
                        w1, w3, w2 = expert(s)
                        after(pe, m.xc, it * 2 + (s + 1))
                        after(pe, m.w1[s], it * 16 + 16)
                        for t in range(KT):
                            last = pe.matmul(ps[:, 0, 0:F], xT[:, s, t, :], w1[:, t, :], start=(t == 0), stop=(t == KT - 1))
                        last.then_inc(m.g1, 1)
                        after(pe, m.w3[s], it * 16 + 16)
                        for t in range(KT):
                            last = pe.matmul(ps[:, 1, 0:F], xT[:, s, t, :], w3[:, t, :], start=(t == 0), stop=(t == KT - 1))
                        last.then_inc(m.up, 1)
                        nxt = it * 16 + (16 if s == 0 else 32)
                        turn_x(1 - s, nxt, 0)
                        after(pe, m.hm, it * 2 + (s + 1))
                        for f in range(FT):
                            last = pe.transpose(ps[:, 4, f * P:(f + 1) * P], ex_h[:, s, :].rearrange("n (m f) -> n f m", f=FT)[:, f, :], ident)
                        last.then_inc(m.ht, 1)
                        turn_x(1 - s, nxt, 1)
                        after(pe, m.hc, it * 2 + (s + 1))
                        after(pe, m.w2[s], it * 16 + 16)
                        after(pe, m.yc, it * 2 + s)
                        for half in range(2):
                            for f in range(FT):
                                last = pe.matmul(ps[:, 5 + half, :], ex_hT[:, s, f, :], w2[:, f, half * W:(half + 1) * W],
                                                 start=(f == 0), stop=(f == FT - 1))
                        last.then_inc(m.y, 1)

            moe(0, "ret")

            turn(n_mix[1], NT, lambda j: cubuf[:, j % 2, :], False)
            pe.wait_ge(s_ncp, n_mix[1].tile + NT)
            pe.wait_ge(s_crow, 16 * 6)
            for cc in range(KT):
                last = pe.transpose(ps[:, 4, cc * 36:(cc + 1) * 36], chrow[0:36, cc * P:(cc + 1) * P], ident[0:36, 0:36])
            last.then_inc(s_ccolp, 1)
            for cc in range(KT):
                if cc >= 2:
                    pe.wait_ge(s_zin, cc - 1)
                for gate in range(2):
                    s = 2 * gate + cc // 4
                    pe.wait_ge(s_cw1[s], 16)
                    for t in range(KT):
                        last = pe.matmul(ps[:, 2 * (cc % 2) + gate, :], panel[s][:, t, (cc % 4) * P:(cc % 4 + 1) * P], uT[:, t, :],
                                         start=(t == 0), stop=(t == KT - 1))
                last.then_inc(s_cag, 1)
            pe.wait_ge(s_ccol, 1)
            for cc in range(KT):
                pe.wait_ge(s_tap, 2 * (cc // 2) + 2)
                last = pe.matmul(ps[:, 4, :], ones, cacc[:, cc, :], start=(cc == 0), stop=(cc == KT - 1))
            last.then_inc(s_lmu, 1)
            for cc in range(KT):
                pe.wait_ge(s_lsq, cc + 1)
                pe.matmul(ps[:, 5, :], ones, lsq[:, cc % 2, :], start=(cc == 0), stop=(cc == KT - 1)).then_inc(s_lvar, 1)
            pe.wait_ge(s_lnu, KT)
            for s in range(2):
                pe.wait_ge(s_cw2[s], 16)
            for j in range(NT):
                if j >= 2:
                    pe.wait_ge(s_y, NT + j - 1)
                for half in range(2):
                    for cc in range(KT):
                        last = pe.matmul(ps[:, 2 * (j % 2) + half, :], zin[:, cc, j * P:(j + 1) * P], panel[2 * half][:, cc, :],
                                         start=(cc == 0), stop=(cc == KT - 1))
                last.then_inc(s_cy, 1)
            moe(1, "conv")

        @block.vector
        def _(dve):
            st = Steps(dve, s_dve)
            MUL, ADD, SUB, MAX, MIN = ALU.mult, ALU.add, ALU.subtract, ALU.max, ALU.min

            def fold(i):
                dve.wait_ge(s_modb[i], 32)
                for r, w in ((1, 0), (4, 2)):
                    dve.scalar_tensor_tensor(modb[:, r, :], modb[:, r, :], 1.0, nrm[:, w, :], ADD, MUL).then_inc(s_folded[i], 1)
                for r, w in ((2, 1), (5, 3)):
                    dve.tensor_tensor(modb[:, r, :], modb[:, r, :], nrm[:, w, :], MUL).then_inc(s_folded[i], 1)

            def norm_modulate(ns, tiles, src, scale, shift, dst, free):
                dve.wait_ge(s_nrms, ns.stage + 1)
                st.then(dve.reciprocal(rs[:, 0:tiles], sd[:, 0:tiles]))
                for j in range(tiles):
                    if j >= 2:
                        free(j)
                    st.then(dve.scalar_tensor_tensor(dst(j), src(j), rs[:, j:j + 1], scale, MUL, MUL))
                    dve.tensor_tensor(dst(j), dst(j), shift, ADD).then_inc(s_nu, 1)

            def residual(key, src, gate, tmp):
                dve.wait_ge(s_yrms, h_base[key] // (2 * NT) + 1)
                st.then(dve.reciprocal(rs[:, 0:NT], sd[:, 0:NT]))
                for j in range(NT):
                    if j >= 1:
                        dve.wait_ge(s_h, h_base[key] + 2 * j)
                    dve.scalar_tensor_tensor(tmp, src(j), rs[:, j:j + 1], gate, MUL, MUL).then_inc(s_h, 1)
                    dve.wait_ge(s_h, h_base[key] + 2 * j + 1)
                    dve.tensor_tensor(h[:, j, :], h[:, j, :], tmp, ADD).then_inc(s_h, 1)

            for i in range(2):
                for n in peeled(dve, MODW // W // 2):
                    for s in range(2):
                        after(dve, s_mps[s], n + (6 * i + 1))
                        after(dve, s_mbias[s], n * 32 + (6 * i + 1) * 32)
                        after(dve, s_mout[s], n * 16 + 6 * i * 16)
                        dve.tensor_tensor(mrow[:, s, :], ps[0:2, s, :], brow[:, s, :], ADD).then_inc(s_mrow[s], 1)
            dve.wait_ge(s_decay, 16)
            st.then(dve.tensor_scalar(dec_t[1], dec, -1.0, None, MUL))
            dve.tensor_tensor(dec_t[0], dec, dec_t[1], MAX).then_inc(s_log, 1)
            dve.wait_ge(s_log, 2)
            z, d2, r2, sv, s2, q = dec_t[1], dec_t[2], dec_t[3], dec_t[4], dec_t[5], dec_t[0]
            st.then(dve.tensor_scalar(d2, z, 2.0, None, ADD))
            st.then(dve.reciprocal(r2, d2))
            st.then(dve.tensor_tensor(sv, z, r2, MUL))
            st.then(dve.tensor_tensor(s2, sv, sv, MUL))
            st.then(dve.tensor_scalar(q, s2, 1.0 / 15, None, MUL))
            for k in (13, 11, 9, 7, 5, 3):
                st.then(dve.scalar_tensor_tensor(q, q, 1.0 / k, s2, ADD, MUL))
            st.then(dve.scalar_tensor_tensor(q, q, 1.0, sv, ADD, MUL))
            st.then(dve.tensor_scalar(d2, dec, 0.0, None, MIN))
            st.then(dve.scalar_tensor_tensor(r2, q, -2.0, d2, MUL, ADD))
            st.then(dve.tensor_copy(lgf, r2[:, 0:4]))
            st.then(dve.tensor_scalar(nlgb, r2[:, 4:8], -1.0, None, MUL))

            fold(0)
            dve.wait_ge(s_cmod, 16)
            dve.scalar_tensor_tensor(cmod[:, 1, :], cmod[:, 1, :], 1.0, nrm[:, 0, :], ADD, MUL).then_inc(s_folded[0], 1)
            dve.wait_ge(s_folded[0], 5)
            dve.wait_ge(s_ctx, 16)
            norm_modulate(n_ctx, 2, lambda j: ctx_x[:, j, :], cmod[:, 1, :], cmod[:, 0, :], lambda j: ubuf[:, j % 2, :], None)
            dve.wait_ge(s_ntp, n_ctx.tile + 2)
            dve.wait_ge(s_x, 16)
            norm_modulate(n_mix[0], NT, lambda j: h[:, j, :], modb[:, 1, :], modb[:, 0, :], lambda j: ubuf[:, j % 2, :],
                          lambda j: dve.wait_ge(s_ntp, n_mix[0].tile + j - 1))
            dve.wait_ge(s_nu, n_mix[0].tile + NT)
            dve.wait_ge(s_ntp, n_mix[0].tile + NT)
            dve.wait_ge(s_const, 16)

            dve.memset(zrow, 0.0).then_inc(s_zrow, 1)
            pos = cst[:, C_POS:C_POS + BAND]
            per_head = 3 + 2 + 12 + 1 + 4
            base = st.n
            for hd in peeled(dve, HEADS):
                st.n = hd * per_head + base
                after(dve, s_sc, hd * KEYT)
                st.then(dve.tensor_scalar(band, pos, 0.0, lgf[:, ds(hd, 1)], MAX, MUL))
                bt = rot.rearrange("p i n -> p (i n)")[:, 0:BAND]
                after(dve, s_o, hd * 4)
                st.then(dve.tensor_scalar(bt, pos, 0.0, nlgb[:, ds(hd, 1)], MIN, MUL))
                dve.tensor_tensor(band, band, bt, ADD).then_inc(s_band, 1)
                after(dve, s_bexp, hd + 1)
                st.then(dve.tensor_tensor(band[:, 640:640 + P], band[:, 640:640 + P], ident, ADD))
                for m in range(2):
                    last = dve.tensor_tensor(dctx[:, m, :], band[:, 640 - P * (m - 2):640 - P * (m - 2) + SEQ],
                                             band[:, 640 - P * (m + 4):640 - P * (m + 4) + SEQ], ADD)
                    st.done(last)
                after(dve, s_oss, hd)
                k0 = 0
                for signal, a, b, cs, dst in (
                    (s_q, ps[:, 0, :], ps[:, 1, :], slice(0, SEQ), qT),
                    (s_k, ps[:, 2, :], ps[:, 3, :], slice(0, SEQ), kT[:, :, 0:SEQ]),
                    (s_kc, ps[:, 4, 0:CTX], ps[:, 4, CTX:2 * CTX], slice(SEQ, SEQ + CTX), kT[:, :, SEQ:SEQ + CTX]),
                ):
                    n = cs.stop - cs.start
                    after(dve, signal, hd + 1)
                    if k0:
                        after(dve, s_qkr, hd * 6 + k0)
                    c_, s_ = cos[:, cs], sin[:, cs]
                    st.done(dve.tensor_tensor(rot[:, 0, 0:n], a, c_, MUL))
                    st.done(dve.tensor_tensor(rot[:, 1, 0:n], b, s_, MUL))
                    st.done(dve.tensor_tensor(rot[:, 2, 0:n], a, s_, MUL))
                    st.then(dve.tensor_tensor(rot[:, 3, 0:n], b, c_, MUL))
                    dve.tensor_tensor(dst[:, 0, :], rot[:, 0, 0:n], rot[:, 1, 0:n], SUB).then_inc(s_qkr, 1)
                    dve.tensor_tensor(dst[:, 1, :], rot[:, 2, 0:n], rot[:, 3, 0:n], ADD).then_inc(s_qkr, 1)
                    k0 += 2
                after(dve, s_qkr, hd * 6 + 6)
                for m in range(KEYT):
                    after(dve, s_s, hd * KEYT + (m + 1))
                    dk = band[:, 640 - P * m:640 - P * m + SEQ] if m < NT else dctx[:, m - NT, :]
                    dve.scalar_tensor_tensor(ST[:, m, :], ps[:, m % 4, :], DK ** -0.5, dk, MUL, MUL).then_inc(s_sc, 1)
                after(dve, s_ord, hd + 1)
                after(dve, s_gc, hd * 4 + 4)
                st.then(dve.reciprocal(orstd, orstd))
                for cc in range(4):
                    if cc:
                        after(dve, s_yT, hd * 4 + cc)
                    ins = dve.tensor_tensor(otmp, ps[:, 4 + cc, :], orstd, MUL)
                    st.then(ins)
                    dve.tensor_tensor(yT[:, ds(hd * 4 + cc, 1), :].rearrange("p o n -> p (o n)"), otmp, sgT[:, cc, :], MUL).then_inc(s_yT, 1)
            st.n = base + HEADS * per_head

            residual("ret", lambda j: ps[:, 2 * j:2 * j + 2, :].rearrange("p b n -> p (b n)"), modb[:, 2, :], junk)

            def moe(i, mixer):
                m = mo[i]
                dve.wait_ge(s_h, h_base[mixer] + 2 * NT)
                def free(j):
                    dve.wait_ge(s_ntp, n_moe[i].tile + j - 1)
                    dve.wait_ge(mf.urow[j % 2], i * (32) + 16)
                norm_modulate(n_moe[i], NT, lambda j: h[:, j, :], modb[:, 4, :], modb[:, 3, :], lambda j: mubuf[:, j % 2, :], free)
                st.done(dve.memset(gsx[:, :, NG:NG + 4], -MARK))
                st.done(dve.memset(grep[:, :, 4:8], -MARK))
                dve.wait_ge(mf.score, i + 1)
                dve.wait_ge(mf.bias, i * 16 + 16)
                st.then(dve.tensor_tensor(biased, score, bias.unsqueeze(1).to_broadcast([P, NT, NE]), ADD))
                for j in range(NT):
                    for g in range(NG):
                        st.done(dve.max(gtop[:, j, g, :], biased[:, j, g * PER:(g + 1) * PER]))
                after(dve, s_dve, st.n)
                st.then(dve.tensor_tensor(gsx[:, :, 0:NG], gtop[:, :, :, 0], gtop[:, :, :, 1], ADD))
                for j in range(NT):
                    st.done(dve.max(gmax[:, j, :], gsx[:, j, :]))
                after(dve, s_dve, st.n)
                st.then(dve.tensor_copy(grep[:, :, 0:4], gmax[:, :, 0:4]))
                for j in range(NT):
                    st.done(dve.match_replace(gout[:, j, :], grep[:, j, :], gsx[:, j, :], MARK))
                after(dve, s_dve, st.n)
                st.then(dve.tensor_scalar(gmask, gout[:, :, 0:NG], MARK, None, ALU.is_equal))
                st.then(dve.tensor_scalar(gneg, gmask, 1.0, -LOW, SUB, MUL))
                for j in range(NT):
                    st.done(dve.tensor_tensor(rep[:, j].rearrange("p (g k) -> p g k", g=NG), biased[:, j].rearrange("p (g k) -> p g k", g=NG),
                                              gmask[:, j].unsqueeze(2).to_broadcast([P, NG, PER]), MUL))
                after(dve, s_dve, st.n)
                for j in range(NT):
                    st.done(dve.tensor_tensor(biased[:, j].rearrange("p (g k) -> p g k", g=NG), rep[:, j].rearrange("p (g k) -> p g k", g=NG),
                                              gneg[:, j].unsqueeze(2).to_broadcast([P, NG, PER]), ADD))
                after(dve, s_dve, st.n)
                for j in range(NT):
                    st.done(dve.max(top8[:, j, :], biased[:, j, :]))
                after(dve, s_dve, st.n)
                for j in range(NT):
                    st.done(dve.match_replace(rep[:, j, :], top8[:, j, :], biased[:, j, :], MARK))
                after(dve, s_dve, st.n)
                for j in range(NT):
                    dve.tensor_scalar(sel[:, j, :], rep[:, j, :], MARK, None, ALU.is_equal).then_inc(mf.sel, 1)
                dve.wait_ge(mf.sel, i * NT + NT)
                dve.wait_ge(mf.cnt, i + 1)
                st.then(dve.tensor_copy(cnt[0:NE, 5:6], ps[0:NE, 4, 256:257]))
                st.then(dve.tensor_scalar(cnt[0:NE, 0:4], cst[0:NE, C_THR:C_THR + NT], cnt[0:NE, 5:6], None, ALU.is_lt))
                dve.tensor_reduce(cnt[0:NE, 4:5], cnt[0:NE, 0:4], AX.X, ADD).then_inc(mf.nblk, 1)
                dve.wait_ge(mf.nblk, i * 2 + 1)
                dve.tensor_scalar(nblk_b[0:NE, :], ones[0:NE, :], cnt[0:NE, 4:5], float(P), MUL, MUL).then_inc(mf.nblk, 1)
                dve.wait_ge(mf.started, i * 3 + 2)
                st.then(dve.tensor_copy(cnt[0:NE, 6:7], ps[0:NE, 6, 0:1]))
                dve.tensor_scalar(started[0:NE, :], cst[0:NE, C_IOTA:C_IOTA + BLOCKS], cnt[0:NE, 6:7], None, ALU.is_ge).then_inc(mf.started, 1)
                dve.wait_ge(mf.pos, i + 1)
                for j in range(NT):
                    st.done(dve.tensor_scalar(slotk[:, j, :], ps[:, 5, j * NE:(j + 1) * NE], -1.0, BIG, MUL, ADD))
                after(dve, s_dve, st.n)
                st.then(dve.tensor_tensor(slotk, slotk, sel, MUL))
                for j in range(NT):
                    st.done(dve.max(topslot[:, j, :], slotk[:, j, :]))
                after(dve, s_dve, st.n)
                for j in range(NT):
                    dve.tensor_scalar(dest[:, j, :], topslot[:, j, :], -1.0, BIG, MUL, ADD).then_inc(mf.dest, 1)
                dve.wait_ge(mf.blk, i + 1)
                st.done(dve.tensor_scalar(ctrl[0:1, 0:BLOCKS], ps[0:1, 7, 0:BLOCKS], float(NE - 1), None, MIN))
                after(dve, s_dve, st.n)
                dve.tensor_scalar(ctrl[0:1, BLOCKS:BLOCKS + 1], ps[0:1, 6, 256:257], 0.5, 0.25, MUL, ADD).then_inc(mf.ctrl, 1)
                for f in range(FT):
                    dve.wait_ge(mf.ssg, i * FT + f + 1)
                    dve.wait_ge(mf.sup, i * 2 * FT + FT + f + 1)
                    dve.tensor_tensor(hsT[:, f, :], ps[:, 2 + f, :], sgs[:, f, :], MUL).then_inc(mf.sh, 1)
                st.then(dve.tensor_tensor(wn, score, sel, MUL))
                st.then(dve.tensor_reduce(wsum[:, 0:NT], wn, AX.X, ADD))
                st.then(dve.reciprocal(wsum[:, 4:8], wsum[:, 0:NT]))
                for j in range(NT):
                    st.done(dve.tensor_scalar(wn[:, j, :], wn[:, j, :], wsum[:, 4 + j:5 + j], ROUTE_SCALE, MUL, MUL))
                after(dve, s_dve, st.n)
                for j in range(NT):
                    st.then(dve.tensor_tensor(eq, slotk[:, j].unsqueeze(1).to_broadcast([P, TOPK, NE]),
                                              topslot[:, j].unsqueeze(2).to_broadcast([P, TOPK, NE]), ALU.is_equal))
                    st.then(dve.tensor_tensor(eq, eq, wn[:, j].unsqueeze(1).to_broadcast([P, TOPK, NE]), MUL))
                    st.then(dve.tensor_reduce(wk[:, j, :], eq, AX.X, ADD))
                dve.wait_ge(mf.listT, i + 1)
                dve.tensor_copy(tok_idx, ps[:, 7, 0:BLOCKS]).then_inc(mf.tok, 1)

                dve.wait_ge(mf.ctrl, i + 1)
                pairs = dve.value_load(ctrl[0:1, BLOCKS:BLOCKS + 1], min_val=1, max_val=PAIRS)

                def copy_xT(s, n):
                    after(dve, m.xt, n)
                    dve.tensor_copy(xT[:, s], ps[:, 2:4, :].rearrange("p b (t n) -> p (b t) n", n=P)).then_inc(m.xc, 1)

                copy_xT(0, 1)
                for it in peeled(dve, pairs):
                    for s in range(2):
                        after(dve, m.sg, it * 2 + (s + 1))
                        after(dve, m.up, it * 2 + (s + 1))
                        dve.tensor_tensor(ex_h[:, s, :], ps[:, 1, 0:F], ex_g[:, s, :], MUL).then_inc(m.hm, 1)
                        copy_xT(1 - s, it * 2 + (s + 2))
                for n in range(NT * TOPK):
                    j, k = divmod(n, TOPK)
                    after(dve, mf.gb[n % 4], i * (16 * NT * TOPK // 4) + 16 * (n // 4 + 1))
                    if n == 0:
                        dve.wait_ge(mf.sacc, i * NT + NT)
                    if k:
                        after(dve, mf.gu, i * NT * TOPK + n)
                    dve.scalar_tensor_tensor(macc[:, j, :], gbuf[:, n % 4, :], wk[:, j, k:k + 1], macc[:, j, :], MUL, ADD).then_inc(mf.gu, 1)
                residual(f"moe{i}", lambda j: macc[:, j, :], modb[:, 5, :], mubuf[:, 0, :])

            moe(0, "ret")

            fold(1)
            dve.wait_ge(s_folded[1], 4)
            st.then(dve.memset(col[:, 140:141], 0.0))
            dve.tensor_copy(col[:, 141:142], col[:, 140:141]).then_inc(s_folded[1], 1)
            norm_modulate(n_mix[1], NT, lambda j: h[:, j, :], modb[:, 1, :], modb[:, 0, :], lambda j: cubuf[:, j % 2, :],
                          lambda j: dve.wait_ge(s_ntp, n_mix[1].tile + j - 1))
            dve.wait_ge(s_ntp, n_mix[1].tile + NT)
            st.done(dve.memset(zin[:, :, 0:HALO], 0.0))
            st.done(dve.memset(zin[:, :, HALO + SEQ:2 * HALO + SEQ], 0.0))
            dve.wait_ge(s_ccol, 1)
            for cc in range(KT):
                dve.wait_ge(s_csg, cc + 1)
                dve.scalar_tensor_tensor(zin[:, cc, HALO:HALO + SEQ], ps[:, 2 * (cc % 2), :], chp[:, cc, 34:35], sgate[:, cc % 2, :], ADD, MUL)\
                    .then_inc(s_zin, 1)
            dve.wait_ge(s_zin, KT)
            after(dve, s_dve, st.n)
            base = st.n
            per = 2 * TAPS - 2
            for pr in peeled(dve, KT // 2):
                st.n = pr * per + base
                for k in range(TAPS):
                    for u in range(2):
                        z_ = zin[:, ds(pr * 2 + u, 1), k:k + SEQ].rearrange("p o n -> p (o n)")
                        a_ = cacc[:, ds(pr * 2 + u, 1), :].rearrange("p o n -> p (o n)")
                        w_ = chp[:, ds(pr * 2 + u, 1), k:k + 1].rearrange("p o n -> p (o n)")
                        if k == 0:
                            b_ = chp[:, ds(pr * 2 + u, 1), TAPS:TAPS + 1].rearrange("p o n -> p (o n)")
                            ins = dve.tensor_scalar(a_, z_, w_, b_, MUL, ADD)
                        else:
                            after(dve, s_dve, st.n - (0 if k == TAPS - 1 and u else 1))
                            ins = dve.scalar_tensor_tensor(a_, z_, w_, a_, MUL, ADD)
                        if k < TAPS - 1:
                            st.done(ins)
                        else:
                            ins.then_inc(s_tap, 1)
            st.n = base + KT // 2 * per
            dve.wait_ge(s_lmuc, 1)
            for cc in range(KT):
                dve.tensor_tensor(cacc[:, cc, :], cacc[:, cc, :], mu, SUB).then_inc(s_lcen, 1)
            dve.wait_ge(s_lsd, 1)
            st.then(dve.reciprocal(lrs, lrs))
            for cc in range(KT):
                dve.wait_ge(s_lcen, KT)
                dve.wait_ge(s_lsq, cc + 1)
                dve.tensor_tensor(cacc[:, cc, :], cacc[:, cc, :], lrs, MUL).then_inc(s_lnx, 1)
            dve.wait_ge(s_cb2, 16)
            for j in range(NT):
                dve.wait_ge(s_cy, j + 1)
                dve.tensor_tensor(ybuf[:, j, :], ps[:, 2 * (j % 2):2 * (j % 2) + 2, :].rearrange("p b n -> p (b n)"), b2row, ADD)\
                    .then_inc(s_y, 1)
            residual("conv", lambda j: ybuf[:, j, :], modb[:, 2, :], chrow)
            moe(1, "conv")


_INS = ['x', 'c', 'ctx', 'c_ctx', 'mod_w', 'mod_b', 'norms', 'ret_w_in', 'ret_w_out', 'ret_decay',
        'conv_w1', 'conv_b1', 'conv_dw', 'conv_b_dw', 'conv_ln_g', 'conv_ln_b', 'conv_w2', 'conv_b2',
        'moe_router', 'moe_bias', 'moe_w1', 'moe_w3', 'moe_w2', 'shared_w1', 'shared_w3', 'shared_w2']


def kernel(**inputs):
    import concourse.bacc as bacc
    from concourse.bass_utils import run_bass_kernel_spmd

    nc = bacc.Bacc("TRN2", target_bir_lowering=False, num_devices=1)
    arrays = {f"in_{n}": np.ascontiguousarray(inputs[n]) for n in _INS}
    arrays["in_consts"] = shape_constants()
    args = [nc.dram_tensor(n, a.shape, F32, kind="ExternalInput").ap() for n, a in arrays.items()]
    out = nc.dram_tensor("out", (1, SEQ, D), F32, kind="ExternalOutput").ap()
    build(nc, *args, out)
    return run_bass_kernel_spmd(nc, [arrays], core_ids=[0]).results[0]["out"]
```

```python
from contextlib import ExitStack

import numpy as np

import concourse.bass as bass
from concourse import mybir

ALU = mybir.AluOpType
ACT = mybir.ActivationFunctionType
AX = mybir.AxisListType
F32 = mybir.dt.float32
I32 = mybir.dt.int32
ds = bass.ds

P = 128
D = 1024
KT = D // P
SEQ = 512
CTX = 256
NT = SEQ // P
HEADS = 4
DK = D // HEADS
DV = 2 * DK
KEYT = (SEQ + CTX) // P
W = 512
MODW = 6 * D
TAPS = 31
HALO = TAPS // 2
NE = 64
TOPK = 8
NG = 8
PER = NE // NG
F = 256
FT = F // P
ROUTE_SCALE = 2.5
BLOCKS = 98
PAIRS = 48
BIG = 16384.0
MARK = 3.0e38
LOW = -1.0e30
BAND = 640 + SEQ + CTX

C_ID = 0
C_TRI = C_ID + P
C_TRII = C_TRI + P
C_ONE = C_TRII + P
C_IOTA = C_ONE + P
C_POS = C_IOTA + P
C_COS = C_POS + BAND
C_SIN = C_COS + SEQ + CTX
C_TOK = C_SIN + SEQ + CTX
C_THR = C_TOK + NT
C_EPS = C_THR + NT
C_DUMP = C_EPS + 2
C_ONEPLUS = C_DUMP + 1
C_ALL = C_ONEPLUS + 4

MOD_PARTS = [(0, 0, 3, 1, (None, 0, 1)), (0, 3, 3, 1, (None, 2, 3)), (1, 0, 2, 1, (None, 0)), (1, 2, 4, 2, (1, None, 2, 3))]
DB = D // P


def shape_constants():
    c = np.zeros((P, C_ALL), np.float32)
    r = np.arange(P)
    c[:, C_ID:C_ID + P] = np.eye(P)
    c[:, C_TRI:C_TRI + P] = r[:, None] < r[None, :]
    c[:, C_TRII:C_TRII + P] = r[:, None] <= r[None, :]
    c[:, C_ONE:C_ONE + P] = 1.0
    c[:, C_IOTA:C_IOTA + P] = r[None, :]
    c[:, C_POS:C_POS + BAND] = np.arange(BAND)[None, :] - 640 - r[:, None]
    at = np.arange(SEQ)
    lat = np.stack([np.full(SEQ, CTX), at // 64, at % 64], -1)
    ctx = np.stack([np.arange(CTX), np.zeros(CTX), np.zeros(CTX)], -1)
    pos = np.concatenate([lat, ctx]).astype(np.float32)
    ang = []
    for a, d in enumerate((64, 96, 96)):
        inv = (10000.0 ** (-np.arange(0, d, 2, dtype=np.float32) / np.float32(d))).astype(np.float32)
        ang.append(pos[:, a:a + 1] * inv[None, :])
    ang = np.concatenate(ang, -1).astype(np.float64).T
    c[:, C_COS:C_COS + SEQ + CTX] = np.cos(ang)
    c[:, C_SIN:C_SIN + SEQ + CTX] = np.sin(ang)
    c[:, C_TOK:C_TOK + NT] = 1 + r[:, None] + P * np.arange(NT)[None, :]
    c[:, C_THR:C_THR + NT] = P * np.arange(NT)[None, :]
    c[:, C_EPS] = 1e-6
    c[:, C_EPS + 1] = 1e-5
    c[:, C_DUMP] = SEQ + 1 + r
    for part, (_, _, _, scale, _) in enumerate(MOD_PARTS):
        c[:, C_ONEPLUS + part] = r // DB == scale
    return c


class Steps:

    def __init__(self, eng, sem):
        self.eng, self.sem, self.n = eng, sem, 0

    def done(self, ins):
        ins.then_inc(self.sem, 1)
        self.n = self.n + 1
        return self.n

    def then(self, ins):
        self.eng.wait_ge(self.sem, self.done(ins))


def peeled(eng, n):
    yield 0
    with eng.Fori(1, n) as i:
        yield i


def after(eng, sem, n):
    if not isinstance(n, int) or n > 0:
        eng.wait_ge(sem, n)


def build(nc, x, c, ctx, c_ctx, mod_w, mod_b, norms, ret_w_in, ret_w_out, ret_decay,
          conv_w1, conv_b1, conv_dw, conv_b_dw, conv_ln_g, conv_ln_b, conv_w2, conv_b2,
          moe_router, moe_bias, moe_w1, moe_w3, moe_w2, shared_w1, shared_w3, shared_w2,
          consts, out):
    with ExitStack() as stack:
        def sem(name):
            return stack.enter_context(nc.semaphore(name))

        def sb(name, cols, dt=F32):
            return stack.enter_context(nc.sbuf_tensor(name, [P, cols], dt))

        mod_raw = nc.dram_tensor("mod_raw", [2, 2, MODW], F32, kind="Internal").ap()
        mod_rows = nc.dram_tensor("mod_rows", [2, 2, MODW], F32, kind="Internal").ap()
        u_rows = [nc.dram_tensor(f"u_rows{i}", [SEQ, D], F32, kind="Internal").ap() for i in range(2)]
        sum_rows = nc.dram_tensor("sum_rows", [SEQ + P, D], F32, kind="Internal").ap()

        cst = sb("cst", C_ALL)
        h = sb("h", NT * D)[:, :].rearrange("p (j d) -> p j d", j=NT)
        modb = sb("modb", MODW)[:, :].rearrange("p (r d) -> p r d", r=6)
        uT = sb("uT", KT * SEQ)[:, :].rearrange("p (t n) -> p t n", t=KT)
        ring_all = sb("ring", 4 * KT * W)
        ring = [ring_all[:, s * KT * W:(s + 1) * KT * W] for s in range(4)]
        col = sb("col", 160)
        arena_cols = 18700
        arena = sb("arena", arena_cols)
        ps = stack.enter_context(nc.psum_tensor("ps", [P, 8, W], F32))

        ident = cst[:, C_ID:C_ID + P]
        ones = cst[:, C_ONE:C_ONE + P]
        cos = cst[:, C_COS:C_COS + SEQ + CTX]
        sin = cst[:, C_SIN:C_SIN + SEQ + CTX]
        eps_norm = cst[:, C_EPS:C_EPS + 1]
        eps_ln = cst[:, C_EPS + 1:C_EPS + 2]

        ss = col[:, 0:8]
        sd = col[:, 8:16]
        rs = col[:, 16:24]
        dec = col[:, 24:32]
        dec_t = [col[:, 32 + 8 * i:40 + 8 * i] for i in range(6)]
        lgf = col[:, 80:84]
        nlgb = col[:, 84:88]
        y_ss = col[:, 128:132]
        y_sd = col[:, 132:136]
        y_rs = col[:, 136:140]
        c_raw = col[:, 96:112].rearrange("p (r t) -> p r t", r=2)
        c_act = col[:, 112:128].rearrange("p (t r) -> p t r", r=2)

        def view(off, n):
            assert off + n <= arena_cols
            return arena[:, off:off + n]

        yT = view(0, 8192).rearrange("p (c n) -> p c n", c=4 * HEADS)
        ctx_x = view(0, 2048).rearrange("p (j d) -> p j d", j=2)
        cmod = view(2048, 2048).rearrange("p (r d) -> p r d", r=2)
        uTc = view(8192, 2048).rearrange("p (t n) -> p t n", t=KT)
        qT = view(10240, 1024).rearrange("p (e n) -> p e n", e=2)
        kT = view(11264, 1536).rearrange("p (e n) -> p e n", e=2)
        osq = view(10240, 2048).rearrange("p (c n) -> p c n", c=4)
        sgT = view(12800, 2048).rearrange("p (c n) -> p c n", c=4)
        ST = view(14848, 3072).rearrange("p (m n) -> p m n", m=KEYT)
        rot = view(14848, 2048).rearrange("p (i n) -> p i n", i=4)
        orstd = view(17920, 512)
        ubuf = view(14848, 2048).rearrange("p (s d) -> p s d", s=2)
        junk = view(16896, 1024)
        band = modb[:, 0:2, :].rearrange("p r d -> p (r d)")[:, 0:BAND]
        otmp = modb[:, 0:2, :].rearrange("p r d -> p (r d)")[:, BAND:BAND + SEQ]
        V = ring[3][:, 0:KEYT * W].rearrange("p (m n) -> p m n", m=KEYT)
        dctx = ring[3][:, KEYT * W:KT * W].rearrange("p (m n) -> p m n", m=2)

        class ModBuffers:

            def __init__(self, at, blocks, conds, products):
                self.bias, self.norm = view(at, P)[0:blocks], view(at + P, P)[0:blocks]
                self.rows = view(at + 2 * P, conds * P).rearrange("p (r n) -> p r n", r=conds)[0:blocks]
                self.blocks, self.conds, self.products = blocks, conds, products[0:conds, 0:blocks * P]

        mod_part = [ModBuffers(12800, 24, 2, ring[3]), ModBuffers(13312, 24, 1, view(4096, 3072)),
                    ModBuffers(5184, 16, 1, view(0, 2048)),
                    ModBuffers(17952, 32, 1, uT.rearrange("p t n -> p (t n)"))]

        zin = view(0, KT * (SEQ + 2 * HALO)).rearrange("p (c n) -> p c n", c=KT)
        cacc = view(4352, 4096).rearrange("p (c n) -> p c n", c=KT)
        sgate = view(8448, 1024).rearrange("p (s n) -> p s n", s=2)
        chp = view(9472, 8 * 36).rearrange("p (c k) -> p c k", c=KT)
        chrow = view(9760, 1024)
        b2row = view(10784, 1024)
        mu = view(11808, 512)
        lrs = view(12320, 512)
        lsq = view(12832, 1024).rearrange("p (s n) -> p s n", s=2)
        ybuf = view(13856, 4096).rearrange("p (j d) -> p j d", j=NT)
        cubuf = view(0, 2048).rearrange("p (s d) -> p s d", s=2)
        cjunk = view(2048, 1024)
        cmubuf = view(4352, 2048).rearrange("p (s d) -> p s d", s=2)

        xg = view(0, 2048).rearrange("p (s d) -> p s d", s=2)
        xT = view(2048, 2048).rearrange("p (s t n) -> p s t n", s=2, t=KT)
        oh_r = view(0, 2048).rearrange("p (s k r) -> p s k r", s=2, k=TOPK)
        oh_b = view(2048, 4 * TOPK * BLOCKS).rearrange("p (s k w b) -> p s k w b", s=2, k=TOPK, w=2)
        yb = view(4096, 2048).rearrange("p (s d) -> p s d", s=2)
        macc = view(6144, 4096).rearrange("p (j d) -> p j d", j=NT)
        mubuf = view(10240, 2048).rearrange("p (s d) -> p s d", s=2)
        hsT = view(12288, 1024).rearrange("p (f n) -> p f n", f=FT)
        sgs = view(13312, 1024).rearrange("p (f n) -> p f n", f=FT)
        ex_g = view(10240, 512).rearrange("p (s n) -> p s n", s=2)
        ex_h = view(10752, 512).rearrange("p (s n) -> p s n", s=2)
        ex_hT = view(11264, 512).rearrange("p (s f n) -> p s f n", s=2, f=FT)
        idx_col = view(11776, 4).bitcast(I32)
        mjunk = view(13312, 1024)
        at = 14336

        def small(n):
            nonlocal at
            at += n
            return view(at - n, n)

        wr = small(KT * NE).rearrange("p (t e) -> p t e", t=KT)
        score = small(256).rearrange("p (j e) -> p j e", j=NT)
        bias = small(64)
        biased = small(256).rearrange("p (j e) -> p j e", j=NT)
        gtop = small(256).rearrange("p (j g k) -> p j g k", j=NT, g=NG)
        gsx = small(48).rearrange("p (j k) -> p j k", j=NT)
        gmax = small(32).rearrange("p (j k) -> p j k", j=NT)
        grep = small(32).rearrange("p (j k) -> p j k", j=NT)
        gout = small(48).rearrange("p (j k) -> p j k", j=NT)
        gmask = small(32).rearrange("p (j g) -> p j g", j=NT)
        gneg = small(32).rearrange("p (j g) -> p j g", j=NT)
        top8 = small(32).rearrange("p (j k) -> p j k", j=NT)
        rep = small(256).rearrange("p (j e) -> p j e", j=NT)
        sel = small(256).rearrange("p (j e) -> p j e", j=NT)
        wn = small(256).rearrange("p (j e) -> p j e", j=NT)
        wsum = small(8)
        slotk = small(256).rearrange("p (j e) -> p j e", j=NT)
        topslot = small(32).rearrange("p (j k) -> p j k", j=NT)
        slot_i = small(32).bitcast(I32)
        slot_ri = small(32).bitcast(I32)
        slot_bi = small(32).bitcast(I32)
        slot_r = small(32).rearrange("p (j k) -> p j k", j=NT)
        slot_b = small(32).rearrange("p (j k) -> p j k", j=NT)
        eq = small(512).rearrange("p (k e) -> p k e", k=TOPK)
        wk = small(32).rearrange("p (j k) -> p j k", j=NT)
        cnt = small(12)
        nblk_b = small(P)
        started = small(P)
        ctrl = small(BLOCKS + 2).bitcast(I32)
        is_pad = small(BLOCKS)
        tok_idx = small(BLOCKS).bitcast(I32)
        sum_idx = small(BLOCKS).bitcast(I32)
        wslot = small(BLOCKS)
        zero = small(P)

        moe_u = (mubuf, cmubuf)

        def expert(s):
            w = ring_all[:, s * 6144:(s + 1) * 6144]
            return (w[:, 0:2048].rearrange("p (t f) -> p t f", t=KT), w[:, 2048:4096].rearrange("p (t f) -> p t f", t=KT),
                    w[:, 4096:6144].rearrange("p (f d) -> p f d", f=FT))

        s_const, s_c, s_x, s_ctx, s_decay = (sem(n) for n in ("const_in", "c_in", "x_in", "ctx_in", "decay_in"))
        s_cact = sem("c_silu")
        s_mw = [sem(f"mod_panel_in{s}") for s in range(3)]
        s_mwh = [sem(f"mod_half_panel_in{s}") for s in range(2)]
        s_mbias = [sem(f"mod_bias_norms_in{s}") for s in range(2)]
        s_mps, s_mcp, s_mraw, s_mback, s_mrow, s_mout = (sem(n) for n in ("mod_product", "mod_copied", "mod_products_stored", "mod_blocks_in",
                                                                          "mod_rows", "mod_stored"))
        s_modm, s_modf, s_cmod = sem("mod_mixer_in"), sem("mod_ffn_in"), sem("ctx_mod_in")
        s_dve, s_act, s_pool = sem("dve_steps"), sem("act_steps"), sem("pool_steps")
        s_log = sem("decay_exp")

        s_nrms, s_nu, s_ntp, s_ncp = (sem(n) for n in ("norm_rms", "norm_u", "norm_turned", "norm_uT"))

        class Norm:
            def __init__(self, tile):
                self.tile = tile

        n_ctx, n_mix, n_moe = Norm(0), [Norm(2), Norm(10)], [Norm(6), Norm(14)]
        s_y, s_yrms, s_h = sem("mixer_y"), sem("y_rms"), sem("h_added")
        SLOW = (("y", 0), ("n", 0), ("y", 1), ("n", 1), ("t", 0), ("y", 2), ("n", 2), ("t", 1), ("y", 3), ("n", 3), ("t", 2), ("t", 3))
        FAST = (("y", 0), ("y", 1), ("n", 0), ("y", 2), ("n", 1), ("t", 0), ("y", 3), ("n", 2), ("t", 1), ("n", 3), ("t", 2), ("t", 3))
        h_base = {"ret": 0, "moe0": 2 * NT, "conv": 4 * NT, "moe1": 6 * NT}

        s_wqk, s_wv, s_wg = sem("qk_panel_in"), sem("v_panel_in"), sem("g_panel_in")
        s_q, s_k, s_kc = sem("q_product"), sem("k_product"), sem("kctx_product")
        s_qkr = sem("qk_rotated")
        s_v, s_vc = sem("v_product"), sem("v_copied")
        s_g, s_gc = sem("g_product"), sem("g_silu")
        s_band, s_bexp, s_bandok = sem("band_exponent"), sem("band_exp"), sem("band_ready")
        s_s, s_sc = sem("scores"), sem("scores_decayed")
        s_o, s_osq, s_oss, s_ord, s_yT = (sem(n) for n in ("o_product", "o_squared", "o_sumsq", "o_rms", "yT_head"))
        s_wo = [sem(f"w_out_in{s}") for s in range(4)]

        s_cw1 = [sem(f"conv_w1_in{s}") for s in range(4)]
        s_crow, s_ccolp, s_ccol = sem("conv_rows_in"), sem("conv_cols_product"), sem("conv_cols")
        s_cag, s_csg, s_zin = sem("conv_glu_product"), sem("conv_gate"), sem("conv_glu")
        s_tap, s_lmu, s_lmuc, s_lcen = sem("conv_taps"), sem("ln_sum"), sem("ln_mean"), sem("ln_centred")
        s_lsq, s_lvar, s_lsd, s_lnx, s_lnu = (sem(n) for n in ("ln_squared", "ln_sumsq", "ln_std", "ln_scaled", "conv_act"))
        s_cw2 = [sem(f"conv_w2_in{s}") for s in range(2)]
        s_cb2 = sem("conv_b2_in")
        s_cy = sem("conv_w2_product")

        class MoeFixed:

            def __init__(self, t):
                self.wr, self.bias = sem(t + "router_in"), sem(t + "bias_in")
                self.urow = [sem(t + f"u_stored{s}") for s in range(2)]
                self.logit, self.score = sem(t + "logits"), sem(t + "scores")
                self.sel, self.cnt, self.nblk = sem(t + "selected"), sem(t + "counts"), sem(t + "blocks")
                self.pos, self.started, self.blk = sem(t + "slots"), sem(t + "started"), sem(t + "block_experts")
                self.ctrl = sem(t + "control")
                self.zero, self.zeroed = sem(t + "zero"), sem(t + "spare_rows_zeroed")
                self.oh, self.list, self.tok = sem(t + "one_hots"), sem(t + "lists"), sem(t + "token_index")
                self.init = sem(t + "sums_started")
                self.sums = [sem(t + f"sums_in{j}") for j in range(NT)]
                self.sw = sem(t + "shared_in")
                self.sup, self.ssg, self.sh = sem(t + "shared_up"), sem(t + "shared_silu"), sem(t + "shared_h")
                self.sy, self.sacc = sem(t + "shared_y"), sem(t + "shared_sum")
                self.tail = sem(t + "blocks_done")

        class MoeLoop:

            def __init__(self, t):
                self.w1 = [sem(t + f"w1_in{s}") for s in range(2)]
                self.w3 = [sem(t + f"w3_in{s}") for s in range(2)]
                self.w2 = [sem(t + f"w2_in{s}") for s in range(2)]
                self.idx = sem(t + "index")
                self.xg = [sem(t + f"x_gathered{s}") for s in range(2)]
                self.xt = sem(t + "x_turned")
                self.xc = sem(t + "xT")
                self.g1 = sem(t + "gate_product")
                self.up = sem(t + "up_product")
                self.sg = sem(t + "gate_silu")
                self.hm = sem(t + "expert_h")
                self.ht = sem(t + "expert_h_turned")
                self.hc = sem(t + "expert_hT")
                self.y = sem(t + "expert_y")
                self.yc = sem(t + "expert_y_copied")
                self.yo = sem(t + "expert_y_added")

        mf = MoeFixed("moe_")
        mo = [MoeLoop(f"moe{i}_") for i in range(2)]
        s_out = sem("out_stored")

        win = ret_w_in[0].rearrange("(p t) n -> p t n", t=KT)
        wqk = ring[0].rearrange("p (t n) -> p t n", t=KT)
        wv = ring[1].rearrange("p (t n) -> p t n", t=KT)
        wg = ring[2].rearrange("p (t n) -> p t n", t=KT)
        wo = [r.rearrange("p (c n) -> p c n", c=4) for r in ring]
        wo_dram = ret_w_out[0].rearrange("(h c p) n -> h p c n", h=HEADS, p=P)
        panel = [r.rearrange("p (t n) -> p t n", t=KT) for r in ring]
        half_panel = [ring[3][:, s * KT * F:(s + 1) * KT * F].rearrange("p (t n) -> p t n", t=KT) for s in range(2)]

        def load_mod_rows(q, part):
            layer, first, _, _, norm_of = MOD_PARTS[part]
            b = mod_part[part]
            cols = slice(first * D, (first + len(norm_of)) * D)
            q.dma_start(b.bias, mod_b[layer, cols].rearrange("(b n) -> b n", n=P)).then_inc(s_mbias[part % 2], 16)
            for row, w in enumerate(norm_of):
                src = consts[0:DB, C_ONE:C_ONE + P] if w is None else norms[layer, w].rearrange("(b n) -> b n", n=P)
                q.dma_start(b.norm[row * DB:(row + 1) * DB, :], src).then_inc(s_mbias[part % 2], 16)

        mod_in = [64, 64, 64 + 48, 64 + 80]
        mod_copied = [6, 12, 16, 24]
        mod_conds = [2, 3, 4, 5]
        mod_w_p = [mod_w[i].rearrange("(p t) n -> p t n", t=KT) for i in range(2)]

        block = stack.enter_context(nc.Block())

        @block.sync
        def _(sp):
            sp.dma_start(c_raw[:, 0, :], c[0].rearrange("(p t) -> p t", t=KT)).then_inc(s_c, 16)
            sp.dma_start(c_raw[:, 1, :], c_ctx.rearrange("(p t) -> p t", t=KT)).then_inc(s_c, 16)

            def mod_panel(n):
                if n >= 3:
                    sp.wait_ge(s_mps, n - 2)
                sp.dma_start(panel[n % 3], mod_w_p[0][:, :, n * W:(n + 1) * W]).then_inc(s_mw[n % 3], 16)

            for n in range(3):
                mod_panel(n)
            sp.dma_start(cst[:, :], consts).then_inc(s_const, 16)
            for part in range(2):
                load_mod_rows(sp, part)
            for n in range(3, 6):
                mod_panel(n)
            sp.dma_start(ctx_x, ctx[0].rearrange("(j p) d -> p j d", p=P)).then_inc(s_ctx, 16)
            sp.dma_start(h, x[0].rearrange("(j p) d -> p j d", p=P)).then_inc(s_x, 16)
            sp.dma_start(dec, ret_decay[0].rearrange("a h -> (a h)").partition_broadcast(P)).then_inc(s_decay, 16)
            for n in range(6, 9):
                mod_panel(n)
            sp.wait_ge(s_mout, 32)
            sp.dma_start(cmod.rearrange("p r d -> p (r d)"), mod_rows[0, 1, 0:2 * D].partition_broadcast(P)).then_inc(s_cmod, 16)
            sp.dma_start(modb[:, 0:3, :].rearrange("p r d -> p (r d)"), mod_rows[0, 0, 0:3 * D].partition_broadcast(P)).then_inc(s_modm, 16)
            for n in range(9, 12):
                mod_panel(n)

            sp.wait_ge(s_mps, 10)
            for hd in peeled(sp, HEADS):
                after(sp, s_kc, hd)
                sp.dma_start(wqk[:, :, 0:DK], win[:, :, ds(hd * DK, DK)]).then_inc(s_wqk, 16)
                sp.dma_start(wqk[:, :, DK:2 * DK], win[:, :, ds(hd * DK + D, DK)]).then_inc(s_wqk, 16)
                if isinstance(hd, int):
                    sp.wait_ge(s_mps, 12)
                after(sp, s_v, hd * KEYT)
                sp.dma_start(wv, win[:, :, ds(hd * DV + 2 * D, DV)]).then_inc(s_wv, 16)
                after(sp, s_g, hd * 4)
                sp.dma_start(wg, win[:, :, ds(hd * DV + 4 * D, DV)]).then_inc(s_wg, 16)
            sp.wait_ge(s_mout, 48)
            sp.dma_start(modb[:, 3:6, :].rearrange("p r d -> p (r d)"), mod_rows[0, 0, 3 * D:6 * D].partition_broadcast(P)).then_inc(s_modf, 16)
            sp.wait_ge(s_kc, HEADS)
            sp.dma_start(wo[0], wo_dram[0]).then_inc(s_wo[0], 16)
            sp.wait_ge(s_v, HEADS * KEYT)
            sp.dma_start(wo[1], wo_dram[1]).then_inc(s_wo[1], 16)
            sp.wait_ge(s_g, HEADS * 4)
            sp.dma_start(wo[2], wo_dram[2]).then_inc(s_wo[2], 16)
            sp.wait_ge(s_o, HEADS * 4)
            sp.dma_start(wo[3], wo_dram[3]).then_inc(s_wo[3], 16)

            def moe(i, mixer):
                m = mo[i]
                w1, w3, w2 = expert(1)

                def store_tokens(j):
                    sp.wait_ge(s_nu, n_moe[i].tile + j + 1)
                    sp.dma_start(u_rows[i][j * P:(j + 1) * P, :], moe_u[i][:, j % 2, :]).then_inc(mf.urow[j % 2], 16)

                for j in range(NT - 1):
                    store_tokens(j)
                sp.wait_ge(s_y if i == 0 else s_cy, NT)
                sp.dma_start(w1, shared_w1[i].rearrange("(p t) f -> p t f", t=KT)).then_inc(mf.sw, 16)
                sp.dma_start(w3, shared_w3[i].rearrange("(p t) f -> p t f", t=KT)).then_inc(mf.sw, 16)
                sp.dma_start(w2, shared_w2[i].rearrange("(p f) d -> p f d", f=FT)).then_inc(mf.sw, 16)
                store_tokens(NT - 1)
                sp.wait_ge(s_h, h_base[mixer] + 2 * NT)
                sp.dma_start(wr, moe_router[i].rearrange("(p t) e -> p t e", t=KT)).then_inc(mf.wr, 16)
                sp.dma_start(bias, moe_bias[i].partition_broadcast(P)).then_inc(mf.bias, 16)
                if i == 0:
                    load_mod_rows(sp, 2)
                if i == 0:
                    sp.wait_ge(mf.zero, 1)
                    sp.dma_start(sum_rows[SEQ:SEQ + P, :].rearrange("p (r z) -> p r z", z=P), zero.unsqueeze(1).to_broadcast([P, D // P, P]))\
                        .then_inc(mf.zeroed, 16)
                sp.wait_ge(mf.ctrl, i + 1)
                pairs = sp.value_load(ctrl[0:1, BLOCKS:BLOCKS + 1], min_val=1, max_val=PAIRS)

                def load(s, b):
                    e = sp.value_load(ctrl[0:1, ds(b, 1)] if not isinstance(b, int) else ctrl[0:1, b:b + 1], min_val=0, max_val=NE - 1)
                    w1, w3, w2 = expert(s)
                    sp.dma_start(w1, moe_w1[i].rearrange("e (p t) f -> p e (t f)", t=KT)[:, ds(e, 1), :].rearrange("p e (t f) -> p (e t) f", t=KT)).then_inc(m.w1[s], 16)
                    sp.dma_start(w3, moe_w3[i].rearrange("e (p t) f -> p e (t f)", t=KT)[:, ds(e, 1), :].rearrange("p e (t f) -> p (e t) f", t=KT)).then_inc(m.w3[s], 16)
                    return w2, e

                def load2(s, w2, e):
                    sp.dma_start(w2, moe_w2[i].rearrange("e (p f) d -> p e (f d)", f=FT)[:, ds(e, 1), :].rearrange("p e (f d) -> p (e f) d", f=FT)).then_inc(m.w2[s], 16)

                load2(0, *load(0, 0))
                for j in range(NT):
                    sp.wait_ge(mf.sacc, i * NT + j + 1)
                    sp.dma_start(sum_rows[j * P:(j + 1) * P, :], macc[:, j, :]).then_inc(mf.init, 16)
                if i == 0:
                    sp.wait_ge(s_mout, 64)
                    sp.dma_start(modb[:, 0:2, :].rearrange("p r d -> p (r d)"), mod_rows[1, 0, 0:2 * D].partition_broadcast(P))\
                        .then_inc(s_modm, 16)
                sp.wait_ge(mf.sy, i * 2 * NT + 2 * NT)
                load2(1, *load(1, 1))
                with sp.Fori(1, pairs) as it:
                    for s in range(2):
                        after(sp, m.up, it * 2 + (s - 1))
                        w2, e = load(s, it * 2 + s)
                        after(sp, m.y, it * 2 + (s - 1))
                        load2(s, w2, e)
                sp.wait_ge(mf.tail, i + 1)
                for j in range(NT):
                    sp.dma_start(macc[:, j, :], sum_rows[j * P:(j + 1) * P, :]).then_inc(mf.sums[j], 16)

            moe(0, "ret")

            sp.wait_ge(s_h, h_base["moe0"] + 2 * NT)
            cw1 = conv_w1[0].rearrange("(p t) n -> p t n", t=KT)
            for s in (0, 2, 1, 3):
                sp.dma_start(panel[s], cw1[:, :, s * W:(s + 1) * W]).then_inc(s_cw1[s], 16)
            for r, a in enumerate([conv_dw[0], conv_b_dw, conv_ln_g, conv_ln_b, conv_b1[0:1, 0:D], conv_b1[0:1, D:2 * D]]):
                r0 = 0 if r == 0 else TAPS - 1 + r
                n = TAPS if r == 0 else 1
                sp.dma_start(chrow[r0:r0 + n, :], a).then_inc(s_crow, 16)
            sp.dma_start(b2row, conv_b2[0].partition_broadcast(P)).then_inc(s_cb2, 16)
            cw2 = conv_w2[0].rearrange("(c p) n -> p c n", p=P)
            sp.wait_ge(s_cag, 4)
            for s in range(2):
                sp.dma_start(panel[2 * s], cw2[:, :, s * W:(s + 1) * W]).then_inc(s_cw2[s], 16)
            load_mod_rows(sp, 3)
            sp.wait_ge(s_cag, KT)
            for n in range(8):
                if n >= 2:
                    sp.wait_ge(s_mps, 20 + n - 1)
                sp.dma_start(panel[1 + 2 * (n % 2)], mod_w_p[1][:, :, 2 * D + n * W:2 * D + (n + 1) * W]).then_inc(s_mw[n % 2], 16)
            sp.wait_ge(s_mout, 80)
            sp.dma_start(modb[:, 2:6, :].rearrange("p r d -> p (r d)"), mod_rows[1, 0, 2 * D:6 * D].partition_broadcast(P)).then_inc(s_modf, 16)
            moe(1, "conv")
            for j in range(NT):
                sp.wait_ge(s_h, h_base["moe1"] + 2 * (j + 1))
                sp.dma_start(out[0, j * P:(j + 1) * P, :], h[:, j, :]).then_inc(s_out, 16)
            sp.wait_ge(s_out, 16 * NT)

        @block.gpsimd
        def _(pool):
            def mod_store(part):
                layer, first, _, _, norm_of = MOD_PARTS[part]
                cols = slice(first * D, (first + len(norm_of)) * D)
                b = mod_part[part]
                pool.wait_ge(s_mcp, mod_copied[part])
                for cond in range(b.conds):
                    pool.dma_start(mod_raw[layer, cond:cond + 1, cols], b.products[cond:cond + 1, :]).then_inc(s_mraw, 16)
                pool.wait_ge(s_mraw, 16 * mod_conds[part])
                for cond in range(b.conds):
                    pool.dma_start(b.rows[:, cond, :], mod_raw[layer, cond, cols].rearrange("(b n) -> b n", n=P)).then_inc(s_mback, 16)
                pool.wait_ge(s_mrow, mod_conds[part])
                for cond in range(b.conds):
                    pool.dma_start(mod_rows[layer, cond, cols].rearrange("(b n) -> b n", n=P), b.rows[:, cond, :]).then_inc(s_mout, 16)

            mod_store(0)
            mod_store(1)
            pool.wait_ge(s_y, NT)
            for n in range(8):
                if n >= 2:
                    pool.wait_ge(s_mps, 12 + n - 1)
                pool.dma_start(half_panel[n % 2], mod_w_p[1][:, :, n * F:(n + 1) * F]).then_inc(s_mwh[n % 2], 16)

            def moe(i, mixer):
                m = mo[i]
                pool.wait_ge(s_h, h_base[mixer] + 2 * NT)
                if i == 0:
                    pool.memset(zero, 0.0).then_inc(mf.zero, 1)
                    mod_store(2)
                pool.wait_ge(mf.tok, i + 1)
                for s in range(2):
                    pool.wait_ge(mf.urow[s], i * 32 + 32)
                pool.wait_ge(mf.ctrl, i + 1)
                pairs = pool.value_load(ctrl[0:1, BLOCKS:BLOCKS + 1], min_val=1, max_val=PAIRS)

                def column(at, table, b, n):
                    colb = table[:, b:b + 1] if isinstance(b, int) else table[:, ds(b, 1)]
                    pool.tensor_copy(idx_col[:, at:at + 1], colb).then_inc(m.idx, 1)
                    pool.wait_ge(m.idx, n)
                    pool.sem_inc(s_pool, 1)

                def gather(s, b, n):
                    column(s, tok_idx, b, n)
                    pool.indirect_dma_start(xg[:, s, :], None, u_rows[i], bass.IndirectOffsetOnAxis(ap=idx_col[:, s:s + 1], axis=0))\
                        .then_inc(m.xg[s], 16)

                def add(s, b, n):
                    column(2 + s, sum_idx, b, n)
                    after(pool, m.yo, b * 16)
                    pool.wait_ge(m.yc, b + 1)
                    pool.sem_inc(s_pool, 1)
                    pool.indirect_dma_start(sum_rows, bass.IndirectOffsetOnAxis(ap=idx_col[:, 2 + s:3 + s], axis=0), yb[:, s, :], None,
                                            compute_op=ALU.add).then_inc(m.yo, 16)

                gather(0, 0, 1)
                gather(1, 1, 2)
                pool.wait_ge(mf.init, (i + 1) * 16 * NT)
                pool.wait_ge(mf.zeroed, 16)
                for it in peeled(pool, pairs):
                    for s in range(2):
                        b = it * 2 + s
                        pool.wait_ge(m.xt, b + 1)
                        gather(s, b + 2, b * 2 + 3)
                        add(s, b, b * 2 + 4)
                for s in range(2):
                    pool.wait_ge(m.xg[s], pairs * 16 + 16)
                pool.wait_ge(m.yo, pairs * 32)
                pool.wait_ge(m.xc, pairs * 2 + 1)
                pool.sem_inc(mf.tail, 1)

            moe(0, "ret")
            mod_store(3)
            moe(1, "conv")

        @block.scalar
        def _(act):
            st = Steps(act, s_act)

            def rms(src, junk, total, root, signal):
                st.then(act.activation(junk, src, ACT.Square, accum_out=total))
                act.activation(root, total, ACT.Sqrt, bias=eps_norm, scale=1.0 / D).then_inc(signal, 1)

            def to_uT(ns, j, dst):
                act.wait_ge(s_ntp, ns.tile + j + 1)
                act.activation(dst[:, :, j * P:(j + 1) * P],
                               ps[:, 2 * (j % 2):2 * (j % 2) + 2, :].rearrange("p b (t n) -> p (b t) n", n=P), ACT.Copy)\
                    .then_inc(s_ncp, 1)

            def between(order, key, ns, y, y_ready, y_junk, junk):
                for step, j in order:
                    if step == "y":
                        y_ready(j)
                        rms(y(j), y_junk, y_ss[:, j:j + 1], y_sd[:, j:j + 1], s_yrms)
                    elif ns is not None and step == "n":
                        act.wait_ge(s_h, h_base[key] + 2 * j + 2)
                        rms(h[:, j, :], junk, ss[:, j:j + 1], sd[:, j:j + 1], s_nrms)
                    elif ns is not None:
                        to_uT(ns, j, uT)

            act.wait_ge(s_c, 32)
            act.activation(c_act.rearrange("p t r -> p r t"), c_raw, ACT.Silu).then_inc(s_cact, 1)

            act.wait_ge(s_const, 16)
            act.wait_ge(s_ctx, 16)
            for j in range(2):
                rms(ctx_x[:, j, :], junk, ss[:, 4 + j:5 + j], sd[:, 4 + j:5 + j], s_nrms)
            act.wait_ge(s_x, 16)
            for j in range(NT):
                rms(h[:, j, :], junk, ss[:, j:j + 1], sd[:, j:j + 1], s_nrms)
            act.wait_ge(s_decay, 16)
            act.wait_ge(s_log, 1)
            act.activation(dec_t[1], dec_t[0], ACT.Exp, scale=-1.0).then_inc(s_log, 1)
            for j in range(2):
                to_uT(n_ctx, j, uTc)
            for j in range(NT):
                to_uT(n_mix[0], j, uT)
            act.wait_ge(s_mout, 48)

            for hd in peeled(act, HEADS):
                after(act, s_band, hd + 1)
                act.activation(band, band, ACT.Exp).then_inc(s_bexp, 1)
                after(act, s_o, hd * 4)
                for m in range(KEYT):
                    after(act, s_v, hd * KEYT + (m + 1))
                    act.activation(V[:, m, :], ps[:, 5 + m % 3, :], ACT.Copy).then_inc(s_vc, 1)
                after(act, s_yT, hd * 4)
                for m in range(4):
                    after(act, s_g, hd * 4 + (m + 1))
                    act.activation(sgT[:, m, :], ps[:, 5 + m % 3, :], ACT.Silu).then_inc(s_gc, 1)
                for m in range(4):
                    after(act, s_o, hd * 4 + (m + 1))
                    act.activation(osq[:, m, :], ps[:, 4 + m, :], ACT.Square).then_inc(s_osq, 1)
                after(act, s_oss, hd + 1)
                act.activation(orstd, ps[:, 3, :], ACT.Sqrt, bias=eps_norm, scale=1.0 / DV).then_inc(s_ord, 1)

            between(SLOW, "ret", n_moe[0], lambda j: ps[:, 2 * j:2 * j + 2, :].rearrange("p b n -> p (b n)"),
                    lambda j: act.wait_ge(s_y, j + 1), junk, mjunk)

            def moe(i, mixer):
                m = mo[i]
                if i == 0:
                    for n in range(4):
                        act.wait_ge(s_mps, 12 + 2 * n + 2)
                        act.activation(mod_part[2].products[:, n * W:(n + 1) * W], ps[0:1, 4 + n, :], ACT.Copy).then_inc(s_mcp, 1)
                act.wait_ge(mf.logit, i + 1)
                act.activation(score, ps[:, 4, 0:NT * NE].rearrange("p (j e) -> p j e", j=NT), ACT.Sigmoid).then_inc(mf.score, 1)
                for f in range(FT):
                    act.wait_ge(mf.sup, i * 2 * FT + f + 1)
                    act.activation(sgs[:, f, :], ps[:, f, :], ACT.Silu).then_inc(mf.ssg, 1)
                for j in range(NT):
                    act.wait_ge(mf.sy, i * 2 * NT + 2 * j + 2)
                    act.activation(macc[:, j, :], ps[:, 2 * (j % 2):2 + 2 * (j % 2), :].rearrange("p b n -> p (b n)"), ACT.Copy)\
                        .then_inc(mf.sacc, 1)
                if i == 0:
                    act.wait_ge(s_mout, 64)
                act.wait_ge(mf.ctrl, i + 1)
                pairs = act.value_load(ctrl[0:1, BLOCKS:BLOCKS + 1], min_val=1, max_val=PAIRS)
                for it in peeled(act, pairs):
                    for s in range(2):
                        after(act, m.g1, it * 2 + (s + 1))
                        act.activation(ex_g[:, s, :], ps[:, 0, 0:F], ACT.Silu).then_inc(m.sg, 1)
                        after(act, m.ht, it * 2 + (s + 1))
                        act.activation(ex_hT[:, s], ps[:, 4, 0:F].rearrange("p (f n) -> p f n", f=FT), ACT.Copy).then_inc(m.hc, 1)
                        after(act, m.y, it * 2 + (s + 1))
                        after(act, m.yo, it * 32 + (s - 1) * 16 if not isinstance(it, int) else 0)
                        act.activation(yb[:, s, :], ps[:, 5:7, :].rearrange("p b n -> p (b n)"), ACT.Copy,
                                       scale=wslot[:, ds(it * 2 + s, 1)] if not isinstance(it, int) else wslot[:, s:s + 1]).then_inc(m.yc, 1)
                between(FAST, f"moe{i}", n_mix[1] if i == 0 else None, lambda j: macc[:, j, :],
                        lambda j: act.wait_ge(mf.sums[j], i * 16 + 16), mjunk, cjunk)

            moe(0, "ret")

            act.wait_ge(s_ccolp, 1)
            act.activation(chp, ps[:, 4, 0:KT * 36].rearrange("p (c k) -> p c k", c=KT), ACT.Copy).then_inc(s_ccol, 1)
            act.wait_ge(s_ccol, 1)
            for cc in range(KT):
                act.wait_ge(s_cag, cc + 1)
                if cc >= 2:
                    act.wait_ge(s_zin, cc - 1)
                act.activation(sgate[:, cc % 2, :], ps[:, 2 * (cc % 2) + 1, :], ACT.Sigmoid, bias=chp[:, cc, 35:36]).then_inc(s_csg, 1)
            for n in range(8):
                act.wait_ge(s_mps, 20 + n + 1)
                act.activation(mod_part[3].products[:, n * W:(n + 1) * W], ps[0:1, 6 + n % 2, :], ACT.Copy).then_inc(s_mcp, 1)
            act.wait_ge(s_lmu, 1)
            act.activation(mu, ps[:, 4, :], ACT.Copy, scale=1.0 / D).then_inc(s_lmuc, 1)
            for cc in range(KT):
                act.wait_ge(s_lcen, cc + 1)
                if cc >= 2:
                    act.wait_ge(s_lvar, cc - 1)
                act.activation(lsq[:, cc % 2, :], cacc[:, cc, :], ACT.Square).then_inc(s_lsq, 1)
            act.wait_ge(s_lvar, KT)
            act.activation(lrs, ps[:, 5, :], ACT.Sqrt, bias=eps_ln, scale=1.0 / D).then_inc(s_lsd, 1)
            for cc in range(KT):
                act.wait_ge(s_lnx, cc + 1)
                act.activation(zin[:, cc, 0:SEQ], cacc[:, cc, :], ACT.Silu, bias=chp[:, cc, 33:34], scale=chp[:, cc, 32:33])\
                    .then_inc(s_lnu, 1)
            between(SLOW, "conv", n_moe[1], lambda j: ybuf[:, j, :], lambda j: act.wait_ge(s_y, NT + j + 1),
                    sgate.rearrange("p s n -> p (s n)"), sgate.rearrange("p s n -> p (s n)"))
            moe(1, "conv")

        @block.tensor
        def _(pe):
            def turn(ns, j, src):
                pe.wait_ge(s_nu, ns.tile + j + 1)
                if j >= 2:
                    pe.wait_ge(s_ncp, ns.tile + j - 1)
                for t in range(KT):
                    last = pe.transpose(ps[:, 2 * (j % 2) + t // 4, (t % 4) * P:(t % 4 + 1) * P],
                                        src[:, j % 2, :].rearrange("n (p t) -> n t p", t=KT)[:, t, :], ident)
                last.then_inc(s_ntp, 1)

            def mod_product(w, loaded, count, conds, out):
                after(pe, loaded, count)
                for t in range(KT):
                    last = pe.matmul(out[0:conds, :], c_act[:, t, 0:conds], w[:, t, :], start=(t == 0), stop=(t == KT - 1))
                last.then_inc(s_mps, 1)

            pe.wait_ge(s_cact, 1)
            for n in range(9):
                if n >= 3:
                    pe.wait_ge(s_mcp, n - 2)
                mod_product(panel[n % 3], s_mw[n % 3], n // 3 * 16 + 16, 2 if n < 6 else 1, ps[:, 4 + n % 3, :])
            pe.wait_ge(s_const, 16)
            for j in range(2):
                turn(n_ctx, j, ubuf)
            pe.wait_ge(s_ncp, n_ctx.tile + 2)
            for j in range(NT):
                turn(n_mix[0], j, ubuf)
            pe.wait_ge(s_ncp, n_mix[0].tile + NT)
            for n in range(9, 12):
                pe.wait_ge(s_mcp, n - 2)
                mod_product(panel[n % 3], s_mw[n % 3], n // 3 * 16 + 16, 1, ps[:, 4 + n % 3, :])
            pe.wait_ge(s_mcp, 12)

            for hd in peeled(pe, HEADS):
                after(pe, s_wqk, hd * 32 + 32)
                after(pe, s_sc, hd * KEYT)
                for e in range(2):
                    for t in range(KT):
                        last = pe.matmul(ps[:, e, :], wqk[:, t, 0:DK].rearrange("p (m e) -> p e m", e=2)[:, e, :], uT[:, t, :],
                                         start=(t == 0), stop=(t == KT - 1))
                last.then_inc(s_q, 1)
                after(pe, s_ord, hd)
                for e in range(2):
                    for t in range(KT):
                        last = pe.matmul(ps[:, 2 + e, :], wqk[:, t, DK:2 * DK].rearrange("p (m e) -> p e m", e=2)[:, e, :], uT[:, t, :],
                                         start=(t == 0), stop=(t == KT - 1))
                last.then_inc(s_k, 1)
                after(pe, s_yT, hd * 4)
                for e in range(2):
                    for t in range(KT):
                        last = pe.matmul(ps[:, 4, e * CTX:(e + 1) * CTX], wqk[:, t, DK:2 * DK].rearrange("p (m e) -> p e m", e=2)[:, e, :],
                                         uTc[:, t, :], start=(t == 0), stop=(t == KT - 1))
                last.then_inc(s_kc, 1)
                after(pe, s_wv, hd * 16 + 16)
                for m in range(KEYT):
                    if m >= 3:
                        after(pe, s_vc, hd * KEYT + (m - 2))
                    src = uT[:, :, m * P:(m + 1) * P] if m < NT else uTc[:, :, (m - NT) * P:(m - NT + 1) * P]
                    for t in range(KT):
                        last = pe.matmul(ps[:, 5 + m % 3, :], src[:, t, :], wv[:, t, :], start=(t == 0), stop=(t == KT - 1))
                    last.then_inc(s_v, 1)
                after(pe, s_wg, hd * 16 + 16)
                for m in range(4):
                    after(pe, s_vc, hd * KEYT + min(m + 4, KEYT))
                    if m == 3:
                        after(pe, s_gc, hd * 4 + 1)
                    for t in range(KT):
                        last = pe.matmul(ps[:, 5 + m % 3, :], wg[:, t, m * P:(m + 1) * P], uT[:, t, :],
                                         start=(t == 0), stop=(t == KT - 1))
                    last.then_inc(s_g, 1)
                for m in range(KEYT):
                    after(pe, s_qkr, hd * 6 + 6)
                    if m >= 4:
                        after(pe, s_sc, hd * KEYT + (m - 3))
                    for e in range(2):
                        last = pe.matmul(ps[:, m % 4, :], kT[:, e, m * P:(m + 1) * P], qT[:, e, :], start=(e == 0), stop=(e == 1))
                    last.then_inc(s_s, 1)
                after(pe, s_vc, hd * KEYT + KEYT)
                after(pe, s_gc, hd * 4 + 4)
                for cc in range(4):
                    for m in range(KEYT):
                        after(pe, s_sc, hd * KEYT + (m + 1))
                        last = pe.matmul(ps[:, 4 + cc, :], V[:, m, cc * P:(cc + 1) * P], ST[:, m, :], start=(m == 0), stop=(m == KEYT - 1))
                    last.then_inc(s_o, 1)
                for cc in range(4):
                    after(pe, s_osq, hd * 4 + (cc + 1))
                    last = pe.matmul(ps[:, 3, :], ones, osq[:, cc, :], start=(cc == 0), stop=(cc == 3))
                last.then_inc(s_oss, 1)

            pe.wait_ge(s_yT, HEADS * 4)
            pe.wait_ge(s_ord, HEADS)
            for j in range(NT):
                if j >= 2:
                    turn(n_moe[0], j - 2, mubuf)
                for half in range(2):
                    for cc in range(4 * HEADS):
                        pe.wait_ge(s_wo[cc // 4], 16)
                        last = pe.matmul(ps[:, 2 * j + half, :], yT[:, cc, j * P:(j + 1) * P], wo[cc // 4][:, cc % 4, half * W:(half + 1) * W],
                                         start=(cc == 0), stop=(cc == 4 * HEADS - 1))
                last.then_inc(s_y, 1)

            def moe(i, mixer):
                m = mo[i]
                turn(n_moe[i], 2, moe_u[i])
                if i == 0:
                    pe.wait_ge(s_h, h_base[mixer] + 2 * NT)
                    for n in range(8):
                        mod_product(half_panel[n % 2], s_mwh[n % 2], n // 2 * 16 + 16, 1, ps[:, 4 + n // 2, n % 2 * F:(n % 2 + 1) * F])
                turn(n_moe[i], 3, moe_u[i])
                pe.wait_ge(s_ncp, n_moe[i].tile + NT)
                pe.wait_ge(mf.wr, i * 16 + 16)
                if i == 0:
                    pe.wait_ge(s_mcp, 13)
                for j in range(NT):
                    for t in range(KT):
                        last = pe.matmul(ps[:, 4, j * NE:(j + 1) * NE], uT[:, t, j * P:(j + 1) * P], wr[:, t, :],
                                         start=(t == 0), stop=(t == KT - 1))
                last.then_inc(mf.logit, 1)
                w1, w3, w2 = expert(1)
                pe.wait_ge(mf.sw, i * 48 + 48)

                def shared_up(wi, f):
                    for t in range(KT):
                        last = pe.matmul(ps[:, 2 * wi + f, :], (w1, w3)[wi][:, t, :].rearrange("p (m f) -> p f m", f=FT)[:, f, :], uT[:, t, :],
                                         start=(t == 0), stop=(t == KT - 1))
                    last.then_inc(mf.sup, 1)

                shared_up(0, 0)
                pe.wait_ge(mf.sel, i * NT + NT)
                if i == 0:
                    pe.wait_ge(s_mcp, 16)
                for j in range(NT):
                    last = pe.matmul(ps[0:NE, 4, 256:257], sel[:, j, :], ones[:, 0:1], start=(j == 0), stop=(j == NT - 1))
                last.then_inc(mf.cnt, 1)
                pe.wait_ge(mf.nblk, i * 2 + 2)
                for j in range(NT):
                    pe.matmul(ps[:, 5, j * NE:(j + 1) * NE], nblk_b[0:NE, :], cst[0:NE, C_TRI:C_TRI + NE], start=True, stop=False)
                    for jj in range(j):
                        pe.matmul(ps[:, 5, j * NE:(j + 1) * NE], ones, sel[:, jj, :], start=False, stop=False)
                    last = pe.matmul(ps[:, 5, j * NE:(j + 1) * NE], cst[:, C_TRI:C_TRI + P], sel[:, j, :], start=False, stop=True)
                last.then_inc(mf.pos, 1)
                pe.matmul(ps[0:NE, 6, 0:1], cst[0:NE, C_TRII:C_TRII + NE], cnt[0:NE, 4:5], start=True, stop=True).then_inc(mf.started, 1)
                pe.matmul(ps[0:1, 6, 256:257], ones[0:NE, 0:1], cnt[0:NE, 4:5], start=True, stop=True).then_inc(mf.started, 1)
                pe.wait_ge(mf.started, i * 3 + 3)
                pe.matmul(ps[0:1, 6, 300:300 + BLOCKS], ones[0:NE, 0:1], started[0:NE, 0:BLOCKS], start=True, stop=True).then_inc(mf.blk, 1)
                for wi, f in ((0, 1), (1, 0), (1, 1)):
                    shared_up(wi, f)
                for j in range(NT):
                    pe.wait_ge(mf.oh, i * NT + j + 1)
                    for k in range(TOPK):
                        last = pe.matmul(ps[:, 7, 0:2 * BLOCKS], oh_r[:, j % 2, k, :], oh_b[:, j % 2, k].rearrange("p w b -> p (w b)"),
                                         start=(j == 0 and k == 0), stop=(j == NT - 1 and k == TOPK - 1))
                    last.then_inc(mf.list, 1)
                pe.wait_ge(mf.sh, (i + 1) * FT)
                for j in range(NT):
                    if j >= 2:
                        pe.wait_ge(mf.sacc, i * NT + j - 1)
                    for half in range(2):
                        for f in range(FT):
                            last = pe.matmul(ps[:, 2 * (j % 2) + half, :], hsT[:, f, j * P:(j + 1) * P], w2[:, f, half * W:(half + 1) * W],
                                             start=(f == 0), stop=(f == FT - 1))
                        last.then_inc(mf.sy, 1)
                pe.wait_ge(mf.sacc, (i + 1) * NT)
                pe.wait_ge(mf.ctrl, i + 1)
                pairs = pe.value_load(ctrl[0:1, BLOCKS:BLOCKS + 1], min_val=1, max_val=PAIRS)

                def turn_x(s, n, part):
                    if part == 0:
                        after(pe, m.xg[s], n)
                    for t in range(4 * part, 4 * part + 4):
                        last = pe.transpose(ps[:, 2 + t // 4, (t % 4) * P:(t % 4 + 1) * P],
                                            xg[:, s, :].rearrange("n (p t) -> n t p", t=KT)[:, t, :], ident)
                    if part == 1:
                        last.then_inc(m.xt, 1)

                turn_x(0, 16, 0)
                turn_x(0, 16, 1)
                for it in peeled(pe, pairs):
                    for s in range(2):
                        w1, w3, w2 = expert(s)
                        after(pe, m.xc, it * 2 + (s + 1))
                        after(pe, m.w1[s], it * 16 + 16)
                        for t in range(KT):
                            last = pe.matmul(ps[:, 0, 0:F], xT[:, s, t, :], w1[:, t, :], start=(t == 0), stop=(t == KT - 1))
                        last.then_inc(m.g1, 1)
                        after(pe, m.w3[s], it * 16 + 16)
                        for t in range(KT):
                            last = pe.matmul(ps[:, 1, 0:F], xT[:, s, t, :], w3[:, t, :], start=(t == 0), stop=(t == KT - 1))
                        last.then_inc(m.up, 1)
                        nxt = it * 16 + (16 if s == 0 else 32)
                        turn_x(1 - s, nxt, 0)
                        after(pe, m.hm, it * 2 + (s + 1))
                        for f in range(FT):
                            last = pe.transpose(ps[:, 4, f * P:(f + 1) * P], ex_h[:, s, :].rearrange("n (m f) -> n f m", f=FT)[:, f, :], ident)
                        last.then_inc(m.ht, 1)
                        turn_x(1 - s, nxt, 1)
                        after(pe, m.hc, it * 2 + (s + 1))
                        after(pe, m.w2[s], it * 16 + 16)
                        after(pe, m.yc, it * 2 + s)
                        for half in range(2):
                            for f in range(FT):
                                last = pe.matmul(ps[:, 5 + half, :], ex_hT[:, s, f, :], w2[:, f, half * W:(half + 1) * W],
                                                 start=(f == 0), stop=(f == FT - 1))
                        last.then_inc(m.y, 1)

            moe(0, "ret")

            for j in range(NT):
                turn(n_mix[1], j, cubuf)
            pe.wait_ge(s_ncp, n_mix[1].tile + NT)
            pe.wait_ge(s_crow, 16 * 6)
            for cc in range(KT):
                last = pe.transpose(ps[:, 4, cc * 36:(cc + 1) * 36], chrow[0:36, cc * P:(cc + 1) * P], ident[0:36, 0:36])
            last.then_inc(s_ccolp, 1)
            for cc in range(KT):
                if cc >= 2:
                    pe.wait_ge(s_zin, cc - 1)
                for gate in range(2):
                    s = 2 * gate + cc // 4
                    pe.wait_ge(s_cw1[s], 16)
                    for t in range(KT):
                        last = pe.matmul(ps[:, 2 * (cc % 2) + gate, :], panel[s][:, t, (cc % 4) * P:(cc % 4 + 1) * P], uT[:, t, :],
                                         start=(t == 0), stop=(t == KT - 1))
                last.then_inc(s_cag, 1)
            pe.wait_ge(s_zin, KT)
            for n in range(8):
                if n >= 2:
                    pe.wait_ge(s_mcp, 16 + n - 1)
                mod_product(panel[1 + 2 * (n % 2)], s_mw[n % 2], n // 2 * 16 + 80, 1, ps[:, 6 + n % 2, :])
            pe.wait_ge(s_ccol, 1)
            for cc in range(KT):
                pe.wait_ge(s_tap, 2 * (cc // 2) + 2)
                last = pe.matmul(ps[:, 4, :], ones, cacc[:, cc, :], start=(cc == 0), stop=(cc == KT - 1))
            last.then_inc(s_lmu, 1)
            for cc in range(KT):
                pe.wait_ge(s_lsq, cc + 1)
                pe.matmul(ps[:, 5, :], ones, lsq[:, cc % 2, :], start=(cc == 0), stop=(cc == KT - 1)).then_inc(s_lvar, 1)
            pe.wait_ge(s_lnu, KT)
            for s in range(2):
                pe.wait_ge(s_cw2[s], 16)
            for j in range(NT):
                if j >= 2:
                    turn(n_moe[1], j - 2, cmubuf)
                for half in range(2):
                    for cc in range(KT):
                        last = pe.matmul(ps[:, 2 * j + half, :], zin[:, cc, j * P:(j + 1) * P], panel[2 * half][:, cc, :],
                                         start=(cc == 0), stop=(cc == KT - 1))
                last.then_inc(s_cy, 1)
            moe(1, "conv")

        @block.vector
        def _(dve):
            st = Steps(dve, s_dve)
            MUL, ADD, SUB, MAX, MIN = ALU.mult, ALU.add, ALU.subtract, ALU.max, ALU.min

            def mod_copy(part, panels):
                b = mod_part[part]
                for n in panels:
                    dve.wait_ge(s_mps, 6 * part + n + 1)
                    dve.tensor_copy(b.products[:, n * W:(n + 1) * W], ps[0:b.conds, 4 + n % 3, :]).then_inc(s_mcp, 1)

            def mod_finish(part):
                b = mod_part[part]
                dve.wait_ge(s_const, 16)
                dve.wait_ge(s_mbias[part % 2], mod_in[part])
                dve.wait_ge(s_mback, 16 * mod_conds[part])
                st.then(dve.tensor_tensor(b.rows, b.rows, b.bias.unsqueeze(1).to_broadcast([b.blocks, b.conds, P]), ADD))
                for cond in range(b.conds):
                    dve.scalar_tensor_tensor(b.rows[:, cond, :], b.rows[:, cond, :], cst[0:b.blocks, C_ONEPLUS + part:C_ONEPLUS + part + 1],
                                             b.norm, ADD, MUL).then_inc(s_mrow, 1)

            def norm_modulate(ns, j, root, src, scale, shift, dst):
                dve.wait_ge(s_nrms, ns.tile + j + 1)
                st.then(dve.reciprocal(rs[:, root:root + 1], sd[:, root:root + 1]))
                if j >= 2:
                    dve.wait_ge(s_ntp, ns.tile + j - 1)
                st.then(dve.scalar_tensor_tensor(dst[:, j % 2, :], src, rs[:, root:root + 1], scale, MUL, MUL))
                dve.tensor_tensor(dst[:, j % 2, :], dst[:, j % 2, :], shift, ADD).then_inc(s_nu, 1)

            def residual(key, j, y, gate, tmp):
                dve.wait_ge(s_yrms, h_base[key] // 2 + j + 1)
                st.then(dve.reciprocal(y_rs[:, j:j + 1], y_sd[:, j:j + 1]))
                dve.scalar_tensor_tensor(tmp, y, y_rs[:, j:j + 1], gate, MUL, MUL).then_inc(s_h, 1)
                dve.wait_ge(s_h, h_base[key] + 2 * j + 1)
                dve.tensor_tensor(h[:, j, :], h[:, j, :], tmp, ADD).then_inc(s_h, 1)

            def between(order, key, ns, y, gate, tmp, rows, dst, stored):
                for step, j in order:
                    if step == "y":
                        if j:
                            dve.wait_ge(s_h, h_base[key] + 2 * j)
                        residual(key, j, y(j), gate, tmp)
                    elif step == "n" and ns is not None:
                        dve.wait_ge(s_h, h_base[key] + 2 * j + 2)
                        if j >= 2 and stored is not None:
                            dve.wait_ge(mf.urow[j % 2], stored)
                        norm_modulate(ns, j, j, h[:, j, :], modb[:, rows + 1, :], modb[:, rows, :], dst)

            mod_copy(0, range(6))
            mod_finish(0)
            dve.wait_ge(s_decay, 16)
            st.then(dve.tensor_scalar(dec_t[1], dec, -1.0, None, MUL))
            dve.tensor_tensor(dec_t[0], dec, dec_t[1], MAX).then_inc(s_log, 1)
            dve.wait_ge(s_log, 2)
            z, d2, r2, sv, s2, q = dec_t[1], dec_t[2], dec_t[3], dec_t[4], dec_t[5], dec_t[0]
            st.then(dve.tensor_scalar(d2, z, 2.0, None, ADD))
            st.then(dve.reciprocal(r2, d2))
            st.then(dve.tensor_tensor(sv, z, r2, MUL))
            st.then(dve.tensor_tensor(s2, sv, sv, MUL))
            st.then(dve.tensor_scalar(q, s2, 1.0 / 15, None, MUL))
            for k in (13, 11, 9, 7, 5, 3):
                st.then(dve.scalar_tensor_tensor(q, q, 1.0 / k, s2, ADD, MUL))
            st.then(dve.scalar_tensor_tensor(q, q, 1.0, sv, ADD, MUL))
            st.then(dve.tensor_scalar(d2, dec, 0.0, None, MIN))
            st.then(dve.scalar_tensor_tensor(r2, q, -2.0, d2, MUL, ADD))
            st.then(dve.tensor_copy(lgf, r2[:, 0:4]))
            st.then(dve.tensor_scalar(nlgb, r2[:, 4:8], -1.0, None, MUL))

            dve.wait_ge(s_cmod, 16)
            dve.wait_ge(s_ctx, 16)
            for j in range(2):
                norm_modulate(n_ctx, j, 4 + j, ctx_x[:, j, :], cmod[:, 1, :], cmod[:, 0, :], ubuf)
            mod_copy(1, range(3))
            dve.wait_ge(s_ntp, n_ctx.tile + 2)
            dve.wait_ge(s_x, 16)
            dve.wait_ge(s_modm, 16)
            for j in range(NT):
                norm_modulate(n_mix[0], j, j, h[:, j, :], modb[:, 1, :], modb[:, 0, :], ubuf)
            dve.wait_ge(s_nu, n_mix[0].tile + NT)
            dve.wait_ge(s_ntp, n_mix[0].tile + NT)
            dve.wait_ge(s_const, 16)

            mod_copy(1, range(3, 6))
            mod_finish(1)
            pos = cst[:, C_POS:C_POS + BAND]
            per_head = 3 + 2 + 12 + 1 + 4
            base = st.n
            for hd in peeled(dve, HEADS):
                st.n = hd * per_head + base
                after(dve, s_sc, hd * KEYT)
                st.then(dve.tensor_scalar(band, pos, 0.0, lgf[:, ds(hd, 1)], MAX, MUL))
                bt = rot.rearrange("p i n -> p (i n)")[:, 0:BAND]
                after(dve, s_o, hd * 4)
                st.then(dve.tensor_scalar(bt, pos, 0.0, nlgb[:, ds(hd, 1)], MIN, MUL))
                dve.tensor_tensor(band, band, bt, ADD).then_inc(s_band, 1)
                after(dve, s_bexp, hd + 1)
                st.then(dve.tensor_tensor(band[:, 640:640 + P], band[:, 640:640 + P], ident, ADD))
                for m in range(2):
                    last = dve.tensor_tensor(dctx[:, m, :], band[:, 640 - P * (m - 2):640 - P * (m - 2) + SEQ],
                                             band[:, 640 - P * (m + 4):640 - P * (m + 4) + SEQ], ADD)
                    st.done(last)
                after(dve, s_oss, hd)
                k0 = 0
                for signal, a, b, cs, dst in (
                    (s_q, ps[:, 0, :], ps[:, 1, :], slice(0, SEQ), qT),
                    (s_k, ps[:, 2, :], ps[:, 3, :], slice(0, SEQ), kT[:, :, 0:SEQ]),
                    (s_kc, ps[:, 4, 0:CTX], ps[:, 4, CTX:2 * CTX], slice(SEQ, SEQ + CTX), kT[:, :, SEQ:SEQ + CTX]),
                ):
                    n = cs.stop - cs.start
                    after(dve, signal, hd + 1)
                    if k0:
                        after(dve, s_qkr, hd * 6 + k0)
                    c_, s_ = cos[:, cs], sin[:, cs]
                    st.done(dve.tensor_tensor(rot[:, 0, 0:n], a, c_, MUL))
                    st.done(dve.tensor_tensor(rot[:, 1, 0:n], b, s_, MUL))
                    st.done(dve.tensor_tensor(rot[:, 2, 0:n], a, s_, MUL))
                    st.then(dve.tensor_tensor(rot[:, 3, 0:n], b, c_, MUL))
                    dve.tensor_tensor(dst[:, 0, :], rot[:, 0, 0:n], rot[:, 1, 0:n], SUB).then_inc(s_qkr, 1)
                    dve.tensor_tensor(dst[:, 1, :], rot[:, 2, 0:n], rot[:, 3, 0:n], ADD).then_inc(s_qkr, 1)
                    k0 += 2
                after(dve, s_qkr, hd * 6 + 6)
                for m in range(KEYT):
                    after(dve, s_s, hd * KEYT + (m + 1))
                    dk = band[:, 640 - P * m:640 - P * m + SEQ] if m < NT else dctx[:, m - NT, :]
                    dve.scalar_tensor_tensor(ST[:, m, :], ps[:, m % 4, :], DK ** -0.5, dk, MUL, MUL).then_inc(s_sc, 1)
                after(dve, s_ord, hd + 1)
                after(dve, s_gc, hd * 4 + 4)
                st.then(dve.reciprocal(orstd, orstd))
                for cc in range(4):
                    if cc:
                        after(dve, s_yT, hd * 4 + cc)
                    ins = dve.tensor_tensor(otmp, ps[:, 4 + cc, :], orstd, MUL)
                    st.then(ins)
                    dve.tensor_tensor(yT[:, ds(hd * 4 + cc, 1), :].rearrange("p o n -> p (o n)"), otmp, sgT[:, cc, :], MUL).then_inc(s_yT, 1)
            st.n = base + HEADS * per_head

            dve.wait_ge(s_modf, 16)
            between(SLOW, "ret", n_moe[0], lambda j: ps[:, 2 * j:2 * j + 2, :].rearrange("p b n -> p (b n)"), modb[:, 2, :], junk,
                    3, mubuf, 16)

            def moe(i, mixer):
                m = mo[i]
                dve.wait_ge(s_h, h_base[mixer] + 2 * NT)
                if i == 0:
                    mod_finish(2)
                st.done(dve.memset(gsx[:, :, NG:NG + 4], -MARK))
                st.done(dve.memset(grep[:, :, 4:8], -MARK))
                dve.wait_ge(mf.score, i + 1)
                dve.wait_ge(mf.bias, i * 16 + 16)
                st.then(dve.tensor_tensor(biased, score, bias.unsqueeze(1).to_broadcast([P, NT, NE]), ADD))
                for j in range(NT):
                    for g in range(NG):
                        st.done(dve.max(gtop[:, j, g, :], biased[:, j, g * PER:(g + 1) * PER]))
                after(dve, s_dve, st.n)
                st.then(dve.tensor_tensor(gsx[:, :, 0:NG], gtop[:, :, :, 0], gtop[:, :, :, 1], ADD))
                for j in range(NT):
                    st.done(dve.max(gmax[:, j, :], gsx[:, j, :]))
                after(dve, s_dve, st.n)
                st.then(dve.tensor_copy(grep[:, :, 0:4], gmax[:, :, 0:4]))
                for j in range(NT):
                    st.done(dve.match_replace(gout[:, j, :], grep[:, j, :], gsx[:, j, :], MARK))
                after(dve, s_dve, st.n)
                st.then(dve.tensor_scalar(gmask, gout[:, :, 0:NG], MARK, None, ALU.is_equal))
                st.then(dve.tensor_scalar(gneg, gmask, 1.0, -LOW, SUB, MUL))
                for j in range(NT):
                    st.done(dve.tensor_tensor(rep[:, j].rearrange("p (g k) -> p g k", g=NG), biased[:, j].rearrange("p (g k) -> p g k", g=NG),
                                              gmask[:, j].unsqueeze(2).to_broadcast([P, NG, PER]), MUL))
                after(dve, s_dve, st.n)
                for j in range(NT):
                    st.done(dve.tensor_tensor(biased[:, j].rearrange("p (g k) -> p g k", g=NG), rep[:, j].rearrange("p (g k) -> p g k", g=NG),
                                              gneg[:, j].unsqueeze(2).to_broadcast([P, NG, PER]), ADD))
                after(dve, s_dve, st.n)
                for j in range(NT):
                    st.done(dve.max(top8[:, j, :], biased[:, j, :]))
                after(dve, s_dve, st.n)
                for j in range(NT):
                    st.done(dve.match_replace(rep[:, j, :], top8[:, j, :], biased[:, j, :], MARK))
                after(dve, s_dve, st.n)
                for j in range(NT):
                    dve.tensor_scalar(sel[:, j, :], rep[:, j, :], MARK, None, ALU.is_equal).then_inc(mf.sel, 1)
                dve.wait_ge(mf.sel, i * NT + NT)
                dve.wait_ge(mf.cnt, i + 1)
                st.then(dve.tensor_copy(cnt[0:NE, 5:6], ps[0:NE, 4, 256:257]))
                st.then(dve.tensor_scalar(cnt[0:NE, 0:4], cst[0:NE, C_THR:C_THR + NT], cnt[0:NE, 5:6], None, ALU.is_lt))
                dve.tensor_reduce(cnt[0:NE, 4:5], cnt[0:NE, 0:4], AX.X, ADD).then_inc(mf.nblk, 1)
                dve.wait_ge(mf.nblk, i * 2 + 1)
                dve.tensor_scalar(nblk_b[0:NE, :], ones[0:NE, :], cnt[0:NE, 4:5], float(P), MUL, MUL).then_inc(mf.nblk, 1)
                dve.wait_ge(mf.started, i * 3 + 2)
                st.then(dve.tensor_copy(cnt[0:NE, 6:7], ps[0:NE, 6, 0:1]))
                dve.tensor_scalar(started[0:NE, 0:BLOCKS], cst[0:NE, C_IOTA:C_IOTA + BLOCKS], cnt[0:NE, 6:7], None, ALU.is_ge).then_inc(mf.started, 1)
                dve.wait_ge(mf.pos, i + 1)
                for j in range(NT):
                    st.done(dve.tensor_scalar(slotk[:, j, :], ps[:, 5, j * NE:(j + 1) * NE], -1.0, BIG, MUL, ADD))
                after(dve, s_dve, st.n)
                st.then(dve.tensor_tensor(slotk, slotk, sel, MUL))
                for j in range(NT):
                    st.done(dve.max(topslot[:, j, :], slotk[:, j, :]))
                after(dve, s_dve, st.n)
                dve.wait_ge(mf.blk, i + 1)
                st.done(dve.tensor_scalar(ctrl[0:1, 0:BLOCKS], ps[0:1, 6, 300:300 + BLOCKS], float(NE - 1), None, MIN))
                after(dve, s_dve, st.n)
                dve.tensor_scalar(ctrl[0:1, BLOCKS:BLOCKS + 1], ps[0:1, 6, 256:257], 0.5, 0.25, MUL, ADD).then_inc(mf.ctrl, 1)
                st.then(dve.tensor_tensor(wn, score, sel, MUL))
                st.then(dve.tensor_reduce(wsum[:, 0:NT], wn, AX.X, ADD))
                st.then(dve.reciprocal(wsum[:, 4:8], wsum[:, 0:NT]))
                for j in range(NT):
                    st.done(dve.tensor_scalar(wn[:, j, :], wn[:, j, :], wsum[:, 4 + j:5 + j], ROUTE_SCALE, MUL, MUL))
                after(dve, s_dve, st.n)
                for j in range(NT):
                    st.then(dve.tensor_tensor(eq, slotk[:, j].unsqueeze(1).to_broadcast([P, TOPK, NE]),
                                              topslot[:, j].unsqueeze(2).to_broadcast([P, TOPK, NE]), ALU.is_equal))
                    st.then(dve.tensor_tensor(eq, eq, wn[:, j].unsqueeze(1).to_broadcast([P, TOPK, NE]), MUL))
                    st.then(dve.tensor_reduce(wk[:, j, :], eq, AX.X, ADD))
                st.then(dve.tensor_scalar(slot_i, topslot.rearrange("p j k -> p (j k)"), -1.0, BIG, MUL, ADD))
                st.done(dve.tensor_scalar(slot_ri, slot_i, P - 1, None, ALU.bitwise_and))
                st.then(dve.tensor_scalar(slot_bi, slot_i, 7, None, ALU.logical_shift_right))
                st.done(dve.tensor_copy(slot_r.rearrange("p j k -> p (j k)"), slot_ri))
                st.then(dve.tensor_copy(slot_b.rearrange("p j k -> p (j k)"), slot_bi))
                iota = cst[:, C_IOTA:C_IOTA + P]
                for s in range(2):
                    dve.wait_ge(mf.urow[s], i * 32 + 32)
                for j in range(NT):
                    if j >= 2:
                        dve.wait_ge(mf.list, i * NT + j - 1)
                    oh, ow = oh_b[:, j % 2, :, 0, :], oh_b[:, j % 2, :, 1, :]
                    st.done(dve.tensor_tensor(oh_r[:, j % 2], iota.unsqueeze(1).to_broadcast([P, TOPK, P]),
                                              slot_r[:, j].unsqueeze(2).to_broadcast([P, TOPK, P]), ALU.is_equal))
                    st.then(dve.tensor_tensor(oh, iota[:, 0:BLOCKS].unsqueeze(1).to_broadcast([P, TOPK, BLOCKS]),
                                              slot_b[:, j].unsqueeze(2).to_broadcast([P, TOPK, BLOCKS]), ALU.is_equal))
                    st.then(dve.tensor_tensor(ow, oh, wk[:, j].unsqueeze(2).to_broadcast([P, TOPK, BLOCKS]), MUL))
                    dve.tensor_scalar(oh, oh, cst[:, C_TOK + j:C_TOK + j + 1], None, MUL).then_inc(mf.oh, 1)
                for f in range(FT):
                    dve.wait_ge(mf.ssg, i * FT + f + 1)
                    dve.wait_ge(mf.sup, i * 2 * FT + FT + f + 1)
                    dve.tensor_tensor(hsT[:, f, :], ps[:, 2 + f, :], sgs[:, f, :], MUL).then_inc(mf.sh, 1)
                dve.wait_ge(mf.list, (i + 1) * NT)
                st.done(dve.tensor_copy(wslot, ps[:, 7, BLOCKS:2 * BLOCKS]))
                st.then(dve.tensor_scalar(is_pad, ps[:, 7, 0:BLOCKS], 0.0, cst[:, C_DUMP:C_DUMP + 1], ALU.is_equal, MUL))
                st.done(dve.scalar_tensor_tensor(sum_idx, ps[:, 7, 0:BLOCKS], -1.0, is_pad, ADD, ADD))
                dve.wait_ge(s_dve, st.n)
                dve.tensor_scalar(tok_idx, ps[:, 7, 0:BLOCKS], -1.0, 0.0, ADD, MAX).then_inc(mf.tok, 1)

                dve.wait_ge(mf.ctrl, i + 1)
                pairs = dve.value_load(ctrl[0:1, BLOCKS:BLOCKS + 1], min_val=1, max_val=PAIRS)

                def copy_xT(s, n):
                    after(dve, m.xt, n)
                    dve.tensor_copy(xT[:, s], ps[:, 2:4, :].rearrange("p b (t n) -> p (b t) n", n=P)).then_inc(m.xc, 1)

                copy_xT(0, 1)
                for it in peeled(dve, pairs):
                    for s in range(2):
                        after(dve, m.sg, it * 2 + (s + 1))
                        after(dve, m.up, it * 2 + (s + 1))
                        dve.tensor_tensor(ex_h[:, s, :], ps[:, 1, 0:F], ex_g[:, s, :], MUL).then_inc(m.hm, 1)
                        copy_xT(1 - s, it * 2 + (s + 2))
                if i == 0:
                    dve.wait_ge(s_modm, 32)
                between(FAST, f"moe{i}", n_mix[1] if i == 0 else None, lambda j: macc[:, j, :], modb[:, 5, :], mubuf[:, 0, :],
                        0, cubuf, None)

            moe(0, "ret")

            dve.wait_ge(s_ntp, n_mix[1].tile + NT)
            st.done(dve.memset(zin[:, :, 0:HALO], 0.0))
            st.done(dve.memset(zin[:, :, HALO + SEQ:2 * HALO + SEQ], 0.0))
            dve.wait_ge(s_ccol, 1)
            for cc in range(KT):
                dve.wait_ge(s_csg, cc + 1)
                dve.scalar_tensor_tensor(zin[:, cc, HALO:HALO + SEQ], ps[:, 2 * (cc % 2), :], chp[:, cc, 34:35], sgate[:, cc % 2, :], ADD, MUL)\
                    .then_inc(s_zin, 1)
            dve.wait_ge(s_zin, KT)
            after(dve, s_dve, st.n)
            base = st.n
            per = 2 * TAPS - 2
            for pr in peeled(dve, KT // 2):
                st.n = pr * per + base
                for k in range(TAPS):
                    for u in range(2):
                        z_ = zin[:, ds(pr * 2 + u, 1), k:k + SEQ].rearrange("p o n -> p (o n)")
                        a_ = cacc[:, ds(pr * 2 + u, 1), :].rearrange("p o n -> p (o n)")
                        w_ = chp[:, ds(pr * 2 + u, 1), k:k + 1].rearrange("p o n -> p (o n)")
                        if k == 0:
                            b_ = chp[:, ds(pr * 2 + u, 1), TAPS:TAPS + 1].rearrange("p o n -> p (o n)")
                            ins = dve.tensor_scalar(a_, z_, w_, b_, MUL, ADD)
                        else:
                            after(dve, s_dve, st.n - (0 if k == TAPS - 1 and u else 1))
                            ins = dve.scalar_tensor_tensor(a_, z_, w_, a_, MUL, ADD)
                        if k < TAPS - 1:
                            st.done(ins)
                        else:
                            ins.then_inc(s_tap, 1)
            st.n = base + KT // 2 * per
            mod_finish(3)
            dve.wait_ge(s_lmuc, 1)
            for cc in range(KT):
                dve.tensor_tensor(cacc[:, cc, :], cacc[:, cc, :], mu, SUB).then_inc(s_lcen, 1)
            dve.wait_ge(s_lsd, 1)
            st.then(dve.reciprocal(lrs, lrs))
            for cc in range(KT):
                dve.wait_ge(s_lcen, KT)
                dve.wait_ge(s_lsq, cc + 1)
                dve.tensor_tensor(cacc[:, cc, :], cacc[:, cc, :], lrs, MUL).then_inc(s_lnx, 1)
            dve.wait_ge(s_cb2, 16)
            dve.wait_ge(s_modf, 32)

            def conv_y(j):
                dve.wait_ge(s_cy, j + 1)
                dve.tensor_tensor(ybuf[:, j, :], ps[:, 2 * j:2 * j + 2, :].rearrange("p b n -> p (b n)"), b2row, ADD).then_inc(s_y, 1)
                dve.wait_ge(s_y, NT + j + 1)
                return ybuf[:, j, :]

            between(SLOW, "conv", n_moe[1], conv_y, modb[:, 2, :], chrow, 3, cmubuf, 48)
            moe(1, "conv")


_INS = ['x', 'c', 'ctx', 'c_ctx', 'mod_w', 'mod_b', 'norms', 'ret_w_in', 'ret_w_out', 'ret_decay',
        'conv_w1', 'conv_b1', 'conv_dw', 'conv_b_dw', 'conv_ln_g', 'conv_ln_b', 'conv_w2', 'conv_b2',
        'moe_router', 'moe_bias', 'moe_w1', 'moe_w3', 'moe_w2', 'shared_w1', 'shared_w3', 'shared_w2']


def kernel(**inputs):
    import concourse.bacc as bacc
    from concourse.bass_utils import run_bass_kernel_spmd

    nc = bacc.Bacc("TRN2", target_bir_lowering=False, num_devices=1)
    arrays = {f"in_{n}": np.ascontiguousarray(inputs[n]) for n in _INS}
    arrays["in_consts"] = shape_constants()
    args = [nc.dram_tensor(n, a.shape, F32, kind="ExternalInput").ap() for n, a in arrays.items()]
    out = nc.dram_tensor("out", (1, SEQ, D), F32, kind="ExternalOutput").ap()
    build(nc, *args, out)
    return run_bass_kernel_spmd(nc, [arrays], core_ids=[0]).results[0]["out"]
```

```python
from contextlib import ExitStack

import numpy as np

import concourse.bass as bass
from concourse import mybir

ALU = mybir.AluOpType
ACT = mybir.ActivationFunctionType
AX = mybir.AxisListType
F32 = mybir.dt.float32
I32 = mybir.dt.int32
ds = bass.ds

P = 128
D = 1024
KT = D // P
SEQ = 512
CTX = 256
NT = SEQ // P
HEADS = 4
DK = D // HEADS
DV = 2 * DK
KEYT = (SEQ + CTX) // P
W = 512
MODW = 6 * D
TAPS = 31
HALO = TAPS // 2
NE = 64
TOPK = 8
NG = 8
PER = NE // NG
F = 256
FT = F // P
ROUTE_SCALE = 2.5
SMALL = 5 * P // 8
PAIRS = 50
BLOCKS = 2 * PAIRS + 2
BIG = 16384.0
MARK = 3.0e38
LOW = -1.0e30
BAND = 640 + SEQ + CTX

C_ID = 0
C_TRI = C_ID + P
C_ONE = C_TRI + P
C_IOTA = C_ONE + P
C_POS = C_IOTA + P
C_COS = C_POS + BAND
C_SIN = C_COS + SEQ + CTX
C_TOK = C_SIN + SEQ + CTX
C_THR = C_TOK + NT
C_EPS = C_THR + NT
C_DUMP = C_EPS + 2
C_SKIP = C_DUMP + 1
C_ONEPLUS = C_SKIP + 1
C_ALL = C_ONEPLUS + 4

MOD_PARTS = [(0, 0, 3, 1, (None, 0, 1)), (0, 3, 3, 1, (None, 2, 3)), (1, 0, 2, 1, (None, 0)), (1, 2, 4, 2, (1, None, 2, 3))]
DB = D // P


def shape_constants():
    c = np.zeros((P, C_ALL), np.float32)
    r = np.arange(P)
    c[:, C_ID:C_ID + P] = np.eye(P)
    c[:, C_TRI:C_TRI + P] = r[:, None] < r[None, :]
    c[:, C_ONE:C_ONE + P] = 1.0
    c[:, C_IOTA:C_IOTA + P] = r[None, :]
    c[:, C_POS:C_POS + BAND] = np.arange(BAND)[None, :] - 640 - r[:, None]
    at = np.arange(SEQ)
    lat = np.stack([np.full(SEQ, CTX), at // 64, at % 64], -1)
    ctx = np.stack([np.arange(CTX), np.zeros(CTX), np.zeros(CTX)], -1)
    pos = np.concatenate([lat, ctx]).astype(np.float32)
    ang = []
    for a, d in enumerate((64, 96, 96)):
        inv = (10000.0 ** (-np.arange(0, d, 2, dtype=np.float32) / np.float32(d))).astype(np.float32)
        ang.append(pos[:, a:a + 1] * inv[None, :])
    ang = np.concatenate(ang, -1).astype(np.float64).T
    c[:, C_COS:C_COS + SEQ + CTX] = np.cos(ang)
    c[:, C_SIN:C_SIN + SEQ + CTX] = np.sin(ang)
    c[:, C_TOK:C_TOK + NT] = 1 + r[:, None] + P * np.arange(NT)[None, :]
    c[:, C_THR:C_THR + NT] = P * np.arange(NT)[None, :]
    c[:, C_EPS] = 1e-6
    c[:, C_EPS + 1] = 1e-5
    c[:, C_DUMP] = SEQ + 1 + r
    c[:, C_SKIP] = np.where(r == 0, 1, SEQ + 1 + r)
    for part, (_, _, _, scale, _) in enumerate(MOD_PARTS):
        c[:, C_ONEPLUS + part] = r // DB == scale
    return c


class Steps:

    def __init__(self, eng, sem):
        self.eng, self.sem, self.n = eng, sem, 0

    def done(self, ins):
        ins.then_inc(self.sem, 1)
        self.n = self.n + 1
        return self.n

    def then(self, ins):
        self.eng.wait_ge(self.sem, self.done(ins))


def peeled(eng, n, last=False):
    yield 0
    with eng.Fori(1, n) as i:
        yield i
    if last:
        yield n


def turns(eng, split, split_1, end_1):
    for i in peeled(eng, split):
        yield i, P, (i * 2 - 1, i * 2)
    with eng.Fori(split_1, end_1) as i:
        yield i + 1, SMALL, (i * 2 + 1, i * 2 + 2)


def after(eng, sem, n):
    if not isinstance(n, int) or n > 0:
        eng.wait_ge(sem, n)


def build(nc, x, c, ctx, c_ctx, mod_w, mod_b, norms, ret_w_in, ret_w_out, ret_decay,
          conv_w1, conv_b1, conv_dw, conv_b_dw, conv_ln_g, conv_ln_b, conv_w2, conv_b2,
          moe_router, moe_bias, moe_w1, moe_w3, moe_w2, shared_w1, shared_w3, shared_w2,
          consts, out):
    with ExitStack() as stack:
        def sem(name):
            return stack.enter_context(nc.semaphore(name))

        def sb(name, cols, dt=F32):
            return stack.enter_context(nc.sbuf_tensor(name, [P, cols], dt))

        mod_raw = nc.dram_tensor("mod_raw", [2, 2, MODW], F32, kind="Internal").ap()
        mod_rows = nc.dram_tensor("mod_rows", [2, 2, MODW], F32, kind="Internal").ap()
        u_rows = [nc.dram_tensor(f"u_rows{i}", [SEQ, D], F32, kind="Internal").ap() for i in range(2)]
        sum_rows = nc.dram_tensor("sum_rows", [SEQ + P, D], F32, kind="Internal").ap()

        cst = sb("cst", C_ALL)
        h = sb("h", NT * D)[:, :].rearrange("p (j d) -> p j d", j=NT)
        modb = sb("modb", MODW)[:, :].rearrange("p (r d) -> p r d", r=6)
        uT = sb("uT", KT * SEQ)[:, :].rearrange("p (t n) -> p t n", t=KT)
        ring_all = sb("ring", 4 * KT * W)
        ring = [ring_all[:, s * KT * W:(s + 1) * KT * W] for s in range(4)]
        col = sb("col", 160)
        arena_cols = 18700
        arena = sb("arena", arena_cols)
        ps = stack.enter_context(nc.psum_tensor("ps", [P, 8, W], F32))

        ident = cst[:, C_ID:C_ID + P]
        ones = cst[:, C_ONE:C_ONE + P]
        cos = cst[:, C_COS:C_COS + SEQ + CTX]
        sin = cst[:, C_SIN:C_SIN + SEQ + CTX]
        eps_norm = cst[:, C_EPS:C_EPS + 1]
        eps_ln = cst[:, C_EPS + 1:C_EPS + 2]

        ss = col[:, 0:8]
        sd = col[:, 8:16]
        rs = col[:, 16:24]
        dec = col[:, 24:32]
        dec_t = [col[:, 32 + 8 * i:40 + 8 * i] for i in range(6)]
        lgf = col[:, 80:84]
        nlgb = col[:, 84:88]
        y_ss = col[:, 128:132]
        y_sd = col[:, 132:136]
        y_rs = col[:, 136:140]
        c_raw = col[:, 96:112].rearrange("p (r t) -> p r t", r=2)
        c_act = col[:, 112:128].rearrange("p (t r) -> p t r", r=2)

        def view(off, n):
            assert off + n <= arena_cols
            return arena[:, off:off + n]

        yT = view(0, 8192).rearrange("p (c n) -> p c n", c=4 * HEADS)
        ctx_x = view(0, 2048).rearrange("p (j d) -> p j d", j=2)
        cmod = view(2048, 2048).rearrange("p (r d) -> p r d", r=2)
        uTc = view(8192, 2048).rearrange("p (t n) -> p t n", t=KT)
        qT = view(10240, 1024).rearrange("p (e n) -> p e n", e=2)
        kT = view(11264, 1536).rearrange("p (e n) -> p e n", e=2)
        osq = view(10240, 2048).rearrange("p (c n) -> p c n", c=4)
        sgT = view(12800, 2048).rearrange("p (c n) -> p c n", c=4)
        ST = view(14848, 3072).rearrange("p (m n) -> p m n", m=KEYT)
        rot = view(14848, 2048).rearrange("p (i n) -> p i n", i=4)
        orstd = view(17920, 512)
        ubuf = view(14848, 2048).rearrange("p (s d) -> p s d", s=2)
        junk = view(16896, 1024)
        band = modb[:, 0:2, :].rearrange("p r d -> p (r d)")[:, 0:BAND]
        otmp = modb[:, 0:2, :].rearrange("p r d -> p (r d)")[:, BAND:BAND + SEQ]
        V = ring[3][:, 0:KEYT * W].rearrange("p (m n) -> p m n", m=KEYT)
        dctx = ring[3][:, KEYT * W:KT * W].rearrange("p (m n) -> p m n", m=2)

        class ModBuffers:

            def __init__(self, at, blocks, conds, products):
                self.bias, self.norm = view(at, P)[0:blocks], view(at + P, P)[0:blocks]
                self.rows = view(at + 2 * P, conds * P).rearrange("p (r n) -> p r n", r=conds)[0:blocks]
                self.blocks, self.conds, self.products = blocks, conds, products[0:conds, 0:blocks * P]

        mod_part = [ModBuffers(12800, 24, 2, ring[3]), ModBuffers(13312, 24, 1, view(4096, 3072)),
                    ModBuffers(5312, 16, 1, view(0, 2048)),
                    ModBuffers(17952, 32, 1, view(13856, 4096))]

        zin = view(0, KT * (SEQ + 2 * HALO)).rearrange("p (c n) -> p c n", c=KT)
        cacc = view(4352, 4096).rearrange("p (c n) -> p c n", c=KT)
        sgate = view(8448, 1024).rearrange("p (s n) -> p s n", s=2)
        chp = view(9472, 8 * 36).rearrange("p (c k) -> p c k", c=KT)
        chrow = view(9760, 1024)
        b2row = view(10784, 1024)
        mu = view(11808, 512)
        lrs = view(12320, 512)
        lsq = view(12832, 1024).rearrange("p (s n) -> p s n", s=2)
        ybuf = view(13856, 4096).rearrange("p (j d) -> p j d", j=NT)
        cubuf = view(0, 2048).rearrange("p (s d) -> p s d", s=2)
        cjunk = view(2048, 1024)
        cmubuf = view(4352, 2048).rearrange("p (s d) -> p s d", s=2)

        xg = view(0, 2048).rearrange("p (s d) -> p s d", s=2)
        xT = view(2048, 2048).rearrange("p (s t n) -> p s t n", s=2, t=KT)
        oh_r = view(0, 2048).rearrange("p (s k r) -> p s k r", s=2, k=TOPK)
        oh_b = view(2048, 4 * TOPK * BLOCKS).rearrange("p (s k w b) -> p s k w b", s=2, k=TOPK, w=2)
        yb = view(4096, 2048).rearrange("p (s d) -> p s d", s=2)
        macc = view(6144, 4096).rearrange("p (j d) -> p j d", j=NT)
        mubuf = view(10240, 2048).rearrange("p (s d) -> p s d", s=2)
        hsT = view(12288, 1024).rearrange("p (f n) -> p f n", f=FT)
        sgs = view(13312, 1024).rearrange("p (f n) -> p f n", f=FT)
        ex_g = view(10240, 512).rearrange("p (s n) -> p s n", s=2)
        ex_hT = view(11264, 512).rearrange("p (s f n) -> p s f n", s=2, f=FT)
        idx_col = view(11776, 4).bitcast(I32)
        mjunk = view(13312, 1024)
        at = 14336

        def small(n):
            nonlocal at
            at += n
            return view(at - n, n)

        wr = [view(at_, KT * NE).rearrange("p (t e) -> p t e", t=KT) for at_ in (12288, 6400)]
        score = small(256).rearrange("p (j e) -> p j e", j=NT)
        bias = small(64)
        biased = small(256).rearrange("p (j e) -> p j e", j=NT)
        gtop = small(256).rearrange("p (j g k) -> p j g k", j=NT, g=NG)
        gsx = small(48).rearrange("p (j k) -> p j k", j=NT)
        gmax = small(32).rearrange("p (j k) -> p j k", j=NT)
        grep = small(32).rearrange("p (j k) -> p j k", j=NT)
        gout = small(48).rearrange("p (j k) -> p j k", j=NT)
        gmask = small(32).rearrange("p (j g) -> p j g", j=NT)
        gneg = small(32).rearrange("p (j g) -> p j g", j=NT)
        top8 = small(32).rearrange("p (j k) -> p j k", j=NT)
        rep = small(256).rearrange("p (j e) -> p j e", j=NT)
        sel = small(256).rearrange("p (j e) -> p j e", j=NT)
        wn = small(256).rearrange("p (j e) -> p j e", j=NT)
        wsum = small(8)
        slotk = small(256).rearrange("p (j e) -> p j e", j=NT)
        topslot = small(32).rearrange("p (j k) -> p j k", j=NT)
        slot_i = small(32).bitcast(I32)
        slot_ri = small(32).bitcast(I32)
        slot_bi = small(32).bitcast(I32)
        slot_r = small(32).rearrange("p (j k) -> p j k", j=NT)
        slot_b = small(32).rearrange("p (j k) -> p j k", j=NT)
        eq = small(512).rearrange("p (k e) -> p k e", k=TOPK)
        wk = small(32).rearrange("p (j k) -> p j k", j=NT)
        cnt = small(12)
        nblk_b = small(P)
        started = small(P)
        begun = small(P)
        key_diag = small(NE)
        precedes = small(NE)
        upto = small(NE)
        ctrl = small(BLOCKS + 4).bitcast(I32)
        is_pad = small(BLOCKS)
        tok_idx = small(BLOCKS).bitcast(I32)
        sum_idx = small(BLOCKS).bitcast(I32)
        wslot = small(BLOCKS)
        zero = small(P)

        moe_u = (mubuf, cmubuf)

        def expert(s):
            w = ring_all[:, s * 6144:(s + 1) * 6144]
            return (w[:, 0:2048].rearrange("p (t f) -> p t f", t=KT), w[:, 2048:4096].rearrange("p (t f) -> p t f", t=KT),
                    w[:, 4096:6144].rearrange("p (f d) -> p f d", f=FT))

        s_const, s_c, s_x, s_ctx, s_decay = (sem(n) for n in ("const_in", "c_in", "x_in", "ctx_in", "decay_in"))
        s_cact = sem("c_silu")
        s_mw = [sem(f"mod_panel_in{s}") for s in range(3)]
        s_mwh = [sem(f"mod_half_panel_in{s}") for s in range(5)]
        s_mbias = [sem(f"mod_bias_norms_in{s}") for s in range(2)]
        s_mps, s_mcp, s_mraw, s_mback, s_mrow, s_mout = (sem(n) for n in ("mod_product", "mod_copied", "mod_products_stored", "mod_blocks_in",
                                                                          "mod_rows", "mod_stored"))
        s_modm, s_modf, s_cmod = sem("mod_mixer_in"), sem("mod_ffn_in"), sem("ctx_mod_in")
        s_dve, s_act, s_pool = sem("dve_steps"), sem("act_steps"), sem("pool_steps")
        s_log = sem("decay_exp")

        s_nrms, s_nu, s_ntp, s_ncp = (sem(n) for n in ("norm_rms", "norm_u", "norm_turned", "norm_uT"))

        class Norm:
            def __init__(self, tile):
                self.tile = tile

        n_ctx, n_mix, n_moe = Norm(0), [Norm(2), Norm(10)], [Norm(6), Norm(14)]
        s_y, s_yrms, s_h = sem("mixer_y"), sem("y_rms"), sem("h_added")
        SLOW = (("y", 0), ("n", 0), ("y", 1), ("n", 1), ("t", 0), ("y", 2), ("n", 2), ("t", 1), ("y", 3), ("n", 3), ("t", 2), ("t", 3))
        FAST = (("y", 0), ("y", 1), ("n", 0), ("y", 2), ("n", 1), ("t", 0), ("y", 3), ("n", 2), ("t", 1), ("n", 3), ("t", 2), ("t", 3))
        h_base = {"ret": 0, "moe0": 2 * NT, "conv": 4 * NT, "moe1": 6 * NT}

        s_wqk, s_wv, s_wg = sem("qk_panel_in"), sem("v_panel_in"), sem("g_panel_in")
        s_q, s_k, s_kc = sem("q_product"), sem("k_product"), sem("kctx_product")
        s_qkr = sem("qk_rotated")
        s_v, s_vc = sem("v_product"), sem("v_copied")
        s_g, s_gc = sem("g_product"), sem("g_silu")
        s_band, s_bexp = sem("band_exponent"), sem("band_exp")
        s_s, s_sc = sem("scores"), sem("scores_decayed")
        s_o, s_osq, s_oss, s_ord, s_yT = (sem(n) for n in ("o_product", "o_squared", "o_sumsq", "o_rms", "yT_head"))
        s_wo = [sem(f"w_out_in{s}") for s in range(4)]

        s_cw1 = [sem(f"conv_w1_in{s}") for s in range(4)]
        s_crow, s_ccolp, s_ccol = sem("conv_rows_in"), sem("conv_cols_product"), sem("conv_cols")
        s_cag, s_csg, s_zin = sem("conv_glu_product"), sem("conv_gate"), sem("conv_glu")
        s_tap, s_lmu, s_lmuc, s_lcen = sem("conv_taps"), sem("ln_sum"), sem("ln_mean"), sem("ln_centred")
        s_lsq, s_lvar, s_lsd, s_lnx, s_lnu = (sem(n) for n in ("ln_squared", "ln_sumsq", "ln_std", "ln_scaled", "conv_act"))
        s_cw2 = [sem(f"conv_w2_in{s}") for s in range(2)]
        s_cb2 = sem("conv_b2_in")
        s_cy = sem("conv_w2_product")

        class MoeFixed:

            def __init__(self, t):
                self.wr, self.bias = sem(t + "router_in"), sem(t + "bias_in")
                self.urow = [sem(t + f"u_stored{s}") for s in range(2)]
                self.logit, self.score = sem(t + "logits"), sem(t + "scores")
                self.sel, self.cnt, self.nblk = sem(t + "selected"), sem(t + "counts"), sem(t + "blocks")
                self.pos, self.started, self.blk = sem(t + "slots"), sem(t + "started"), sem(t + "block_experts")
                self.ctrl = sem(t + "control")
                self.zero, self.zeroed = sem(t + "zero"), sem(t + "spare_rows_zeroed")
                self.oh, self.list, self.tok = sem(t + "one_hots"), sem(t + "lists"), sem(t + "token_index")
                self.init = sem(t + "sums_started")
                self.sums = [sem(t + f"sums_in{j}") for j in range(NT)]
                self.sw = sem(t + "shared_in")
                self.sup, self.ssg, self.sh = sem(t + "shared_up"), sem(t + "shared_silu"), sem(t + "shared_h")
                self.sy, self.sacc = sem(t + "shared_y"), sem(t + "shared_sum")
                self.tail = sem(t + "blocks_done")

        class MoeLoop:

            def __init__(self, t):
                self.w1 = [sem(t + f"w1_in{s}") for s in range(2)]
                self.w3 = [sem(t + f"w3_in{s}") for s in range(2)]
                self.w2 = [sem(t + f"w2_in{s}") for s in range(2)]
                self.idx = sem(t + "index")
                self.xg = [sem(t + f"x_gathered{s}") for s in range(2)]
                self.xt = sem(t + "x_turned")
                self.xc = sem(t + "xT")
                self.g1 = sem(t + "gate_product")
                self.up = sem(t + "up_product")
                self.sg = sem(t + "gate_silu")
                self.hm = sem(t + "expert_h")
                self.y = sem(t + "expert_y")
                self.yc = sem(t + "expert_y_copied")
                self.yo = sem(t + "expert_y_added")

        mf = MoeFixed("moe_")
        mo = [MoeLoop(f"moe{i}_") for i in range(2)]
        s_out = sem("out_stored")

        win = ret_w_in[0].rearrange("(p t) n -> p t n", t=KT)
        wqk = ring[0].rearrange("p (t n) -> p t n", t=KT)
        wv = ring[1].rearrange("p (t n) -> p t n", t=KT)
        wg = ring[2].rearrange("p (t n) -> p t n", t=KT)
        wo = [r.rearrange("p (c n) -> p c n", c=4) for r in ring]
        wo_dram = ret_w_out[0].rearrange("(h c p) n -> h p c n", h=HEADS, p=P)
        panel = [r.rearrange("p (t n) -> p t n", t=KT) for r in ring]
        half_panel = [ring_all[:, s * KT * F:(s + 1) * KT * F].rearrange("p (t n) -> p t n", t=KT) for s in (6, 7, 0, 1, 2)]

        def load_mod_rows(q, part):
            layer, first, _, _, norm_of = MOD_PARTS[part]
            b = mod_part[part]
            cols = slice(first * D, (first + len(norm_of)) * D)
            q.dma_start(b.bias, mod_b[layer, cols].rearrange("(b n) -> b n", n=P)).then_inc(s_mbias[part % 2], 16)
            for row, w in enumerate(norm_of):
                src = consts[0:DB, C_ONE:C_ONE + P] if w is None else norms[layer, w].rearrange("(b n) -> b n", n=P)
                q.dma_start(b.norm[row * DB:(row + 1) * DB, :], src).then_inc(s_mbias[part % 2], 16)

        mod_in = [64, 64, 64 + 48, 64 + 80]
        mod_copied = [6, 12, 16, 24]
        mod_conds = [2, 3, 4, 5]
        mod_w_p = [mod_w[i].rearrange("(p t) n -> p t n", t=KT) for i in range(2)]

        block = stack.enter_context(nc.Block())

        @block.sync
        def _(sp):
            sp.dma_start(c_raw[:, 0, :], c[0].rearrange("(p t) -> p t", t=KT)).then_inc(s_c, 16)
            sp.dma_start(c_raw[:, 1, :], c_ctx.rearrange("(p t) -> p t", t=KT)).then_inc(s_c, 16)

            def mod_panel(n):
                if n >= 3:
                    sp.wait_ge(s_mps, n - 2)
                sp.dma_start(panel[n % 3], mod_w_p[0][:, :, n * W:(n + 1) * W]).then_inc(s_mw[n % 3], 16)

            for n in range(4):
                mod_panel(n)
            sp.dma_start(cst[:, :], consts).then_inc(s_const, 16)
            for part in range(2):
                load_mod_rows(sp, part)
            mod_panel(4)
            mod_panel(5)
            sp.dma_start(ctx_x, ctx[0].rearrange("(j p) d -> p j d", p=P)).then_inc(s_ctx, 16)
            sp.dma_start(dec, ret_decay[0].rearrange("a h -> (a h)").partition_broadcast(P)).then_inc(s_decay, 16)
            mod_panel(6)
            mod_panel(7)
            sp.wait_ge(s_mraw, 16)
            mod_panel(8)
            sp.wait_ge(s_mback, 16)
            sp.dma_start(h, x[0].rearrange("(j p) d -> p j d", p=P)).then_inc(s_x, 16)
            mod_panel(9)
            sp.wait_ge(s_mout, 16)
            sp.dma_start(cmod.rearrange("p r d -> p (r d)"), mod_rows[0, 1, 0:2 * D].partition_broadcast(P)).then_inc(s_cmod, 16)
            sp.dma_start(modb[:, 0:3, :].rearrange("p r d -> p (r d)"), mod_rows[0, 0, 0:3 * D].partition_broadcast(P)).then_inc(s_modm, 16)
            mod_panel(10)
            mod_panel(11)

            sp.wait_ge(s_mps, 10)
            for hd in peeled(sp, HEADS):
                after(sp, s_kc, hd)
                sp.dma_start(wqk[:, :, 0:DK], win[:, :, ds(hd * DK, DK)]).then_inc(s_wqk, 16)
                sp.dma_start(wqk[:, :, DK:2 * DK], win[:, :, ds(hd * DK + D, DK)]).then_inc(s_wqk, 16)
                if isinstance(hd, int):
                    sp.wait_ge(s_mps, 12)
                after(sp, s_v, hd * KEYT)
                sp.dma_start(wv, win[:, :, ds(hd * DV + 2 * D, DV)]).then_inc(s_wv, 16)
                after(sp, s_g, hd * 4)
                sp.dma_start(wg, win[:, :, ds(hd * DV + 4 * D, DV)]).then_inc(s_wg, 16)
            sp.wait_ge(s_mout, 32)
            sp.dma_start(modb[:, 3:6, :].rearrange("p r d -> p (r d)"), mod_rows[0, 0, 3 * D:6 * D].partition_broadcast(P)).then_inc(s_modf, 16)
            sp.wait_ge(s_kc, HEADS)
            sp.dma_start(wo[0], wo_dram[0]).then_inc(s_wo[0], 16)
            sp.wait_ge(s_v, HEADS * KEYT)
            sp.dma_start(wo[1], wo_dram[1]).then_inc(s_wo[1], 16)
            sp.wait_ge(s_g, HEADS * 4)
            sp.dma_start(wo[2], wo_dram[2]).then_inc(s_wo[2], 16)
            sp.wait_ge(s_o, HEADS * 4)
            sp.dma_start(wo[3], wo_dram[3]).then_inc(s_wo[3], 16)

            def load_router(i):
                sp.dma_start(wr[i], moe_router[i].rearrange("(p t) e -> p t e", t=KT)).then_inc(mf.wr, 16)

            load_router(0)

            def moe(i, mixer):
                m = mo[i]
                w1, w3, w2 = expert(1)

                def store_tokens(j):
                    sp.wait_ge(s_nu, n_moe[i].tile + j + 1)
                    sp.dma_start(u_rows[i][j * P:(j + 1) * P, :], moe_u[i][:, j % 2, :]).then_inc(mf.urow[j % 2], 16)

                for j in range(NT - 1):
                    store_tokens(j)
                sp.wait_ge(s_y if i == 0 else s_cy, NT)
                sp.dma_start(w1, shared_w1[i].rearrange("(p t) f -> p t f", t=KT)).then_inc(mf.sw, 16)
                sp.dma_start(w3, shared_w3[i].rearrange("(p t) f -> p t f", t=KT)).then_inc(mf.sw, 16)
                sp.dma_start(w2, shared_w2[i].rearrange("(p f) d -> p f d", f=FT)).then_inc(mf.sw, 16)
                store_tokens(NT - 1)
                sp.wait_ge(s_h, h_base[mixer] + 2 * NT)
                sp.dma_start(bias, moe_bias[i].partition_broadcast(P)).then_inc(mf.bias, 16)
                if i == 0:
                    load_mod_rows(sp, 2)
                if i == 0:
                    sp.wait_ge(mf.zero, 1)
                    sp.dma_start(sum_rows[SEQ:SEQ + P, :].rearrange("p (r z) -> p r z", z=P), zero.unsqueeze(1).to_broadcast([P, D // P, P]))\
                        .then_inc(mf.zeroed, 16)
                sp.wait_ge(mf.ctrl, i + 1)
                pairs = sp.value_load(ctrl[0:1, BLOCKS:BLOCKS + 1], min_val=1, max_val=PAIRS)

                def load(s, b):
                    e = sp.value_load(ctrl[0:1, ds(b, 1)] if not isinstance(b, int) else ctrl[0:1, b:b + 1], min_val=0, max_val=NE - 1)
                    w1, w3, w2 = expert(s)
                    sp.dma_start(w1, moe_w1[i].rearrange("e (p t) f -> p e (t f)", t=KT)[:, ds(e, 1), :].rearrange("p e (t f) -> p (e t) f", t=KT)).then_inc(m.w1[s], 16)
                    sp.dma_start(w3, moe_w3[i].rearrange("e (p t) f -> p e (t f)", t=KT)[:, ds(e, 1), :].rearrange("p e (t f) -> p (e t) f", t=KT)).then_inc(m.w3[s], 16)
                    return w2, e

                def load2(s, w2, e):
                    sp.dma_start(w2, moe_w2[i].rearrange("e (p f) d -> p e (f d)", f=FT)[:, ds(e, 1), :].rearrange("p e (f d) -> p (e f) d", f=FT)).then_inc(m.w2[s], 16)

                if i == 0:
                    sp.wait_ge(s_mps, 20)
                load2(0, *load(0, 0))
                for j in range(NT):
                    sp.wait_ge(mf.sacc, i * NT + j + 1)
                    sp.dma_start(sum_rows[j * P:(j + 1) * P, :], macc[:, j, :]).then_inc(mf.init, 16)
                if i == 0:
                    sp.wait_ge(s_mout, 48)
                    sp.dma_start(modb[:, 0:2, :].rearrange("p r d -> p (r d)"), mod_rows[1, 0, 0:2 * D].partition_broadcast(P))\
                        .then_inc(s_modm, 16)
                sp.wait_ge(mf.sy, i * 2 * NT + 2 * NT)
                load2(1, *load(1, 1))
                with sp.Fori(1, pairs) as it:
                    for s in range(2):
                        after(sp, m.up, it * 2 + (s - 1))
                        w2, e = load(s, it * 2 + s)
                        after(sp, m.y, it * 2 + (s - 1))
                        load2(s, w2, e)
                sp.wait_ge(mf.tail, i + 1)
                for j in range(NT):
                    sp.dma_start(macc[:, j, :], sum_rows[j * P:(j + 1) * P, :]).then_inc(mf.sums[j], 16)

            moe(0, "ret")

            cw1 = conv_w1[0].rearrange("(p t) n -> p t n", t=KT)
            for s in (0, 2):
                sp.dma_start(panel[s], cw1[:, :, s * W:(s + 1) * W]).then_inc(s_cw1[s], 16)
            sp.wait_ge(s_h, h_base["moe0"] + 2 * NT)
            for r, a in enumerate([conv_dw[0], conv_b_dw, conv_ln_g, conv_ln_b, conv_b1[0:1, 0:D], conv_b1[0:1, D:2 * D]]):
                r0 = 0 if r == 0 else TAPS - 1 + r
                n = TAPS if r == 0 else 1
                sp.dma_start(chrow[r0:r0 + n, :], a).then_inc(s_crow, 16)
            sp.dma_start(b2row, conv_b2[0].partition_broadcast(P)).then_inc(s_cb2, 16)
            for s in (1, 3):
                sp.dma_start(panel[s], cw1[:, :, s * W:(s + 1) * W]).then_inc(s_cw1[s], 16)
            load_mod_rows(sp, 3)
            sp.wait_ge(s_cag, 4)
            for n in range(8):
                if n >= 2:
                    sp.wait_ge(s_mps, 20 + n - 1)
                sp.dma_start(panel[2 * (n % 2)], mod_w_p[1][:, :, 2 * D + n * W:2 * D + (n + 1) * W]).then_inc(s_mw[n % 2], 16)
            cw2 = conv_w2[0].rearrange("(c p) n -> p c n", p=P)
            sp.wait_ge(s_cag, KT)
            for s in range(2):
                sp.dma_start(panel[1 + 2 * s], cw2[:, :, s * W:(s + 1) * W]).then_inc(s_cw2[s], 16)
            sp.wait_ge(s_lnu, KT)
            load_router(1)
            sp.wait_ge(s_mout, 64)
            sp.dma_start(modb[:, 2:6, :].rearrange("p r d -> p (r d)"), mod_rows[1, 0, 2 * D:6 * D].partition_broadcast(P)).then_inc(s_modf, 16)
            moe(1, "conv")
            for j in range(NT):
                sp.wait_ge(s_h, h_base["moe1"] + 2 * (j + 1))
                sp.dma_start(out[0, j * P:(j + 1) * P, :], h[:, j, :]).then_inc(s_out, 16)
            sp.wait_ge(s_out, 16 * NT)

        @block.gpsimd
        def _(pool):
            def mod_store(part):
                layer, first, _, _, norm_of = MOD_PARTS[part]
                cols = slice(first * D, (first + len(norm_of)) * D)
                b = mod_part[part]
                pool.wait_ge(s_mcp, mod_copied[part])
                pool.dma_start(mod_raw[layer, 0:b.conds, cols], b.products).then_inc(s_mraw, 16)
                pool.wait_ge(s_mraw, 16 * (part + 1))
                pool.dma_start(b.rows, mod_raw[layer, 0:b.conds, cols].rearrange("c (b n) -> b c n", n=P)).then_inc(s_mback, 16)
                pool.wait_ge(s_mrow, mod_conds[part])
                pool.dma_start(mod_rows[layer, 0:b.conds, cols].rearrange("c (b n) -> b c n", n=P), b.rows).then_inc(s_mout, 16)

            mod_store(0)
            mod_store(1)
            pool.wait_ge(s_y, NT)
            for n in range(8):
                if n >= 5:
                    pool.wait_ge(s_mps, 12 + n - 4)
                pool.dma_start(half_panel[n % 5], mod_w_p[1][:, :, n * F:(n + 1) * F]).then_inc(s_mwh[n % 5], 16)

            def moe(i, mixer):
                m = mo[i]
                pool.wait_ge(s_h, h_base[mixer] + 2 * NT)
                if i == 0:
                    pool.memset(zero, 0.0).then_inc(mf.zero, 1)
                    mod_store(2)
                pool.wait_ge(mf.tok, i + 1)
                for s in range(2):
                    pool.wait_ge(mf.urow[s], i * 32 + 32)
                pool.wait_ge(mf.ctrl, i + 1)
                pairs = pool.value_load(ctrl[0:1, BLOCKS:BLOCKS + 1], min_val=1, max_val=PAIRS)
                before = pool.value_load(ctrl[0:1, BLOCKS + 1:BLOCKS + 2], min_val=0, max_val=PAIRS - 1)
                split = pool.value_load(ctrl[0:1, BLOCKS + 2:BLOCKS + 3], min_val=2, max_val=PAIRS - 1)
                split_1 = pool.value_load(ctrl[0:1, BLOCKS + 3:BLOCKS + 4], min_val=1, max_val=PAIRS - 2)

                def column(at, table, b, n):
                    colb = table[:, b:b + 1] if isinstance(b, int) else table[:, ds(b, 1)]
                    pool.tensor_copy(idx_col[:, at:at + 1], colb).then_inc(m.idx, 1)
                    pool.wait_ge(m.idx, n)
                    pool.sem_inc(s_pool, 1)

                def gather(s, b, n, rows=P):
                    column(s, tok_idx, b, n)
                    pool.indirect_dma_start(xg[0:rows, s, :], None, u_rows[i], bass.IndirectOffsetOnAxis(ap=idx_col[0:rows, s:s + 1], axis=0),
                                            bounds_check=SEQ - 1, oob_is_err=False)\
                        .then_inc(m.xg[s], 16)

                def add(s, b, n, rows=P):
                    column(2 + s, sum_idx, b, n)
                    after(pool, m.yo, b * 16)
                    pool.wait_ge(m.yc, b + 1)
                    pool.sem_inc(s_pool, 1)
                    pool.indirect_dma_start(sum_rows, bass.IndirectOffsetOnAxis(ap=idx_col[0:rows, 2 + s:3 + s], axis=0), yb[0:rows, s, :], None,
                                            compute_op=ALU.add).then_inc(m.yo, 16)

                gather(0, 0, 1)
                gather(1, 1, 2)
                pool.wait_ge(mf.init, (i + 1) * 16 * NT)
                pool.wait_ge(mf.zeroed, 16)
                for it, rows, last in turns(pool, split, split_1, before):
                    for s in range(2):
                        b = it * 2 + s
                        pool.wait_ge(m.xt, b + 1)
                        first = isinstance(b, int) and b == 0
                        gather(s, b + 2, 3 if first else b * 2 + 2, rows)
                        if not first:
                            add(1 - s, last[s], b * 2 + 3, rows)
                add(1, before * 2 + 1, pairs * 4 + 2)
                for s in range(2):
                    pool.wait_ge(m.xg[s], pairs * 16 + 16)
                pool.wait_ge(m.yo, pairs * 32)
                pool.wait_ge(m.xc, pairs * 2 + 1)
                pool.sem_inc(mf.tail, 1)

            moe(0, "ret")
            mod_store(3)
            moe(1, "conv")

        @block.scalar
        def _(act):
            st = Steps(act, s_act)

            def rms(src, junk, total, root, signal):
                st.then(act.activation(junk, src, ACT.Square, accum_out=total))
                act.activation(root, total, ACT.Sqrt, bias=eps_norm, scale=1.0 / D).then_inc(signal, 1)

            def to_uT(ns, j, dst):
                act.wait_ge(s_ntp, ns.tile + j + 1)
                act.activation(dst[:, :, j * P:(j + 1) * P],
                               ps[:, 2 * (j % 2):2 * (j % 2) + 2, :].rearrange("p b (t n) -> p (b t) n", n=P), ACT.Copy)\
                    .then_inc(s_ncp, 1)

            def between(order, key, ns, y, y_ready, y_junk, junk):
                for step, j in order:
                    if step == "y":
                        y_ready(j)
                        rms(y(j), y_junk, y_ss[:, j:j + 1], y_sd[:, j:j + 1], s_yrms)
                    elif ns is not None and step == "n":
                        act.wait_ge(s_h, h_base[key] + 2 * j + 2)
                        rms(h[:, j, :], junk, ss[:, j:j + 1], sd[:, j:j + 1], s_nrms)
                    elif ns is not None:
                        to_uT(ns, j, uT)

            act.wait_ge(s_c, 32)
            act.activation(c_act.rearrange("p t r -> p r t"), c_raw, ACT.Silu).then_inc(s_cact, 1)

            act.wait_ge(s_const, 16)
            act.wait_ge(s_ctx, 16)
            for j in range(2):
                rms(ctx_x[:, j, :], junk, ss[:, 4 + j:5 + j], sd[:, 4 + j:5 + j], s_nrms)
            act.wait_ge(s_decay, 16)
            act.wait_ge(s_log, 1)
            act.activation(dec_t[1], dec_t[0], ACT.Exp, scale=-1.0).then_inc(s_log, 1)
            act.wait_ge(s_x, 16)
            for j in range(NT):
                rms(h[:, j, :], junk, ss[:, j:j + 1], sd[:, j:j + 1], s_nrms)
            for j in range(2):
                to_uT(n_ctx, j, uTc)
            for j in range(NT):
                to_uT(n_mix[0], j, uT)
            act.wait_ge(s_mout, 32)

            for hd in peeled(act, HEADS):
                after(act, s_band, hd + 1)
                act.activation(band, band, ACT.Exp).then_inc(s_bexp, 1)
                after(act, s_o, hd * 4)
                for m in range(KEYT):
                    after(act, s_v, hd * KEYT + (m + 1))
                    act.activation(V[:, m, :], ps[:, 5 + m % 3, :], ACT.Copy).then_inc(s_vc, 1)
                after(act, s_yT, hd * 4)
                for m in range(4):
                    after(act, s_g, hd * 4 + (m + 1))
                    act.activation(sgT[:, m, :], ps[:, 5 + m % 3, :], ACT.Silu).then_inc(s_gc, 1)
                for m in range(4):
                    after(act, s_o, hd * 4 + (m + 1))
                    act.activation(osq[:, m, :], ps[:, 4 + m, :], ACT.Square).then_inc(s_osq, 1)
                after(act, s_oss, hd + 1)
                act.activation(orstd, ps[:, 3, :], ACT.Sqrt, bias=eps_norm, scale=1.0 / DV).then_inc(s_ord, 1)

            between(SLOW, "ret", n_moe[0], lambda j: ps[:, 2 * j:2 * j + 2, :].rearrange("p b n -> p (b n)"),
                    lambda j: act.wait_ge(s_y, j + 1), junk, mjunk)

            def moe(i, mixer):
                m = mo[i]
                def mod_copy2(n):
                    act.wait_ge(s_mps, 12 + 2 * n + 2)
                    act.activation(mod_part[2].products[:, n * W:(n + 1) * W], ps[0:1, 5 + n % 3, :], ACT.Copy).then_inc(s_mcp, 1)

                if i == 0:
                    for n in range(3):
                        mod_copy2(n)
                act.wait_ge(mf.logit, i + 1)
                act.activation(score, ps[:, 4, 0:NT * NE].rearrange("p (j e) -> p j e", j=NT), ACT.Sigmoid).then_inc(mf.score, 1)
                if i == 0:
                    mod_copy2(3)
                for f in range(FT):
                    act.wait_ge(mf.sup, i * 2 * FT + f + 1)
                    act.activation(sgs[:, f, :], ps[:, f, :], ACT.Silu).then_inc(mf.ssg, 1)
                for j in range(NT):
                    act.wait_ge(mf.sy, i * 2 * NT + 2 * j + 2)
                    act.activation(macc[:, j, :], ps[:, 2 * (j % 2):2 + 2 * (j % 2), :].rearrange("p b n -> p (b n)"), ACT.Copy)\
                        .then_inc(mf.sacc, 1)
                if i == 0:
                    act.wait_ge(s_mout, 48)
                act.wait_ge(mf.ctrl, i + 1)
                pairs = act.value_load(ctrl[0:1, BLOCKS:BLOCKS + 1], min_val=1, max_val=PAIRS)
                before = act.value_load(ctrl[0:1, BLOCKS + 1:BLOCKS + 2], min_val=0, max_val=PAIRS - 1)

                def scale_y(s, b, y, yo):
                    after(act, m.y, y)
                    after(act, m.yo, yo)
                    act.activation(yb[:, s, :], ps[:, 5:7, :].rearrange("p b n -> p (b n)"), ACT.Copy,
                                   scale=wslot[:, b:b + 1] if isinstance(b, int) else wslot[:, ds(b, 1)]).then_inc(m.yc, 1)

                for it in peeled(act, pairs):
                    for s in range(2):
                        after(act, m.g1, it * 2 + (s + 1))
                        act.activation(ex_g[:, s, :], ps[:, 0, 0:F], ACT.Silu).then_inc(m.sg, 1)
                        if s == 1 or not isinstance(it, int):
                            scale_y(1 - s, it * 2 + (s - 1), it * 2 + s, it * 32 + (s - 1) * 16)
                scale_y(1, before * 2 + 1, pairs * 2, before * 32 + 16)
                between(FAST, f"moe{i}", n_mix[1] if i == 0 else None, lambda j: macc[:, j, :],
                        lambda j: act.wait_ge(mf.sums[j], i * 16 + 16), mjunk, cjunk)

            moe(0, "ret")

            act.wait_ge(s_ccolp, 1)
            act.activation(chp, ps[:, 4, 0:KT * 36].rearrange("p (c k) -> p c k", c=KT), ACT.Copy).then_inc(s_ccol, 1)
            act.wait_ge(s_ccol, 1)
            def mod_copy3(n):
                act.wait_ge(s_mps, 20 + n + 1)
                act.activation(mod_part[3].products[:, n * W:(n + 1) * W], ps[0:1, 6 + n % 2, :], ACT.Copy).then_inc(s_mcp, 1)

            for cc in range(KT):
                if cc >= 5:
                    mod_copy3(cc - 5)
                act.wait_ge(s_cag, cc + 1)
                if cc >= 2:
                    act.wait_ge(s_zin, cc - 1)
                act.activation(sgate[:, cc % 2, :], ps[:, 2 * (cc % 2) + 1, :], ACT.Sigmoid, bias=chp[:, cc, 35:36]).then_inc(s_csg, 1)
            for n in range(3, 8):
                mod_copy3(n)
            act.wait_ge(s_lmu, 1)
            act.activation(mu, ps[:, 4, :], ACT.Copy, scale=1.0 / D).then_inc(s_lmuc, 1)
            for cc in range(KT):
                act.wait_ge(s_lcen, cc + 1)
                if cc >= 2:
                    act.wait_ge(s_lvar, cc - 1)
                act.activation(lsq[:, cc % 2, :], cacc[:, cc, :], ACT.Square).then_inc(s_lsq, 1)
            act.wait_ge(s_lvar, KT)
            act.activation(lrs, ps[:, 5, :], ACT.Sqrt, bias=eps_ln, scale=1.0 / D).then_inc(s_lsd, 1)
            for cc in range(KT):
                act.wait_ge(s_lnx, cc + 1)
                act.activation(zin[:, cc, 0:SEQ], cacc[:, cc, :], ACT.Silu, bias=chp[:, cc, 33:34], scale=chp[:, cc, 32:33])\
                    .then_inc(s_lnu, 1)
            between(SLOW, "conv", n_moe[1], lambda j: ybuf[:, j, :], lambda j: act.wait_ge(s_y, NT + j + 1),
                    sgate.rearrange("p s n -> p (s n)"), sgate.rearrange("p s n -> p (s n)"))
            moe(1, "conv")

        @block.tensor
        def _(pe):
            def turn(ns, j, src):
                pe.wait_ge(s_nu, ns.tile + j + 1)
                if j >= 2:
                    pe.wait_ge(s_ncp, ns.tile + j - 1)
                for t in range(KT):
                    last = pe.transpose(ps[:, 2 * (j % 2) + t // 4, (t % 4) * P:(t % 4 + 1) * P],
                                        src[:, j % 2, :].rearrange("n (p t) -> n t p", t=KT)[:, t, :], ident)
                last.then_inc(s_ntp, 1)

            def mod_product(w, loaded, count, conds, out):
                after(pe, loaded, count)
                for t in range(KT):
                    last = pe.matmul(out[0:conds, :], c_act[:, t, 0:conds], w[:, t, :], start=(t == 0), stop=(t == KT - 1))
                last.then_inc(s_mps, 1)

            pe.wait_ge(s_cact, 1)
            for n in range(10):
                if 3 <= n < 9:
                    pe.wait_ge(s_mcp, n - 2)
                mod_product(panel[n % 3], s_mw[n % 3], n // 3 * 16 + 16, 2 if n < 6 else 1, ps[:, 7 if n == 9 else 4 + n % 3, :])
            pe.wait_ge(s_const, 16)
            for j in range(2):
                turn(n_ctx, j, ubuf)
            pe.wait_ge(s_ncp, n_ctx.tile + 2)

            def last_panel(n):
                pe.wait_ge(s_mcp, n - 2)
                mod_product(panel[n % 3], s_mw[n % 3], n // 3 * 16 + 16, 1, ps[:, 4 + n % 3, :])

            for j in range(NT):
                turn(n_mix[0], j, ubuf)
            pe.wait_ge(s_ncp, n_mix[0].tile + NT)
            last_panel(10)
            last_panel(11)
            pe.wait_ge(s_mcp, 12)

            for hd in peeled(pe, HEADS):
                after(pe, s_wqk, hd * 32 + 32)
                after(pe, s_sc, hd * KEYT)
                for e in range(2):
                    for t in range(KT):
                        last = pe.matmul(ps[:, e, :], wqk[:, t, 0:DK].rearrange("p (m e) -> p e m", e=2)[:, e, :], uT[:, t, :],
                                         start=(t == 0), stop=(t == KT - 1))
                last.then_inc(s_q, 1)
                after(pe, s_ord, hd)
                for e in range(2):
                    for t in range(KT):
                        last = pe.matmul(ps[:, 2 + e, :], wqk[:, t, DK:2 * DK].rearrange("p (m e) -> p e m", e=2)[:, e, :], uT[:, t, :],
                                         start=(t == 0), stop=(t == KT - 1))
                last.then_inc(s_k, 1)
                after(pe, s_yT, hd * 4)
                for e in range(2):
                    for t in range(KT):
                        last = pe.matmul(ps[:, 4, e * CTX:(e + 1) * CTX], wqk[:, t, DK:2 * DK].rearrange("p (m e) -> p e m", e=2)[:, e, :],
                                         uTc[:, t, :], start=(t == 0), stop=(t == KT - 1))
                last.then_inc(s_kc, 1)
                after(pe, s_wv, hd * 16 + 16)
                for m in range(KEYT):
                    if m >= 3:
                        after(pe, s_vc, hd * KEYT + (m - 2))
                    src = uT[:, :, m * P:(m + 1) * P] if m < NT else uTc[:, :, (m - NT) * P:(m - NT + 1) * P]
                    for t in range(KT):
                        last = pe.matmul(ps[:, 5 + m % 3, :], src[:, t, :], wv[:, t, :], start=(t == 0), stop=(t == KT - 1))
                    last.then_inc(s_v, 1)
                after(pe, s_wg, hd * 16 + 16)
                for m in range(4):
                    after(pe, s_vc, hd * KEYT + min(m + 4, KEYT))
                    if m == 3:
                        after(pe, s_gc, hd * 4 + 1)
                    for t in range(KT):
                        last = pe.matmul(ps[:, 5 + m % 3, :], wg[:, t, m * P:(m + 1) * P], uT[:, t, :],
                                         start=(t == 0), stop=(t == KT - 1))
                    last.then_inc(s_g, 1)
                for m in range(KEYT):
                    after(pe, s_qkr, hd * 6 + 6)
                    if m >= 4:
                        after(pe, s_sc, hd * KEYT + (m - 3))
                    for e in range(2):
                        last = pe.matmul(ps[:, m % 4, :], kT[:, e, m * P:(m + 1) * P], qT[:, e, :], start=(e == 0), stop=(e == 1))
                    last.then_inc(s_s, 1)
                after(pe, s_vc, hd * KEYT + KEYT)
                after(pe, s_gc, hd * 4 + 4)
                for cc in range(4):
                    for m in range(KEYT):
                        after(pe, s_sc, hd * KEYT + (m + 1))
                        last = pe.matmul(ps[:, 4 + cc, :], V[:, m, cc * P:(cc + 1) * P], ST[:, m, :], start=(m == 0), stop=(m == KEYT - 1))
                    last.then_inc(s_o, 1)
                for cc in range(4):
                    after(pe, s_osq, hd * 4 + (cc + 1))
                    last = pe.matmul(ps[:, 3, :], ones, osq[:, cc, :], start=(cc == 0), stop=(cc == 3))
                last.then_inc(s_oss, 1)

            for j in range(NT):
                if j >= 2:
                    turn(n_moe[0], j - 2, mubuf)
                for half in range(2):
                    for cc in range(4 * HEADS):
                        pe.wait_ge(s_wo[cc // 4], 16)
                        pe.wait_ge(s_yT, 4 * (cc // 4 + 1))
                        last = pe.matmul(ps[:, 2 * j + half, :], yT[:, cc, j * P:(j + 1) * P], wo[cc // 4][:, cc % 4, half * W:(half + 1) * W],
                                         start=(cc == 0), stop=(cc == 4 * HEADS - 1))
                last.then_inc(s_y, 1)

            def moe(i, mixer):
                m = mo[i]
                def logits(j):
                    pe.wait_ge(s_ncp, n_moe[i].tile + j + 1)
                    for t in range(KT):
                        last = pe.matmul(ps[:, 4, j * NE:(j + 1) * NE], uT[:, t, j * P:(j + 1) * P], wr[i][:, t, :],
                                         start=(t == 0), stop=(t == KT - 1))
                    return last

                def mod_product2(n):
                    mod_product(half_panel[n % 5], s_mwh[n % 5], n // 5 * 16 + 16, 1, ps[:, 5 + n // 2 % 3, n % 2 * F:(n % 2 + 1) * F])

                pe.wait_ge(mf.wr, i * 16 + 16)
                turn(n_moe[i], 2, moe_u[i])
                logits(0)
                logits(1)
                logits(2)
                if i == 0:
                    pe.wait_ge(s_h, h_base[mixer] + 2 * NT)
                    for n in range(6):
                        mod_product2(n)
                turn(n_moe[i], 3, moe_u[i])
                logits(3).then_inc(mf.logit, 1)
                if i == 0:
                    pe.wait_ge(s_mcp, 13)
                    mod_product2(6)
                    mod_product2(7)
                w1, w3, w2 = expert(1)
                pe.wait_ge(mf.sw, i * 48 + 48)

                def shared_up(wi, f):
                    for t in range(KT):
                        last = pe.matmul(ps[:, 2 * wi + f, :], (w1, w3)[wi][:, t, :].rearrange("p (m f) -> p f m", f=FT)[:, f, :], uT[:, t, :],
                                         start=(t == 0), stop=(t == KT - 1))
                    last.then_inc(mf.sup, 1)

                shared_up(0, 0)
                pe.wait_ge(mf.sel, i * NT + NT)
                if i == 0:
                    pe.wait_ge(s_mcp, 16)
                for j in range(NT):
                    last = pe.matmul(ps[0:NE, 4, 256:257], sel[:, j, :], ones[:, 0:1], start=(j == 0), stop=(j == NT - 1))
                last.then_inc(mf.cnt, 1)
                pe.wait_ge(mf.nblk, i * 3 + 2)
                pe.matmul(ps[0:NE, 6, 440:440 + NE], ones[0:NE, 0:NE], key_diag[0:NE, :], start=True, stop=True).then_inc(mf.started, 1)
                pe.wait_ge(mf.nblk, i * 3 + 3)
                pe.matmul(ps[0:NE, 6, 0:1], upto[0:NE, :], cnt[0:NE, 4:5], start=True, stop=True).then_inc(mf.started, 1)
                pe.matmul(ps[0:1, 6, 256:257], ones[0:NE, 0:1], cnt[0:NE, 4:5], start=True, stop=True).then_inc(mf.started, 1)
                pe.matmul(ps[0:1, 6, 257:258], ones[0:NE, 0:1], cnt[0:NE, 9:10], start=True, stop=True).then_inc(mf.started, 1)
                for j in range(NT):
                    pe.matmul(ps[:, 5, j * NE:(j + 1) * NE], nblk_b[0:NE, :], precedes[0:NE, :], start=True, stop=False)
                    for jj in range(j):
                        pe.matmul(ps[:, 5, j * NE:(j + 1) * NE], ones, sel[:, jj, :], start=False, stop=False)
                    last = pe.matmul(ps[:, 5, j * NE:(j + 1) * NE], cst[:, C_TRI:C_TRI + P], sel[:, j, :], start=False, stop=True)
                last.then_inc(mf.pos, 1)
                pe.wait_ge(mf.started, i * 5 + 5)
                pe.matmul(ps[0:1, 6, 300:300 + BLOCKS], cst[0:NE, C_TOK:C_TOK + 1], begun[0:NE, 0:BLOCKS], start=True, stop=True).then_inc(mf.blk, 1)
                for wi, f in ((0, 1), (1, 0), (1, 1)):
                    shared_up(wi, f)
                for j in range(NT):
                    pe.wait_ge(mf.oh, i * NT + j + 1)
                    for k in range(TOPK):
                        last = pe.matmul(ps[:, 7, 0:2 * BLOCKS], oh_r[:, j % 2, k, :], oh_b[:, j % 2, k].rearrange("p w b -> p (w b)"),
                                         start=(j == 0 and k == 0), stop=(j == NT - 1 and k == TOPK - 1))
                    last.then_inc(mf.list, 1)
                pe.wait_ge(mf.ctrl, i + 1)
                pairs = pe.value_load(ctrl[0:1, BLOCKS:BLOCKS + 1], min_val=1, max_val=PAIRS)
                before = pe.value_load(ctrl[0:1, BLOCKS + 1:BLOCKS + 2], min_val=0, max_val=PAIRS - 1)
                split = pe.value_load(ctrl[0:1, BLOCKS + 2:BLOCKS + 3], min_val=2, max_val=PAIRS - 1)
                split_1 = pe.value_load(ctrl[0:1, BLOCKS + 3:BLOCKS + 4], min_val=1, max_val=PAIRS - 2)

                pe.wait_ge(mf.sh, (i + 1) * FT)
                for j in range(NT):
                    if j >= 2:
                        pe.wait_ge(mf.sacc, i * NT + j - 1)
                    for half in range(2):
                        for f in range(FT):
                            last = pe.matmul(ps[:, 2 * (j % 2) + half, :], hsT[:, f, j * P:(j + 1) * P], w2[:, f, half * W:(half + 1) * W],
                                             start=(f == 0), stop=(f == FT - 1))
                        last.then_inc(mf.sy, 1)
                pe.wait_ge(mf.sacc, (i + 1) * NT)

                def turn_x(s, n, rows=P):
                    after(pe, m.xg[s], n)
                    for t in range(KT):
                        r = rows if t else P
                        last = pe.transpose(ps[:, 2 + t // 4, (t % 4) * P:(t % 4) * P + r],
                                            xg[0:r, s, :].rearrange("n (p t) -> n t p", t=KT)[:, t, :], ident[0:r, 0:r])
                    last.then_inc(m.xt, 1)

                def up(s, bank, w, rows):
                    for f in range(FT):
                        for t in range(KT):
                            last = pe.matmul(ps[:, bank, f * P:f * P + rows], w[:, t, :].rearrange("p (m f) -> p f m", f=FT)[:, f, :],
                                             xT[:, s, t, 0:rows], start=(t == 0), stop=(t == KT - 1))
                    return last

                def down(s, hm, w2_in, yc):
                    w2 = expert(s)[2]
                    after(pe, m.hm, hm)
                    after(pe, m.w2[s], w2_in)
                    after(pe, m.yc, yc)
                    for half in range(2):
                        for f in range(FT):
                            last = pe.matmul(ps[:, 5 + half, :], ex_hT[:, s, f, :], w2[:, f, half * W:(half + 1) * W],
                                             start=(f == 0), stop=(f == FT - 1))
                    last.then_inc(m.y, 1)

                turn_x(0, 16)
                for it, rows, last in turns(pe, split, split_1, before):
                    for s in range(2):
                        w1, w3, _ = expert(s)
                        after(pe, m.xc, it * 2 + (s + 1))
                        after(pe, m.hm, it * 2 + s)
                        after(pe, m.w1[s], it * 16 + 16)
                        up(s, 0, w1, rows).then_inc(m.g1, 1)
                        turn_x(1 - s, it * 16 + (16 if s == 0 else 32), rows)
                        after(pe, m.w3[s], it * 16 + 16)
                        up(s, 1, w3, rows).then_inc(m.up, 1)
                        if s == 1 or not isinstance(it, int):
                            down(1 - s, it * 2 + s, it * 16 + 16 * s, last[s])
                down(1, pairs * 2, pairs * 16, before * 2 + 1)

            moe(0, "ret")

            for j in range(NT):
                turn(n_mix[1], j, cubuf)
            pe.wait_ge(s_ncp, n_mix[1].tile + NT)

            def mod_product3(n):
                if n >= 2:
                    pe.wait_ge(s_mcp, 16 + n - 1)
                mod_product(panel[2 * (n % 2)], s_mw[n % 2], n // 2 * 16 + 80, 1, ps[:, 6 + n % 2, :])

            for cc in range(KT):
                if cc >= 5:
                    mod_product3(cc - 5)
                if cc >= 2:
                    pe.wait_ge(s_zin, cc - 1)
                for gate in range(2):
                    s = 2 * gate + cc // 4
                    pe.wait_ge(s_cw1[s], 16)
                    for t in range(KT):
                        last = pe.matmul(ps[:, 2 * (cc % 2) + gate, :], panel[s][:, t, (cc % 4) * P:(cc % 4 + 1) * P], uT[:, t, :],
                                         start=(t == 0), stop=(t == KT - 1))
                last.then_inc(s_cag, 1)
                if cc == 0:
                    pe.wait_ge(s_crow, 16 * 6)
                    for c8 in range(KT):
                        last = pe.transpose(ps[:, 4, c8 * 36:(c8 + 1) * 36], chrow[0:36, c8 * P:(c8 + 1) * P], ident[0:36, 0:36])
                    last.then_inc(s_ccolp, 1)
            for n in range(3, 8):
                mod_product3(n)
            pe.wait_ge(s_ccol, 1)
            for cc in range(KT):
                pe.wait_ge(s_tap, cc + 1)
                last = pe.matmul(ps[:, 4, :], ones, cacc[:, cc, :], start=(cc == 0), stop=(cc == KT - 1))
            last.then_inc(s_lmu, 1)
            for cc in range(KT):
                pe.wait_ge(s_lsq, cc + 1)
                pe.matmul(ps[:, 5, :], ones, lsq[:, cc % 2, :], start=(cc == 0), stop=(cc == KT - 1)).then_inc(s_lvar, 1)
            pe.wait_ge(s_lnu, KT)
            for s in range(2):
                pe.wait_ge(s_cw2[s], 16)
            for j in range(NT):
                if j >= 2:
                    turn(n_moe[1], j - 2, cmubuf)
                for half in range(2):
                    for cc in range(KT):
                        last = pe.matmul(ps[:, 2 * j + half, :], zin[:, cc, j * P:(j + 1) * P], panel[1 + 2 * half][:, cc, :],
                                         start=(cc == 0), stop=(cc == KT - 1))
                last.then_inc(s_cy, 1)
            moe(1, "conv")

        @block.vector
        def _(dve):
            st = Steps(dve, s_dve)
            MUL, ADD, SUB, MAX, MIN = ALU.mult, ALU.add, ALU.subtract, ALU.max, ALU.min

            def mod_copy(part, panels):
                b = mod_part[part]
                for n in panels:
                    dve.wait_ge(s_mps, 6 * part + n + 1)
                    dve.tensor_copy(b.products[:, n * W:(n + 1) * W], ps[0:b.conds, 7 if (part, n) == (1, 3) else 4 + n % 3, :]).then_inc(s_mcp, 1)

            def mod_finish(part):
                b = mod_part[part]
                dve.wait_ge(s_const, 16)
                dve.wait_ge(s_mbias[part % 2], mod_in[part])
                dve.wait_ge(s_mback, 16 * (part + 1))
                st.then(dve.tensor_tensor(b.rows, b.rows, b.bias.unsqueeze(1).to_broadcast([b.blocks, b.conds, P]), ADD))
                for cond in range(b.conds):
                    dve.scalar_tensor_tensor(b.rows[:, cond, :], b.rows[:, cond, :], cst[0:b.blocks, C_ONEPLUS + part:C_ONEPLUS + part + 1],
                                             b.norm, ADD, MUL).then_inc(s_mrow, 1)

            def norm_modulate(ns, j, root, src, scale, shift, dst):
                dve.wait_ge(s_nrms, ns.tile + j + 1)
                st.then(dve.reciprocal(rs[:, root:root + 1], sd[:, root:root + 1]))
                if j >= 2:
                    dve.wait_ge(s_ntp, ns.tile + j - 1)
                st.then(dve.scalar_tensor_tensor(dst[:, j % 2, :], src, rs[:, root:root + 1], scale, MUL, MUL))
                dve.tensor_tensor(dst[:, j % 2, :], dst[:, j % 2, :], shift, ADD).then_inc(s_nu, 1)

            def residual(key, j, y, gate, tmp):
                dve.wait_ge(s_yrms, h_base[key] // 2 + j + 1)
                st.then(dve.reciprocal(y_rs[:, j:j + 1], y_sd[:, j:j + 1]))
                dve.scalar_tensor_tensor(tmp, y, y_rs[:, j:j + 1], gate, MUL, MUL).then_inc(s_h, 1)
                dve.wait_ge(s_h, h_base[key] + 2 * j + 1)
                dve.tensor_tensor(h[:, j, :], h[:, j, :], tmp, ADD).then_inc(s_h, 1)

            def between(order, key, ns, y, gate, tmp, rows, dst, stored):
                for step, j in order:
                    if step == "y":
                        if j:
                            dve.wait_ge(s_h, h_base[key] + 2 * j)
                        residual(key, j, y(j), gate, tmp)
                    elif step == "n" and ns is not None:
                        dve.wait_ge(s_h, h_base[key] + 2 * j + 2)
                        if j >= 2 and stored is not None:
                            dve.wait_ge(mf.urow[j % 2], stored)
                        norm_modulate(ns, j, j, h[:, j, :], modb[:, rows + 1, :], modb[:, rows, :], dst)

            mod_copy(0, range(6))
            dve.wait_ge(s_decay, 16)
            st.then(dve.tensor_scalar(dec_t[1], dec, -1.0, None, MUL))
            dve.tensor_tensor(dec_t[0], dec, dec_t[1], MAX).then_inc(s_log, 1)
            dve.wait_ge(s_log, 2)
            z, d2, r2, sv, s2, q = dec_t[1], dec_t[2], dec_t[3], dec_t[4], dec_t[5], dec_t[0]
            st.then(dve.tensor_scalar(d2, z, 2.0, None, ADD))
            st.then(dve.reciprocal(r2, d2))
            st.then(dve.tensor_tensor(sv, z, r2, MUL))
            st.then(dve.tensor_tensor(s2, sv, sv, MUL))
            st.then(dve.tensor_scalar(q, s2, 1.0 / 15, None, MUL))
            for k in (13, 11, 9, 7, 5, 3):
                st.then(dve.scalar_tensor_tensor(q, q, 1.0 / k, s2, ADD, MUL))
            st.then(dve.scalar_tensor_tensor(q, q, 1.0, sv, ADD, MUL))
            st.then(dve.tensor_scalar(d2, dec, 0.0, None, MIN))
            st.then(dve.scalar_tensor_tensor(r2, q, -2.0, d2, MUL, ADD))
            st.then(dve.tensor_copy(lgf, r2[:, 0:4]))
            st.then(dve.tensor_scalar(nlgb, r2[:, 4:8], -1.0, None, MUL))

            mod_finish(0)
            dve.wait_ge(s_cmod, 16)
            dve.wait_ge(s_ctx, 16)
            for j in range(2):
                norm_modulate(n_ctx, j, 4 + j, ctx_x[:, j, :], cmod[:, 1, :], cmod[:, 0, :], ubuf)
            mod_copy(1, range(3))
            dve.wait_ge(s_ntp, n_ctx.tile + 2)
            dve.wait_ge(s_x, 16)
            dve.wait_ge(s_modm, 16)
            for j in range(NT):
                norm_modulate(n_mix[0], j, j, h[:, j, :], modb[:, 1, :], modb[:, 0, :], ubuf)
            dve.wait_ge(s_nu, n_mix[0].tile + NT)
            dve.wait_ge(s_ntp, n_mix[0].tile + NT)
            dve.wait_ge(s_const, 16)

            mod_copy(1, range(3, 6))
            mod_finish(1)
            pos = cst[:, C_POS:C_POS + BAND]
            per_head = 3 + 2 + 12 + 1 + 4
            base = st.n
            for hd in peeled(dve, HEADS):
                st.n = hd * per_head + base
                after(dve, s_sc, hd * KEYT)
                st.then(dve.tensor_scalar(band, pos, 0.0, lgf[:, ds(hd, 1)], MAX, MUL))
                bt = rot.rearrange("p i n -> p (i n)")[:, 0:BAND]
                after(dve, s_o, hd * 4)
                st.then(dve.tensor_scalar(bt, pos, 0.0, nlgb[:, ds(hd, 1)], MIN, MUL))
                dve.tensor_tensor(band, band, bt, ADD).then_inc(s_band, 1)
                after(dve, s_bexp, hd + 1)
                st.then(dve.tensor_tensor(band[:, 640:640 + P], band[:, 640:640 + P], ident, ADD))
                for m in range(2):
                    last = dve.tensor_tensor(dctx[:, m, :], band[:, 640 - P * (m - 2):640 - P * (m - 2) + SEQ],
                                             band[:, 640 - P * (m + 4):640 - P * (m + 4) + SEQ], ADD)
                    st.done(last)
                after(dve, s_oss, hd)
                k0 = 0
                for signal, a, b, cs, dst in (
                    (s_q, ps[:, 0, :], ps[:, 1, :], slice(0, SEQ), qT),
                    (s_k, ps[:, 2, :], ps[:, 3, :], slice(0, SEQ), kT[:, :, 0:SEQ]),
                    (s_kc, ps[:, 4, 0:CTX], ps[:, 4, CTX:2 * CTX], slice(SEQ, SEQ + CTX), kT[:, :, SEQ:SEQ + CTX]),
                ):
                    n = cs.stop - cs.start
                    after(dve, signal, hd + 1)
                    if k0:
                        after(dve, s_qkr, hd * 6 + k0)
                    c_, s_ = cos[:, cs], sin[:, cs]
                    st.done(dve.tensor_tensor(rot[:, 0, 0:n], a, c_, MUL))
                    st.done(dve.tensor_tensor(rot[:, 1, 0:n], b, s_, MUL))
                    st.done(dve.tensor_tensor(rot[:, 2, 0:n], a, s_, MUL))
                    st.then(dve.tensor_tensor(rot[:, 3, 0:n], b, c_, MUL))
                    dve.tensor_tensor(dst[:, 0, :], rot[:, 0, 0:n], rot[:, 1, 0:n], SUB).then_inc(s_qkr, 1)
                    dve.tensor_tensor(dst[:, 1, :], rot[:, 2, 0:n], rot[:, 3, 0:n], ADD).then_inc(s_qkr, 1)
                    k0 += 2
                after(dve, s_qkr, hd * 6 + 6)
                for m in range(KEYT):
                    after(dve, s_s, hd * KEYT + (m + 1))
                    dk = band[:, 640 - P * m:640 - P * m + SEQ] if m < NT else dctx[:, m - NT, :]
                    dve.scalar_tensor_tensor(ST[:, m, :], ps[:, m % 4, :], DK ** -0.5, dk, MUL, MUL).then_inc(s_sc, 1)
                after(dve, s_ord, hd + 1)
                after(dve, s_gc, hd * 4 + 4)
                st.then(dve.reciprocal(orstd, orstd))
                for cc in range(4):
                    if cc:
                        after(dve, s_yT, hd * 4 + cc)
                    ins = dve.tensor_tensor(otmp, ps[:, 4 + cc, :], orstd, MUL)
                    st.then(ins)
                    dve.tensor_tensor(yT[:, ds(hd * 4 + cc, 1), :].rearrange("p o n -> p (o n)"), otmp, sgT[:, cc, :], MUL).then_inc(s_yT, 1)
            st.n = base + HEADS * per_head

            dve.wait_ge(s_modf, 16)
            between(SLOW, "ret", n_moe[0], lambda j: ps[:, 2 * j:2 * j + 2, :].rearrange("p b n -> p (b n)"), modb[:, 2, :], junk,
                    3, mubuf, 16)

            def moe(i, mixer):
                m = mo[i]
                dve.wait_ge(s_h, h_base[mixer] + 2 * NT)
                st.done(dve.memset(gsx[:, :, NG:NG + 4], -MARK))
                st.done(dve.memset(grep[:, :, 4:8], -MARK))
                dve.wait_ge(mf.score, i + 1)
                dve.wait_ge(mf.bias, i * 16 + 16)
                st.then(dve.tensor_tensor(biased, score, bias.unsqueeze(1).to_broadcast([P, NT, NE]), ADD))
                for j in range(NT):
                    for g in range(NG):
                        st.done(dve.max(gtop[:, j, g, :], biased[:, j, g * PER:(g + 1) * PER]))
                after(dve, s_dve, st.n)
                st.then(dve.tensor_tensor(gsx[:, :, 0:NG], gtop[:, :, :, 0], gtop[:, :, :, 1], ADD))
                for j in range(NT):
                    st.done(dve.max(gmax[:, j, :], gsx[:, j, :]))
                after(dve, s_dve, st.n)
                st.then(dve.tensor_copy(grep[:, :, 0:4], gmax[:, :, 0:4]))
                for j in range(NT):
                    st.done(dve.match_replace(gout[:, j, :], grep[:, j, :], gsx[:, j, :], MARK))
                after(dve, s_dve, st.n)
                st.then(dve.tensor_scalar(gmask, gout[:, :, 0:NG], MARK, None, ALU.is_equal))
                st.then(dve.tensor_scalar(gneg, gmask, 1.0, -LOW, SUB, MUL))
                for j in range(NT):
                    st.done(dve.tensor_tensor(rep[:, j].rearrange("p (g k) -> p g k", g=NG), biased[:, j].rearrange("p (g k) -> p g k", g=NG),
                                              gmask[:, j].unsqueeze(2).to_broadcast([P, NG, PER]), MUL))
                after(dve, s_dve, st.n)
                for j in range(NT):
                    st.done(dve.tensor_tensor(biased[:, j].rearrange("p (g k) -> p g k", g=NG), rep[:, j].rearrange("p (g k) -> p g k", g=NG),
                                              gneg[:, j].unsqueeze(2).to_broadcast([P, NG, PER]), ADD))
                after(dve, s_dve, st.n)
                for j in range(NT):
                    st.done(dve.max(top8[:, j, :], biased[:, j, :]))
                after(dve, s_dve, st.n)
                for j in range(NT):
                    st.done(dve.match_replace(rep[:, j, :], top8[:, j, :], biased[:, j, :], MARK))
                after(dve, s_dve, st.n)
                for j in range(NT):
                    dve.tensor_scalar(sel[:, j, :], rep[:, j, :], MARK, None, ALU.is_equal).then_inc(mf.sel, 1)
                dve.wait_ge(mf.sel, i * NT + NT)
                dve.wait_ge(mf.cnt, i + 1)
                st.then(dve.tensor_copy(cnt[0:NE, 5:6], ps[0:NE, 4, 256:257]))
                st.then(dve.tensor_scalar(cnt[0:NE, 0:4], cst[0:NE, C_THR:C_THR + NT], cnt[0:NE, 5:6], None, ALU.is_lt))
                dve.tensor_reduce(cnt[0:NE, 4:5], cnt[0:NE, 0:4], AX.X, ADD).then_inc(mf.nblk, 1)
                dve.wait_ge(mf.nblk, i * 3 + 1)
                st.done(dve.tensor_scalar(cnt[0:NE, 7:8], cnt[0:NE, 5:6], float(SMALL), float(NE), ALU.is_le, MUL))
                st.done(dve.tensor_scalar(cnt[0:NE, 9:10], cnt[0:NE, 5:6], float(SMALL), cnt[0:NE, 4:5], ALU.is_gt, MUL))
                dve.wait_ge(s_dve, st.n)
                st.then(dve.tensor_tensor(cnt[0:NE, 8:9], cnt[0:NE, 7:8], cst[0:NE, C_TOK:C_TOK + 1], ADD))
                st.then(dve.tensor_scalar(key_diag[0:NE, :], ident[0:NE, 0:NE], cnt[0:NE, 8:9], None, MUL))
                dve.tensor_scalar(nblk_b[0:NE, :], ones[0:NE, :], cnt[0:NE, 4:5], float(P), MUL, MUL).then_inc(mf.nblk, 1)
                dve.wait_ge(mf.started, i * 5 + 1)
                st.then(dve.tensor_scalar(precedes[0:NE, :], ps[0:NE, 6, 440:440 + NE], cnt[0:NE, 8:9], None, ALU.is_gt))
                dve.tensor_scalar(upto[0:NE, :], ps[0:NE, 6, 440:440 + NE], cnt[0:NE, 8:9], None, ALU.is_ge).then_inc(mf.nblk, 1)
                dve.wait_ge(mf.started, i * 5 + 4)
                st.then(dve.tensor_copy(cnt[0:NE, 6:7], ps[0:NE, 6, 0:1]))
                st.done(dve.tensor_tensor(cnt[0:NE, 10:11], cnt[0:NE, 6:7], cnt[0:NE, 4:5], SUB))
                st.done(dve.tensor_scalar(started[0:NE, 0:BLOCKS], cst[0:NE, C_IOTA:C_IOTA + BLOCKS], cnt[0:NE, 6:7], None, ALU.is_ge))
                dve.wait_ge(s_dve, st.n)
                dve.scalar_tensor_tensor(begun[0:NE, 0:BLOCKS], cst[0:NE, C_IOTA:C_IOTA + BLOCKS], cnt[0:NE, 10:11], started[0:NE, 0:BLOCKS],
                                         ALU.is_ge, SUB).then_inc(mf.started, 1)
                dve.wait_ge(mf.pos, i + 1)
                for j in range(NT):
                    st.done(dve.tensor_scalar(slotk[:, j, :], ps[:, 5, j * NE:(j + 1) * NE], -1.0, BIG, MUL, ADD))
                after(dve, s_dve, st.n)
                st.then(dve.tensor_tensor(slotk, slotk, sel, MUL))
                for j in range(NT):
                    st.done(dve.max(topslot[:, j, :], slotk[:, j, :]))
                after(dve, s_dve, st.n)
                dve.wait_ge(mf.blk, i + 1)
                split = ctrl[0:1, BLOCKS + 2:BLOCKS + 3]
                end = ctrl[0:1, BLOCKS:BLOCKS + 1]
                st.done(dve.tensor_scalar(ctrl[0:1, 0:BLOCKS], ps[0:1, 6, 300:300 + BLOCKS], -1.0, 0.0, ADD, MAX))
                st.done(dve.tensor_scalar(split, ps[0:1, 6, 257:258], 0.5, 1.25, MUL, ADD))
                st.done(dve.tensor_scalar(end, ps[0:1, 6, 256:257], 0.5, 0.25, MUL, ADD))
                dve.wait_ge(s_dve, st.n)
                st.then(dve.tensor_scalar(split, split, 2.0, None, MAX))
                st.then(dve.tensor_scalar(ctrl[0:1, BLOCKS + 3:BLOCKS + 4], split, 1.0, None, ADD))
                st.then(dve.tensor_tensor(end, end, ctrl[0:1, BLOCKS + 3:BLOCKS + 4], MAX))
                st.done(dve.tensor_scalar(ctrl[0:1, BLOCKS + 3:BLOCKS + 4], split, 1.0, None, SUB))
                dve.wait_ge(s_dve, st.n)
                dve.tensor_scalar(ctrl[0:1, BLOCKS + 1:BLOCKS + 2], end, 1.0, None, SUB).then_inc(mf.ctrl, 1)
                st.then(dve.tensor_tensor(wn, score, sel, MUL))
                st.then(dve.tensor_reduce(wsum[:, 0:NT], wn, AX.X, ADD))
                st.then(dve.reciprocal(wsum[:, 4:8], wsum[:, 0:NT]))
                for j in range(NT):
                    st.done(dve.tensor_scalar(wn[:, j, :], wn[:, j, :], wsum[:, 4 + j:5 + j], ROUTE_SCALE, MUL, MUL))
                after(dve, s_dve, st.n)
                for j in range(NT):
                    st.then(dve.tensor_tensor(eq, slotk[:, j].unsqueeze(1).to_broadcast([P, TOPK, NE]),
                                              topslot[:, j].unsqueeze(2).to_broadcast([P, TOPK, NE]), ALU.is_equal))
                    st.then(dve.tensor_tensor(eq, eq, wn[:, j].unsqueeze(1).to_broadcast([P, TOPK, NE]), MUL))
                    st.then(dve.tensor_reduce(wk[:, j, :], eq, AX.X, ADD))
                st.then(dve.tensor_scalar(slot_i, topslot.rearrange("p j k -> p (j k)"), -1.0, BIG, MUL, ADD))
                st.done(dve.tensor_scalar(slot_ri, slot_i, P - 1, None, ALU.bitwise_and))
                st.then(dve.tensor_scalar(slot_bi, slot_i, 7, None, ALU.logical_shift_right))
                st.done(dve.tensor_copy(slot_r.rearrange("p j k -> p (j k)"), slot_ri))
                st.then(dve.tensor_copy(slot_b.rearrange("p j k -> p (j k)"), slot_bi))
                iota = cst[:, C_IOTA:C_IOTA + P]
                for s in range(2):
                    dve.wait_ge(mf.urow[s], i * 32 + 32)
                if i == 0:
                    dve.wait_ge(s_mraw, 48)
                for j in range(NT):
                    if j >= 2:
                        dve.wait_ge(mf.list, i * NT + j - 1)
                    oh, ow = oh_b[:, j % 2, :, 0, :], oh_b[:, j % 2, :, 1, :]
                    st.done(dve.tensor_tensor(oh_r[:, j % 2], iota.unsqueeze(1).to_broadcast([P, TOPK, P]),
                                              slot_r[:, j].unsqueeze(2).to_broadcast([P, TOPK, P]), ALU.is_equal))
                    st.then(dve.tensor_tensor(oh, iota[:, 0:BLOCKS].unsqueeze(1).to_broadcast([P, TOPK, BLOCKS]),
                                              slot_b[:, j].unsqueeze(2).to_broadcast([P, TOPK, BLOCKS]), ALU.is_equal))
                    st.then(dve.tensor_tensor(ow, oh, wk[:, j].unsqueeze(2).to_broadcast([P, TOPK, BLOCKS]), MUL))
                    dve.tensor_scalar(oh, oh, cst[:, C_TOK + j:C_TOK + j + 1], None, MUL).then_inc(mf.oh, 1)
                for f in range(FT):
                    dve.wait_ge(mf.ssg, i * FT + f + 1)
                    dve.wait_ge(mf.sup, i * 2 * FT + FT + f + 1)
                    dve.tensor_tensor(hsT[:, f, :], ps[:, 2 + f, :], sgs[:, f, :], MUL).then_inc(mf.sh, 1)
                if i == 0:
                    mod_finish(2)
                dve.wait_ge(mf.list, (i + 1) * NT)
                st.done(dve.tensor_copy(wslot, ps[:, 7, BLOCKS:2 * BLOCKS]))
                st.then(dve.tensor_scalar(is_pad, ps[:, 7, 0:BLOCKS], 0.0, cst[:, C_DUMP:C_DUMP + 1], ALU.is_equal, MUL))
                st.done(dve.scalar_tensor_tensor(sum_idx, ps[:, 7, 0:BLOCKS], -1.0, is_pad, ADD, ADD))
                after(dve, s_dve, st.n)
                st.then(dve.tensor_scalar(is_pad, ps[:, 7, 0:BLOCKS], 0.0, cst[:, C_SKIP:C_SKIP + 1], ALU.is_equal, MUL))
                dve.scalar_tensor_tensor(tok_idx, ps[:, 7, 0:BLOCKS], -1.0, is_pad, ADD, ADD).then_inc(mf.tok, 1)

                dve.wait_ge(mf.ctrl, i + 1)
                pairs = dve.value_load(ctrl[0:1, BLOCKS:BLOCKS + 1], min_val=1, max_val=PAIRS)

                def copy_xT(s, n):
                    after(dve, m.xt, n)
                    dve.tensor_copy(xT[:, s], ps[:, 2:4, :].rearrange("p b (t n) -> p (b t) n", n=P)).then_inc(m.xc, 1)

                copy_xT(0, 1)
                for it in peeled(dve, pairs):
                    for s in range(2):
                        after(dve, m.sg, it * 2 + (s + 1))
                        after(dve, m.up, it * 2 + (s + 1))
                        dve.tensor_tensor(ex_hT[:, s].rearrange("p f n -> p (f n)"), ps[:, 1, 0:F], ex_g[:, s, :], MUL).then_inc(m.hm, 1)
                        copy_xT(1 - s, it * 2 + (s + 2))
                if i == 0:
                    dve.wait_ge(s_modm, 32)
                between(FAST, f"moe{i}", n_mix[1] if i == 0 else None, lambda j: macc[:, j, :], modb[:, 5, :], mubuf[:, 0, :],
                        0, cubuf, None)

            moe(0, "ret")

            dve.wait_ge(s_ntp, n_mix[1].tile + NT)
            st.done(dve.memset(zin[:, :, 0:HALO], 0.0))
            st.done(dve.memset(zin[:, :, HALO + SEQ:2 * HALO + SEQ], 0.0))
            dve.wait_ge(s_ccol, 1)

            def tile(a, cc):
                return a[:, ds(cc, 1)].rearrange("p o n -> p (o n)")

            def glu(cc, u):
                dve.wait_ge(s_csg, cc + 1)
                dve.scalar_tensor_tensor(tile(zin[:, :, HALO:HALO + SEQ], cc), ps[:, 2 * u, :], tile(chp[:, :, 34:35], cc), sgate[:, u, :], ADD, MUL)\
                    .then_inc(s_zin, 1)

            def taps(cc, ks):
                for k in ks:
                    z_, w_ = tile(zin[:, :, k:k + SEQ], cc), tile(chp[:, :, k:k + 1], cc)
                    a_ = lrs if k % 2 else tile(cacc, cc)
                    if k >= 2:
                        dve.wait_ge(s_dve, st.n - 1)
                        st.done(dve.scalar_tensor_tensor(a_, z_, w_, a_, MUL, ADD))
                    elif k:
                        after(dve, s_tap, cc)
                        st.done(dve.tensor_scalar(a_, z_, w_, None, MUL))
                    else:
                        st.done(dve.tensor_scalar(a_, z_, w_, tile(chp[:, :, TAPS:TAPS + 1], cc), MUL, ADD))

            glu(0, 0)
            base = st.n
            for pr in peeled(dve, 3, True):
                for u in range(2):
                    cc = pr * 2 + u
                    st.n = cc * TAPS + base
                    dve.wait_ge(s_zin, cc + 1)
                    taps(cc, range(21))
                    if not (isinstance(cc, int) and cc == KT - 1):
                        glu(cc + 1, 1 - u)
                    taps(cc, range(21, TAPS))
                    dve.wait_ge(s_dve, st.n)
                    dve.tensor_tensor(tile(cacc, cc), tile(cacc, cc), lrs, ADD).then_inc(s_tap, 1)
            dve.wait_ge(s_tap, KT)
            dve.wait_ge(s_lmuc, 1)
            for cc in range(KT):
                dve.tensor_tensor(cacc[:, cc, :], cacc[:, cc, :], mu, SUB).then_inc(s_lcen, 1)
            dve.wait_ge(s_lsd, 1)
            st.then(dve.reciprocal(lrs, lrs))
            for cc in range(KT):
                dve.wait_ge(s_lcen, KT)
                dve.wait_ge(s_lsq, cc + 1)
                dve.tensor_tensor(cacc[:, cc, :], cacc[:, cc, :], lrs, MUL).then_inc(s_lnx, 1)
            mod_finish(3)
            dve.wait_ge(s_cb2, 16)
            dve.wait_ge(s_modf, 32)

            def conv_y(j):
                dve.wait_ge(s_cy, j + 1)
                dve.tensor_tensor(ybuf[:, j, :], ps[:, 2 * j:2 * j + 2, :].rearrange("p b n -> p (b n)"), b2row, ADD).then_inc(s_y, 1)
                dve.wait_ge(s_y, NT + j + 1)
                return ybuf[:, j, :]

            between(SLOW, "conv", n_moe[1], conv_y, modb[:, 2, :], chrow, 3, cmubuf, 48)
            moe(1, "conv")


_INS = ['x', 'c', 'ctx', 'c_ctx', 'mod_w', 'mod_b', 'norms', 'ret_w_in', 'ret_w_out', 'ret_decay',
        'conv_w1', 'conv_b1', 'conv_dw', 'conv_b_dw', 'conv_ln_g', 'conv_ln_b', 'conv_w2', 'conv_b2',
        'moe_router', 'moe_bias', 'moe_w1', 'moe_w3', 'moe_w2', 'shared_w1', 'shared_w3', 'shared_w2']


def kernel(**inputs):
    import concourse.bacc as bacc
    from concourse.bass_utils import run_bass_kernel_spmd

    nc = bacc.Bacc("TRN2", target_bir_lowering=False, num_devices=1)
    arrays = {f"in_{n}": np.ascontiguousarray(inputs[n]) for n in _INS}
    arrays["in_consts"] = shape_constants()
    args = [nc.dram_tensor(n, a.shape, F32, kind="ExternalInput").ap() for n, a in arrays.items()]
    out = nc.dram_tensor("out", (1, SEQ, D), F32, kind="ExternalOutput").ap()
    build(nc, *args, out)
    return run_bass_kernel_spmd(nc, [arrays], core_ids=[0]).results[0]["out"]
```
